# Optimizing a Trainium2 kernel written in Bass

```python
import math
import jax, jax.numpy as jnp
from jax import lax
import numpy as np

D_MODEL = 1024
BATCH = 1
SEQ = 1024
DEPTH = 1
DEC_BATCH = 8
DEC_SEQ = 4
PAST_LEN = 8192
PAGE_SIZE = 128

N_DN_HEADS = 8
DN_HEAD_DIM = 64
DN_WIDTH = N_DN_HEADS * DN_HEAD_DIM
CONV_CH = D_MODEL - DN_WIDTH
CONV_GROUPS = 8
CONV_GROUP_DIM = CONV_CH // CONV_GROUPS
SHORT_CONV = 4
DW_CONV = 31
CHUNK = 64
D_FF = 4 * D_MODEL
D_PLE = 256
EPS = 1e-6
IN_COLS = 4 * DN_WIDTH + 2 * N_DN_HEADS + 2 * CONV_CH

kernel_name = 'hybrid_gdn_conformer_decode_step'

def rmsnorm(x, gain):
    xf = x.astype(jnp.float32)
    y = xf * lax.rsqrt(jnp.mean(xf * xf, axis=-1, keepdims=True) + EPS)
    return (y * gain.astype(jnp.float32)).astype(x.dtype)

def l2norm(x):
    xf = x.astype(jnp.float32)
    return xf * lax.rsqrt(jnp.sum(xf * xf, axis=-1, keepdims=True) + EPS)

def causal_depthwise_conv(x_full, w):
    ch = x_full.shape[-1]
    return lax.conv_general_dilated(
        x_full, w[:, None, :].astype(x_full.dtype), window_strides=(1,), padding='VALID',
        dimension_numbers=('NWC', 'WIO', 'NWC'), feature_group_count=ch)

def gated_delta_rule(q, k, v, g, beta, s0):
    b, t, h, dk = q.shape
    dv = v.shape[-1]
    c = min(CHUNK, t)
    n = -(-t // c)
    pad = n * c - t
    f32 = jnp.float32

    def prep(a):
        a = a.astype(f32)
        a = jnp.pad(a, [(0, 0), (0, pad)] + [(0, 0)] * (a.ndim - 2))
        a = a.reshape((b, n, c) + a.shape[2:])
        return jnp.moveaxis(a, 3, 1)

    q, k, v, g, beta = prep(q), prep(k), prep(v), prep(g), prep(beta)
    q = q * (dk ** -0.5)
    gc = jnp.cumsum(g, axis=-1)
    k_beta = k * beta[..., None]
    v_beta = v * beta[..., None]
    idx = jnp.arange(c)
    causal = idx[:, None] >= idx[None, :]
    strict = idx[:, None] > idx[None, :]
    diff = gc[..., :, None] - gc[..., None, :]
    decay = jnp.exp(jnp.where(causal, diff, -jnp.inf))
    lmat = jnp.where(strict, jnp.einsum('bhncd,bhnmd->bhncm', k_beta, k) * decay, 0.0)
    eye = jnp.eye(c, dtype=f32)
    tmat = lax.linalg.triangular_solve(eye + lmat, jnp.broadcast_to(eye, lmat.shape),
                                       left_side=True, lower=True, unit_diagonal=True)
    u = jnp.einsum('bhncm,bhnmd->bhncd', tmat, v_beta)
    w = jnp.einsum('bhncm,bhnmd->bhncd', tmat, k_beta * jnp.exp(gc)[..., None])
    qk = jnp.einsum('bhncd,bhnmd->bhncm', q, k) * decay
    q_dec = q * jnp.exp(gc)[..., None]
    k_dec = k * jnp.exp(gc[..., -1:] - gc)[..., None]
    g_last = jnp.exp(gc[..., -1])

    def step(s, xs):
        u_c, w_c, qk_c, qd_c, kd_c, gl_c = xs
        v_new = u_c - jnp.einsum('bhcd,bhde->bhce', w_c, s)
        o_c = jnp.einsum('bhcd,bhde->bhce', qd_c, s) + jnp.einsum('bhcm,bhme->bhce', qk_c, v_new)
        s = s * gl_c[..., None, None] + jnp.einsum('bhcd,bhce->bhde', kd_c, v_new)
        return s, o_c

    xs = tuple(jnp.moveaxis(a, 2, 0) for a in (u, w, qk, q_dec, k_dec, g_last))
    s_final, o = lax.scan(step, s0.astype(f32), xs)
    o = jnp.transpose(o, (1, 0, 3, 2, 4)).reshape(b, n * c, h, dv)[:, :t]
    return o, s_final

def decoder_layer(x, p_emb, qkv_buf, conf_buf, s0, g_mix, w_in, w_short, a_log, dt_bias, g_o,
                  w_dw, b_dw, g_cln, b_cln, w_out, g_mlp, w_up, w_down, w_ple, g_ple, w_ple_gate):
    f32 = jnp.float32
    bsz, t, _ = x.shape
    h = rmsnorm(x, g_mix)
    proj = h @ w_in
    o0 = 3 * DN_WIDTH
    o1 = o0 + DN_WIDTH
    o2 = o1 + 2 * N_DN_HEADS
    qkv_in = proj[..., :o0]
    z = proj[..., o0:o1]
    b_logit = proj[..., o1:o1 + N_DN_HEADS]
    a_logit = proj[..., o1 + N_DN_HEADS:o2]
    glu_in = proj[..., o2:]

    qkv_full = jnp.concatenate([qkv_buf.astype(x.dtype), qkv_in], axis=1)
    new_qkv_buf = qkv_full[:, -(SHORT_CONV - 1):]
    qkv = jax.nn.silu(causal_depthwise_conv(qkv_full, w_short))
    heads = lambda a: a.reshape(bsz, t, N_DN_HEADS, DN_HEAD_DIM)
    q = l2norm(heads(qkv[..., :DN_WIDTH]))
    k = l2norm(heads(qkv[..., DN_WIDTH:2 * DN_WIDTH]))
    v = heads(qkv[..., 2 * DN_WIDTH:])
    beta = jax.nn.sigmoid(b_logit.astype(f32))
    g = -jnp.exp(a_log.astype(f32)) * jax.nn.softplus(a_logit.astype(f32) + dt_bias.astype(f32))
    o, s_new = gated_delta_rule(q, k, v, g, beta, s0)
    o = rmsnorm(o, g_o) * jax.nn.silu(heads(z).astype(f32))
    o = o.reshape(bsz, t, DN_WIDTH).astype(x.dtype)

    glu = glu_in[..., :CONV_CH] * jax.nn.sigmoid(glu_in[..., CONV_CH:])
    conf_full = jnp.concatenate([conf_buf.astype(x.dtype), glu], axis=1)
    new_conf_buf = conf_full[:, -(DW_CONV - 1):]
    cv = causal_depthwise_conv(conf_full, w_dw) + b_dw.astype(x.dtype)
    cf = cv.astype(f32).reshape(bsz, t, CONV_GROUPS, CONV_GROUP_DIM)
    mu = jnp.mean(cf, axis=-1, keepdims=True)
    var = jnp.mean(jnp.square(cf - mu), axis=-1, keepdims=True)
    cf = ((cf - mu) * lax.rsqrt(var + EPS)).reshape(bsz, t, CONV_CH) * g_cln.astype(f32) + b_cln.astype(f32)
    cv = jax.nn.silu(cf).astype(x.dtype)

    x = x + jnp.concatenate([o, cv], axis=-1) @ w_out

    h = rmsnorm(x, g_mlp)
    x = x + jnp.square(jax.nn.relu(h @ w_up)) @ w_down

    gate = jax.nn.sigmoid(rmsnorm(x, g_ple) @ w_ple_gate)
    x = x + (p_emb.astype(x.dtype) @ w_ple) * gate
    return x, new_qkv_buf, new_conf_buf, s_new.astype(s0.dtype)

def setup_inputs(seed: int = 0) -> dict:
    key = jax.random.key(seed)
    ks = jax.random.split(key, 32)
    f32 = jnp.float32
    nrm = lambda k, shape, scale: jax.random.normal(k, shape, f32) * scale
    gain = lambda k, shape: 1.0 + 0.05 * jax.random.normal(k, shape, f32)
    dt = jnp.exp(jax.random.uniform(ks[20], (DEPTH, N_DN_HEADS), f32, math.log(1e-3), math.log(0.1)))
    dt_bias = dt + jnp.log(-jnp.expm1(-dt))
    a_log = jnp.log(jax.random.uniform(ks[21], (DEPTH, N_DN_HEADS), f32, 1.0, 16.0))
    return {
        'x_prompt': nrm(ks[0], (BATCH, SEQ, D_MODEL), 1.0),
        'x_sample': nrm(ks[1], (DEC_BATCH, DEC_SEQ, D_MODEL), 1.0),
        'state_ssm': nrm(ks[2], (DEPTH, DEC_BATCH, N_DN_HEADS, DN_HEAD_DIM, DN_HEAD_DIM), 0.05),
        'state_qkv_conv': nrm(ks[3], (DEPTH, DEC_BATCH, SHORT_CONV - 1, 3 * DN_WIDTH), 1.0),
        'state_conf_conv': nrm(ks[4], (DEPTH, DEC_BATCH, DW_CONV - 1, CONV_CH), 0.5),
        'p_prompt': nrm(ks[5], (DEPTH, BATCH, SEQ, D_PLE), 1.0),
        'p_sample': nrm(ks[6], (DEPTH, DEC_BATCH, DEC_SEQ, D_PLE), 1.0),
        'g_mix': gain(ks[7], (DEPTH, D_MODEL)),
        'w_in': nrm(ks[8], (DEPTH, D_MODEL, IN_COLS), D_MODEL ** -0.5),
        'w_short': nrm(ks[9], (DEPTH, SHORT_CONV, 3 * DN_WIDTH), SHORT_CONV ** -0.5),
        'a_log': a_log,
        'dt_bias': dt_bias,
        'g_o': gain(ks[10], (DEPTH, DN_HEAD_DIM)),
        'w_dw': nrm(ks[11], (DEPTH, DW_CONV, CONV_CH), DW_CONV ** -0.5),
        'b_dw': nrm(ks[12], (DEPTH, CONV_CH), 0.02),
        'g_cln': gain(ks[13], (DEPTH, CONV_CH)),
        'b_cln': nrm(ks[14], (DEPTH, CONV_CH), 0.02),
        'w_out': nrm(ks[15], (DEPTH, D_MODEL, D_MODEL), D_MODEL ** -0.5),
        'g_mlp': gain(ks[16], (DEPTH, D_MODEL)),
        'w_up': nrm(ks[17], (DEPTH, D_MODEL, D_FF), D_MODEL ** -0.5),
        'w_down': nrm(ks[18], (DEPTH, D_FF, D_MODEL), D_FF ** -0.5),
        'w_ple': nrm(ks[19], (DEPTH, D_PLE, D_MODEL), D_PLE ** -0.5),
        'g_ple': gain(ks[22], (DEPTH, D_MODEL)),
        'w_ple_gate': nrm(ks[23], (DEPTH, D_MODEL, D_MODEL), D_MODEL ** -0.5),
        'g_final': gain(ks[24], (D_MODEL,)),
    }

def reference(x_prompt, x_sample, state_ssm, state_qkv_conv, state_conf_conv, p_prompt, p_sample,
              g_mix, w_in, w_short, a_log, dt_bias, g_o, w_dw, b_dw, g_cln, b_cln, w_out,
              g_mlp, w_up, w_down, w_ple, g_ple, w_ple_gate, g_final):
    bp = x_prompt.shape[0]
    yp, ys = x_prompt, x_sample
    ssm_p, qkv_p, conf_p, ssm_s, qkv_s, conf_s = [], [], [], [], [], []
    for i in range(DEPTH):
        params = (g_mix[i], w_in[i], w_short[i], a_log[i], dt_bias[i], g_o[i], w_dw[i], b_dw[i],
                  g_cln[i], b_cln[i], w_out[i], g_mlp[i], w_up[i], w_down[i], w_ple[i], g_ple[i],
                  w_ple_gate[i])
        zq = jnp.zeros((bp, SHORT_CONV - 1, 3 * DN_WIDTH), x_prompt.dtype)
        zc = jnp.zeros((bp, DW_CONV - 1, CONV_CH), x_prompt.dtype)
        zs = jnp.zeros((bp, N_DN_HEADS, DN_HEAD_DIM, DN_HEAD_DIM), state_ssm.dtype)
        yp, bq, bc, sp = decoder_layer(yp, p_prompt[i], zq, zc, zs, *params)
        ys, sq, sc, ss = decoder_layer(ys, p_sample[i], state_qkv_conv[i], state_conf_conv[i],
                                       state_ssm[i], *params)
        ssm_p.append(sp); qkv_p.append(bq); conf_p.append(bc)
        ssm_s.append(ss); qkv_s.append(sq); conf_s.append(sc)
    y_prompt = rmsnorm(yp, g_final)
    y_sample = rmsnorm(ys, g_final)
    return (y_prompt, y_sample, jnp.stack(ssm_p), jnp.stack(qkv_p), jnp.stack(conf_p),
            jnp.stack(ssm_s), jnp.stack(qkv_s), jnp.stack(conf_s))


_drawn_inputs = setup_inputs


def setup_inputs(seed=0):
    import zlib

    import numpy as np

    out = dict(_drawn_inputs(seed))
    spreads = {}
    factors = {'b_dw': 3.822, 'b_cln': 7.576, 'g_ple': 23.014}
    for name, (base, spread) in spreads.items():
        noise = np.random.default_rng([zlib.crc32(name.encode()), seed]).standard_normal(out[name].shape)
        drawn = base * np.exp(spread * noise) if base else spread * noise
        out[name] = __import__('jax').numpy.asarray(drawn.astype(out[name].dtype))
    for name, factor in factors.items():
        out[name] = (out[name] * factor).astype(out[name].dtype)
    return out
```

```python
from contextlib import ExitStack

import numpy as np

import concourse.bass as bass
from concourse import mybir

F32 = mybir.dt.float32
F32R = mybir.dt.float32r
ALU = mybir.AluOpType
ACT = mybir.ActivationFunctionType
AX = mybir.AxisListType.X

P = 128
SEQ, DB, DS = 1024, 8, 4
NS = DB * DS
TOK = SEQ + NS
D = 1024
KT = D // P
NCH = 3
CW = TOK // NCH
H, HD = 8, 64
PR = H // 2
DW = H * HD
SC, DWC = 4, 31
CC = D - DW
CT = CC // P
C = 32
CPT = P // C
FF = 4 * D
FQ = FF // D
PLE = 256
PK = PLE // P
EPS = 1e-6
NT = SEQ // P
HIST, QH = DWC - 1, SC - 1
QT = 3 * DW // P
O_Z, O_B, O_GA, O_GB = 3 * DW, 4 * DW, 4 * DW + 2 * H, 4 * DW + 2 * H + CC

J_AB, J_QKV, J_GLU, J_Z, J_OUT = 0, 1, 13, 21, 25
J_MLP = J_OUT + KT
J_GATE = J_MLP + 2 * FQ * KT
J_END = J_GATE + 2 * KT

CONSTS = [("ident", P), ("ones", P), ("bd64", P), ("uinc", P), ("sgt", P), ("uinc4", P), ("sgt4", P),
          ("blk", CPT), ("blk4", DB), ("tri", C), ("tri4", C), ("str4", C)]
NV = 4 * KT + 3 * CT + 1


def shape_constants():
    r, c = np.arange(P)[:, None], np.arange(P)[None, :]

    def inside(n):
        return r // n == c // n

    low = (r < NS) & (c < NS)
    parts = {
        "ident": r == c, "ones": r >= 0 * c, "bd64": inside(HD) / HD,
        "uinc": (r <= c) & inside(C), "sgt": (r > c) & inside(C),
        "uinc4": (r <= c) & inside(DS) & low, "sgt4": (r > c) & inside(DS) & low,
        "blk": r // C == c[:, :CPT], "blk4": (r // DS == c[:, :DB]) & (r < NS),
        "tri": r % C <= c[:, :C], "tri4": (r <= c[:, :C]) & (r // DS == c[:, :C] // DS),
        "str4": (r < c[:, :C]) & (r // DS == c[:, :C] // DS),
    }
    return np.concatenate([parts[n].astype(np.float32) for n, _ in CONSTS], axis=1)


class Job:

    def __init__(self, i, c):
        self.i, self.c, self.slot = i, c, c % 2

    def num(self, off=0):
        return 2 * self.i + (self.c + off) if not isinstance(self.i, int) else 2 * self.i + self.c + off

    def half(self, off=0):
        return self.i + (self.c + off) // 2

    def next(self):
        return Job(self.i, self.c + 1)


def wait(eng, sem, value):
    if isinstance(value, int) and value <= 0:
        return
    eng.wait_ge(sem, value)


def jobs(eng, first, n, body):
    for j in range(min(n, 2)):
        body(Job(0, first + j), j)
    if n > 2:
        with eng.Fori(0, (n - 2) // 2) as i:
            for u in range(2):
                body(Job(i, first + 2 + u), 2 * i + (2 + u))


class Chain:

    def __init__(self, eng, sem):
        self.eng, self.sem, self.n = eng, sem, 0

    def step(self, ins):
        self.n += 1
        ins.then_inc(self.sem, 1)
        self.eng.wait_ge(self.sem, self.n)


def build(nc, a, o):
    ctx = ExitStack()
    with ctx:
        base = (nc.sbuf_base + 31) // 32 * 32
        LIM = nc.sbuf_base + nc.sbuf_bytes_remaining
        R1 = base
        WR = R1 + 67584
        TR = WR + 24576
        XR = TR + 4 * 4224
        PRS = XR + 33792 + 67584
        cur = {}

        def at(region, name, shape, dt=F32, off=None):
            if off is None:
                off = cur.get(region, 0)
            size = int(np.prod(shape[1:])) * 4
            size = (size + 31) // 32 * 32
            cur[region] = off + size
            t = nc.alloc_sbuf_tensor_at(name, shape, dt, offset=region + off)
            assert region + off + size <= LIM, name
            return t

        sem = lambda name: ctx.enter_context(nc.semaphore(name))

        ident = at(PRS, "ident", [P, P])
        ones = at(PRS, "ones", [P, P])
        vec = at(PRS, "vec", [P, NV])
        gains = vec[:, 0:4 * KT].rearrange("p (n k) -> p n k", k=KT)
        cvp = vec[:, 4 * KT:4 * KT + 3 * CT].rearrange("p (n k) -> p n k", k=CT)
        g2 = vec[:, NV - 1:NV]
        eps = at(PRS, "eps", [P, 1])
        rtok = at(PRS, "rtok", [P, 16])
        ltok = at(PRS, "ltok", [P, 16])
        assert PRS + cur[PRS] <= LIM

        w_raw = [at(WR, f"w_raw{s}", [P, KT, P]) for s in range(2)]
        w_hi = [at(WR, f"w_hi{s}", [P, KT, P], F32R) for s in range(2)]
        w_lo = [at(WR, f"w_lo{s}", [P, KT, P], F32R) for s in range(2)]
        tmp = [at(TR, f"tmp{n}", [P, TOK]) for n in range(4)]
        rsb, t1, t2, t3 = tmp

        hm = [at(R1, f"hm_{n}", [P, KT, TOK], F32R, off=o_) for n, o_ in (("hi", 0), ("lo", 33792))]
        op = [at(R1, f"op_{n}", [P, KT, TOK], F32R, off=o_) for n, o_ in (("hi", 0), ("lo", 33792))]
        uu = [at(R1, f"u_{n}", [P, KT, TOK], F32R, off=o_) for n, o_ in (("hi", 0), ("lo", 33792))]
        pT = at(R1, "pT", [P, PK, TOK], off=0)
        pp = [at(R1, f"p_{n}", [P, PK, TOK], F32R) for n in ("hi", "lo")]
        prow = at(R1, "prow", [P, NT + 1, PLE])
        gt = at(R1, "gt", [P, TOK])
        pg = at(R1, "pg", [P, TOK])
        yrow = at(R1, "yrow", [P, NT + 1, D], off=0)
        hh = [at(XR, f"h_{n}", [P, KT, TOK], F32R, off=33792 * o_) for n, o_ in (("hi", 1), ("lo", 2))]
        xT = at(XR, "xT", [P, KT, TOK], off=0)

        xT0 = at(XR, "xT0", [P, KT, TOK], off=0)
        zs = at(XR, "zs", [P, PR, TOK], off=0)
        gl = at(XR, "gl", [P, CT, TOK])
        qkv0 = cur[XR]
        xin = at(XR, "xin", [P, NT + 1, D])
        hq = at(XR, "hq", [DB * QH, QT * P])
        hc = at(XR, "hc", [4 * HIST, 2, CC])
        assert cur[XR] <= qkv0 + QT * TOK * 4
        qkvT = at(XR, "qkvT", [P, QT, TOK], off=qkv0)
        gls = at(XR, "gls", [P, CT, DB, HIST + DS])
        raws = at(XR, "raws", [P, QT, DB, QH + DS])
        tail = at(XR, "tail", [P, QT, QH + DB * QH])
        consts = {}
        for name, w in CONSTS[2:]:
            consts[name] = at(XR, "c_" + name, [P, w])
        wsh = at(XR, "wsh", [P, SC, QT])
        wdw = at(XR, "wdw", [P, DWC, CT])
        ab = at(XR, "ab", [P, NT + 1, 2 * H])
        hp = at(XR, "hp", [P, 2, H])
        sm = [at(XR, f"sm{n}", [P, NT + 1, H]) for n in range(4)]
        beta = at(XR, "beta", [P, NT + 1, H])
        gg = at(XR, "gg", [P, NT + 1, H])
        egc = at(XR, "egc", [P, NT + 1, H])
        ekd = at(XR, "ekd", [P, NT + 1, H])
        gld = at(XR, "gld", [P, NT, CPT, PR])
        glds = at(XR, "glds", [P, DB, PR])
        assert cur[XR] <= 33792 + 67584, cur[XR]

        sqd = at(TR, "sqd", [P, D], off=3 * 4224)
        vrow = at(TR, "vrow", [NV, P], off=4224)
        srow = at(TR, "srow", [SC * QT, P])
        drow = at(TR, "drow", [DWC * CT, P])
        qrow = at(R1, "qrow", [QH + DB * QH, QT * P], off=0)
        grow = at(R1, "grow", [HIST, CC])
        gsrow = at(R1, "gsrow", [NS, CC])

        HT = NT // 2
        Vb = at(R1, "Vb", [P, HT, DW], off=0)
        Kbe = at(R1, "Kbe", [P, HT, DW])
        Kd = at(R1, "Kd", [P, HT, DW])
        QdT = at(R1, "QdT", [P, HT, PR, P])
        LQ = at(R1, "LQ", [P, HT, H, 2, C])
        Tbd = at(R1, "Tbd", [P, HT, H, P])
        WT = at(R1, "WT", [P, HT, PR, P])
        S = at(R1, "S", [P, PR, HD])
        assert cur[R1] <= 67584
        tk = [at(WR, f"tk{n}", [P, DW], off=2048 * n) for n in range(4)]
        KTl = at(WR, "KTl", [P, PR, P])
        RR = at(WR, "RR", [P, PR, 2, P])
        ug = at(WR, "ug", [P, H, P])
        Dm = at(WR, "Dm", [P, H, C])
        sc = at(WR, "sc", [P, 6, H])
        ss = at(WR, "ss", [P, 2 * H])
        Sd = at(WR, "Sd", [P, PR, HD])
        gr = at(WR, "gr", [P, NT, CPT, H])
        grs = at(WR, "grs", [NS, DB, H])
        assert cur[WR] <= 24576, cur[WR]
        Lp = at(TR, "Lp", [P, C * C], off=0)
        Xp = at(TR, "Xp", [P, C * C])
        prod = at(TR, "prod", [P, C * C])
        sqt = at(TR, "sqt", [P, 2 * DW])
        onr = at(TR, "onr", [P, DW], off=0)
        Vn = at(TR, "Vn", [P, DW])
        S0 = at(R1, "S0", [P, PR, DB, HD], off=40960)
        VnM = at(R1, "VnM", [NS, H, DB, HD])
        WQ = at(R1, "WQ", [P, PR, 2, NS], off=24576)
        WSt = at(R1, "WSt", [P, PR, 2, NS])
        Ns = at(R1, "Ns", [NS, H, C])
        NTs = at(R1, "NTs", [NS, H, C])
        Ms = at(R1, "Ms", [NS, H, C])
        Ts = at(R1, "Ts", [NS, H, C])
        assert cur[R1] <= 32768

        ps = ctx.enter_context(nc.psum_tensor("ps", [P, 8, 512], F32))

        def acc(slot, m=P):
            return ps[0:m, 3 * slot:3 * slot + 3, 0:CW]

        def tri3(t):
            return t.rearrange("p (c n) -> p c n", c=NCH)

        xT_dram = nc.dram_tensor("xT_dram", [D, TOK], F32).ap().rearrange("(k p) t -> p k t", p=P)
        lt_dram = nc.dram_tensor("lt_dram", [2, P, C * C], F32).ap()
        tt_dram = nc.dram_tensor("tt_dram", [2, P, C * C], F32).ap()

        ld_x = [sem(f"ld_x{i}") for i in range(NT + 1)]
        ld_i = sem("ld_ident")
        ld_c = sem("ld_consts")
        init = sem("init_done")
        vec_tr = sem("vec_tr")
        vec_cp = sem("vec_cp")
        ld_h = sem("ld_h")
        x_sq = sem("x_sq")
        x_tr = sem("x_tr")
        x_cp = sem("x_cp")
        x_ln = sem("x_ln")
        x_dg = sem("x_dg")
        x_bc = sem("x_bc")
        x_rs = sem("x_rs")
        h_hi = sem("h_hi")
        h_lo = sem("h_lo")
        hs_tr = sem("hs_tr")
        hs_cp = sem("hs_cp")
        st_x = sem("st_x")
        w_dma = [sem(f"w_dma{s}") for s in range(2)]
        w_hid = sem("w_hi_done")
        w_lod = sem("w_lo_done")
        mm = sem("mm_done")
        pf = sem("psum_free")
        y_done = sem("conv_done")
        silu_done = sem("silu_done")
        raw_done = sem("raw_done")
        sg_in = sem("sg_in")
        sg_done = sem("sg_done")
        sgr_done = sem("sgr_done")
        z_in = sem("z_in")
        z_done = sem("z_done")
        dch = sem("dve_chain")
        ach = sem("act_chain")
        cv_acc = sem("cv_acc")
        cv_mm = sem("cv_mm")
        cv_c = sem("cv_centred")
        cv_sq = sem("cv_sq")
        cv_var = sem("cv_var")
        cv_r = sem("cv_r")
        cv_n = sem("cv_n")
        cv_out = sem("cv_out")
        hist_tr = sem("hist_tr")
        hist_cp = sem("hist_cp")
        st_h = sem("st_h")
        ab_tr, ab_cp = sem("ab_tr"), sem("ab_cp")
        gs_act, gs_dve, gs_mm = sem("gs_act"), sem("gs_dve"), sem("gs_mm")
        d_ug, d_mm, d_exp, d_msk = sem("d_ug"), sem("d_mm"), sem("d_exp"), sem("d_msk")
        g_tok, g_sq, g_ss, g_r, g_sc = (sem(n) for n in ("g_tok", "g_sq", "g_ss", "g_r", "g_sc"))
        g_big, g_bt, g_ev, g_aq, g_lq = (sem(n) for n in ("g_big", "g_bt", "g_ev", "g_aq", "g_lq"))
        tb0, lt_st, lt_ld, inv, tt_st, tt_ld = (sem(n) for n in ("tbd_zero", "lt_st", "lt_ld", "inv_done", "tt_st", "tt_ld"))
        uw_mm, uw_ev = sem("uw_mm"), sem("uw_ev")
        ws_mm, vn_d, ds_mm, s_up, o_mm = (sem(n) for n in ("ws_mm", "vn_done", "ds_mm", "s_up", "o_mm"))
        o_sq, o_ss, o_r, o_n, o_tr, o_g = (sem(n) for n in ("o_sq", "o_ss", "o_r", "o_n", "o_tr", "o_gated"))
        st_s, ld_s = sem("st_s"), sem("ld_s")
        sp_mm, sp_dve, sp_act = sem("sample_mm"), sem("sample_dve"), sem("sample_act")
        op_hi, op_lo = sem("op_hi"), sem("op_lo")
        ld_xT = sem("ld_xT")
        x_new = sem("x_new")
        sq_done, ss_done = sem("sq_done"), sem("ss_done")
        st_mm, st_ln = sem("stat_mm"), sem("stat_ln")
        rs_done = sem("rs_done")
        r_done, t_done, u_hi, u_sq, u_lo = (sem(n) for n in ("relu_done", "t_done", "u_hi_done", "u_sq", "u_lo_done"))
        gt_in, gt_done, pg_done = sem("gt_in"), sem("gt_done"), sem("pg_done")
        ld_p, p_tr, p_cp, p_hi, p_lo = (sem(n) for n in ("ld_p", "p_tr", "p_cp", "p_hi_done", "p_lo_done"))
        xg_done, y_mm, y_r, y_tr, y_cp, st_y = (sem(n) for n in ("xg_done", "y_mm", "y_r", "y_tr", "y_cp", "st_y"))

        w_in, w_out = a["w_in"][0], a["w_out"][0]
        w_up, w_down = a["w_up"][0], a["w_down"][0]
        w_ple, w_gate = a["w_ple"][0], a["w_ple_gate"][0]

        def tile_tokens(i):
            return (P, i * P) if i < NT else (NS, SEQ)

        def dg(i):
            return t1[:, i * P:(i + 1) * P] if i < NT else t2[:, 0:P]

        def pick(t, m):
            return t[:, m, :] if isinstance(m, int) else t[:, bass.ds(m, 1), :].rearrange("p a t -> p (a t)")

        block = ctx.enter_context(nc.Block())

        @block.sync
        def _(sp):
            def load_w(job, src, kts=KT, cols=P):
                wait(sp, w_lod, job.num(-1))
                sp.dma_start(w_raw[job.slot][:, 0:kts, 0:cols], src.rearrange("(k p) c -> p k c", p=P))\
                  .then_inc(w_dma[job.slot], 16)

            cin = a["consts"]
            off = 0
            for name, w in CONSTS:
                dst = {"ident": ident, "ones": ones}.get(name) or consts[name]
                sp.dma_start(dst[:, :], cin[:, off:off + w]).then_inc(ld_i if off == 0 else ld_c, 16)
                off += w
                if name == "ident":
                    for i in range(2):
                        n, t0 = tile_tokens(i)
                        sp.dma_start(xin[0:n, i, :], a["x_prompt"][0, t0:t0 + n, :]).then_inc(ld_x[i], 16)
            for i in range(2, NT + 1):
                n, t0 = tile_tokens(i)
                src = a["x_prompt"][0, t0:t0 + n, :] if i < NT else a["x_sample"].rearrange("b t d -> (b t) d")
                sp.dma_start(xin[0:n, i, :], src).then_inc(ld_x[i], 16)
            load_w(Job(0, J_AB), w_in[:, O_B:O_B + 2 * H], cols=2 * H)
            load_w(Job(0, 1), w_in[:, 0:P])
            sp.wait_ge(x_cp, 2 * (NT + 1))
            sp.dma_start(xT_dram, xT0[:, :, :]).then_inc(st_x, 16)
            for j in range(1, QT):
                load_w(Job(0, J_QKV + j), w_in[:, j * P:(j + 1) * P])
            for p in range(CT):
                load_w(Job(0, J_GLU + 2 * p), w_in[:, O_GB + p * P:O_GB + (p + 1) * P])
                load_w(Job(0, J_GLU + 2 * p + 1), w_in[:, O_GA + p * P:O_GA + (p + 1) * P])
            for j in range(PR):
                load_w(Job(0, J_Z + j), w_in[:, O_Z + j * P:O_Z + (j + 1) * P])
            sp.dma_start(o["conf_s"][0, :, 0:HIST - DS, :], a["state_conf_conv"][0, :, DS:HIST, :]).then_inc(st_h, 16)
            sp.wait_ge(hist_cp, 1)
            sp.dma_start(o["conf_p"][0, 0], grow[0:HIST, :]).then_inc(st_h, 16)
            sp.wait_ge(hist_cp, 2)
            for b in range(DB):
                sp.dma_start(o["conf_s"][0, b, HIST - DS:HIST, :], gsrow[b * DS:(b + 1) * DS, :]).then_inc(st_h, 16)
            sp.wait_ge(hist_cp, 5)
            sp.dma_start(o["qkv_p"][0, 0], qrow[0:QH, :]).then_inc(st_h, 16)
            sp.dma_start(o["qkv_s"][0].rearrange("b r c -> (b r) c"), qrow[QH:QH + DB * QH, :]).then_inc(st_h, 16)
            for half in range(2):
                for ti in range(HT):
                    sp.wait_ge(g_lq, half * HT + ti + 1)
                    dst = lt_dram[half].rearrange("(s t b) (m c) -> t (b m) s c", t=HT, b=CPT, c=C)[ti]
                    sp.dma_start(dst, LQ[:, ti, :, 0, :]).then_inc(lt_st, 16)
                sp.wait_ge(lt_st, 16 * HT * (half + 1))
                if half == 0:
                    sp.wait_ge(hist_cp, 5)
                else:
                    sp.wait_ge(o_g, HT)
                sp.dma_start(Lp[:, :], lt_dram[half]).then_inc(lt_ld, 16)
                sp.wait_ge(inv, half + 1)
                sp.dma_start(tt_dram[half], Xp[:, :]).then_inc(tt_st, 16)
                sp.wait_ge(tt_st, 16 * (half + 1))
                if half == 0:
                    sp.wait_ge(tb0, 1)
                for ti in range(HT):
                    for b in range(CPT):
                        src = tt_dram[half].rearrange("(s t b) (m c) -> t b m s c", t=HT, b=CPT, c=C)[ti, b]
                        sp.dma_start(Tbd[b * C:(b + 1) * C, ti, :, b * C:(b + 1) * C], src).then_inc(tt_ld, 16)
            sp.wait_ge(s_up, NT * CPT + 1)
            for par in range(2):
                sp.dma_start(o["ssm_p"][0, 0].rearrange("(q r) d e -> r d q e", r=2)[par],
                             S[par * HD:(par + 1) * HD, :, :]).then_inc(st_s, 16)
            sp.wait_ge(o_tr, NT)
            for par in range(2):
                for q in range(PR):
                    sp.dma_start(S0[par * HD:(par + 1) * HD, q, :, :],
                                 a["state_ssm"][0, :, 2 * q + par].rearrange("b d e -> d b e")).then_inc(ld_s, 16)
            sp.wait_ge(sp_dve, 13)
            for par in range(2):
                for q in range(PR):
                    sp.dma_start(o["ssm_s"][0, :, 2 * q + par].rearrange("b d e -> d b e"),
                                 S0[par * HD:(par + 1) * HD, q, :, :]).then_inc(st_s, 16)
            sp.wait_ge(o_g, NT + 1)
            for j in range(2):
                load_w(Job(0, J_OUT + j), w_out[:, j * P:(j + 1) * P])
            sp.wait_ge(op_lo, KT)
            sp.wait_ge(st_x, 16)
            sp.dma_start(xT[:, :, :], xT_dram).then_inc(ld_xT, 16)
            with sp.Fori(0, (KT - 2) // 2) as i:
                for u in range(2):
                    load_w(Job(i, J_OUT + 2 + u), w_out[:, bass.ds((2 * i + 2 + u) * P, P)])
            for q in range(FQ):
                up, down = J_MLP + 2 * KT * q, J_MLP + 2 * KT * q + KT
                with sp.Fori(0, KT // 2) as i:
                    for u in range(2):
                        load_w(Job(i, up + u), w_up[:, bass.ds((2 * i + u + q * KT) * P, P)])
                with sp.Fori(0, KT // 2) as i:
                    for u in range(2):
                        load_w(Job(i, down + u), w_down[q * D:(q + 1) * D, bass.ds((2 * i + u) * P, P)])
            for i in range(NT + 1):
                n, t0 = tile_tokens(i)
                src = a["p_prompt"][0, 0, t0:t0 + n, :] if i < NT else a["p_sample"][0].rearrange("b t d -> (b t) d")
                if i == 0:
                    sp.wait_ge(mm, J_GATE)
                sp.dma_start(prow[0:n, i, :], src).then_inc(ld_p, 16)
            for m in range(KT):
                load_w(Job(0, J_GATE + 2 * m), w_gate[:, m * P:(m + 1) * P])
                load_w(Job(0, J_GATE + 2 * m + 1), w_ple[:, m * P:(m + 1) * P], kts=PK)
            for i in range(NT + 1):
                n, t0 = tile_tokens(i)
                sp.wait_ge(y_cp, i + 1)
                dst = o["y_p"][0, t0:t0 + n, :] if i < NT else o["y_s"].rearrange("b t d -> (b t) d")
                sp.dma_start(dst, yrow[0:n, i, :]).then_inc(st_y, 16)
            sp.wait_ge(st_y, 16 * (NT + 1))
            sp.wait_ge(st_s, 16 * (2 + 2 * PR))
            sp.wait_ge(st_h, 16 * (2 + DB + 2))
            sp.wait_ge(lt_st, 16 * NT)
            sp.wait_ge(tt_st, 32)
            sp.wait_ge(st_x, 16)

        @block.gpsimd
        def _(pool):
            for p in range(CT):
                pool.wait_ge(sg_done, p + 1)
                if p:
                    pool.wait_ge(pf, J_GLU + 2 * p)
                nc.gpsimd.tensor_tensor(t2[:, :], t1[:, :], rsb[:, :], ALU.mult).then_inc(sgr_done, 1)

            pool.wait_ge(mm, J_OUT)
            nc.gpsimd.memset(Tbd[:, :, :, :], 0.0).then_inc(tb0, 1)

            def sum_squares(phase):
                for m in range(1, KT):
                    pool.wait_ge(sq_done, phase * KT + m + 1)
                    if m > 1:
                        pool.wait_ge(ss_done, phase * (KT - 1) + m - 1)
                    nc.gpsimd.tensor_tensor(t3[:, :], t3[:, :], t2[:, :], ALU.add).then_inc(ss_done, 1)

            sum_squares(0)
            for q in range(FQ):
                def hidden(job, j, q=q):
                    n = q * KT + j
                    wait(pool, t_done, n + 1)
                    if q or not isinstance(j, int) or j:
                        wait(pool, u_lo, n)
                    nc.gpsimd.tensor_tensor(t3[:, :], t2[:, :], t2[:, :], ALU.mult).then_inc(u_sq, 1)
                jobs(pool, J_MLP + 2 * KT * q, KT, hidden)
            sum_squares(1)
            sum_squares(2)

        @block.scalar
        def _(act):
            ac = Chain(act, ach)

            def split_hi(job, kts=KT, cols=P):
                wait(act, w_dma[job.slot], 16 * job.half() + 16)
                wait(act, mm, job.num(-1))
                nc.scalar.activation(w_hi[job.slot][:, 0:kts, 0:cols], w_raw[job.slot][:, 0:kts, 0:cols],
                                     ACT.Copy).then_inc(w_hid, 1)

            for n, (name, k) in enumerate((("g_mix", KT), ("g_mlp", KT), ("g_ple", KT), ("g_final", KT),
                                           ("b_dw", CT), ("g_cln", CT), ("b_cln", CT))):
                src = a[name] if name == "g_final" else a[name][0]
                r0 = n * KT if n < 4 else 4 * KT + (n - 4) * CT
                act.dma_start(vrow[r0:r0 + k, :], src.rearrange("(k p) -> k p", p=P)).then_inc(ld_h, 16)
            for par in range(2):
                act.dma_start(vrow[NV - 1:NV, par * HD:(par + 1) * HD], a["g_o"]).then_inc(ld_h, 16)
            act.dma_start(srow[:, :], a["w_short"][0].rearrange("j (m p) -> (j m) p", p=P)).then_inc(ld_h, 16)
            act.dma_start(drow[:, :], a["w_dw"][0].rearrange("j (m p) -> (j m) p", p=P)).then_inc(ld_h, 16)
            act.dma_start(hq[:, :], a["state_qkv_conv"][0].rearrange("b r c -> (b r) c")).then_inc(ld_h, 16)
            for g in range(2):
                act.dma_start(hc[:, g, :], a["state_conf_conv"][0, 4 * g:4 * g + 4].rearrange("b r c -> (b r) c")).then_inc(ld_h, 16)
            act.dma_start(hp[:, 0, :], a["a_log"].to_broadcast([P, H])).then_inc(ld_h, 16)
            act.dma_start(hp[:, 1, :], a["dt_bias"].to_broadcast([P, H])).then_inc(ld_h, 16)
            act.wait_ge(init, 3)
            for i in range(NT + 1):
                n, t0 = tile_tokens(i)
                act.wait_ge(ld_x[i], 16)
                if i:
                    act.wait_ge(x_sq, i)
                nc.scalar.activation(sqd[0:n, :], xin[0:n, i, :], ACT.Square, accum_out=rtok[0:n, i:i + 1]).then_inc(x_sq, 1)
                for g in range(2):
                    act.wait_ge(x_tr, 2 * i + g + 1)
                    nc.scalar.activation(xT0[:, 4 * g:4 * g + 4, t0:t0 + n],
                                         ps[:, (2 * i + g) % 6, :].rearrange("p (k t) -> p k t", k=4)[:, :, 0:n],
                                         ACT.Copy).then_inc(x_cp, 1)
            act.wait_ge(x_sq, NT + 1)
            ac.step(nc.scalar.activation(ltok[:, 0:NT + 1], rtok[:, 0:NT + 1], ACT.Ln, bias=eps[:, :], scale=1.0 / D))
            nc.scalar.activation(rtok[:, 0:NT + 1], ltok[:, 0:NT + 1], ACT.Exp, scale=-0.5).then_inc(x_ln, 1)
            split_hi(Job(0, J_AB), cols=2 * H)
            act.wait_ge(x_cp, 2 * (NT + 1))
            act.wait_ge(vec_cp, 3)
            for k in range(KT):
                nc.scalar.activation(hm[0][:, k, :], xT0[:, k, :], ACT.Copy, scale=gains[:, 0, k:k + 1]).then_inc(h_hi, 1)
            for g in range(3):
                act.wait_ge(x_bc, g + 1)
                w = 4 * P if g < 2 else NS
                nc.scalar.activation(rsb[:, g * 512:g * 512 + w], ps[:, 3 + g, 0:w], ACT.Copy).then_inc(x_rs, 1)
            split_hi(Job(0, 1))

            for j in range(QT):
                split_hi(Job(0, J_QKV + j + 1))
                act.wait_ge(y_done, j + 1)
                nc.scalar.activation(qkvT[:, j, :], (t2, t3)[j % 2][:, :], ACT.Silu).then_inc(silu_done, 1)
            for p in range(CT):
                split_hi(Job(0, J_GLU + 2 * p + 1))
                act.wait_ge(pf, J_GLU + 2 * p + 1)
                if p:
                    act.wait_ge(sgr_done, p)
                nc.scalar.activation(t1[:, :], t3[:, :], ACT.Sigmoid).then_inc(sg_done, 1)
                split_hi(Job(0, J_GLU + 2 * p + 2))
            act.wait_ge(st_x, 16)
            for j in range(PR):
                if j < PR - 1:
                    split_hi(Job(0, J_Z + j + 1))
                act.wait_ge(pf, J_Z + j + 1)
                nc.scalar.activation(zs[:, j, :], (t1, t2)[j % 2][:, :], ACT.Silu).then_inc(z_done, 1)

            act.wait_ge(hist_tr, 1)
            act.wait_ge(z_done, PR)
            nc.scalar.activation(grow[0:HIST, :], ps[0:HIST, 6, :], ACT.Copy).then_inc(hist_cp, 1)
            act.wait_ge(hist_tr, 2)
            nc.scalar.activation(gsrow[0:NS, :], ps[0:NS, 7, :], ACT.Copy).then_inc(hist_cp, 1)
            for g in range(3):
                act.wait_ge(hist_tr, 3 + g)
                nc.scalar.activation(qrow[:, g * 512:(g + 1) * 512], ps[0:QH + DB * QH, g, :], ACT.Copy).then_inc(hist_cp, 1)
            for p in range(CT):
                act.wait_ge(cv_c, p + 1)
                nc.scalar.activation(t2[:, :], t1[:, :], ACT.Square).then_inc(cv_sq, 1)
                act.wait_ge(cv_var, p + 1)
                ac.step(nc.scalar.activation(tri3(t2[:, :]), acc(1), ACT.Ln, bias=eps[:, :]))
                nc.scalar.activation(t2[:, :], t2[:, :], ACT.Exp, scale=-0.5).then_inc(cv_r, 1)
                act.wait_ge(cv_n, p + 1)
                nc.scalar.activation(gl[:, p, 0:TOK], t1[:, :], ACT.Silu, bias=cvp[:, 2, p:p + 1],
                                     scale=cvp[:, 1, p:p + 1]).then_inc(cv_out, 1)

            a_n = [0]

            def small(out, in_, f, **kw):
                nc.scalar.activation(out, in_, f, **kw).then_inc(gs_act, 1)
                a_n[0] += 1
                act.wait_ge(gs_act, a_n[0])

            act.wait_ge(ab_cp, 1)
            small(beta[:, :, :], ab[:, :, 0:H], ACT.Exp, scale=-1.0)
            act.wait_ge(gs_dve, 3)
            small(sm[1][:, :, :], sm[1][:, :, :], ACT.Exp, scale=-1.0)
            small(sm[2][:, :, :], sm[1][:, :, :], ACT.Ln, bias=1.0)
            small(hp[:, 0, :], hp[:, 0, :], ACT.Exp)
            act.wait_ge(gs_mm, 1)
            nc.scalar.activation(egc[:, :, :], ps[:, 0, 0:(NT + 1) * H].rearrange("p (t h) -> p t h", h=H), ACT.Exp).then_inc(gs_act, 1)
            nc.scalar.activation(ekd[:, :, :], ps[:, 1, 0:(NT + 1) * H].rearrange("p (t h) -> p t h", h=H), ACT.Exp).then_inc(gs_act, 1)
            for par in range(2):
                rows = slice(par * HD, (par + 1) * HD)
                nc.scalar.activation(gld[rows, :, :, :].rearrange("p t b q -> p (t b) q"),
                                     ps[rows, 2, 0:NT * CPT * H].rearrange("p (t q r) -> p t q r", q=PR, r=2)[:, :, :, par],
                                     ACT.Exp).then_inc(gs_act, 1)
                nc.scalar.activation(glds[rows, :, :], ps[rows, 3, 0:DB * H].rearrange("p (t q r) -> p t q r", q=PR, r=2)[:, :, :, par],
                                     ACT.Exp).then_inc(gs_act, 1)

            def prep(t):
                n, _ = tile_tokens(t)
                ti = t % HT
                act.wait_ge(d_mm, t + 1)
                if t:
                    act.wait_ge(g_lq, t)
                for b in range(n // C):
                    r = slice(b * C, (b + 1) * C)
                    nc.scalar.activation(Dm[r, :, :], ps[r, 6:8, :].rearrange("p k (s c) -> p (k s) c", c=P)[:, :, r],
                                         ACT.Exp).then_inc(d_exp, 1)
                act.wait_ge(g_tok, 3 * t + 2)
                if t:
                    act.wait_ge(g_ss, t)
                nc.scalar.activation(sqt[0:n, :].rearrange("p (a b) -> p a b", a=2), ps[0:n, 0:2, :], ACT.Square).then_inc(g_sq, 1)
                act.wait_ge(g_ss, t + 1)
                ac.step(nc.scalar.activation(ss[0:n, :], ss[0:n, :], ACT.Ln, bias=eps[0:n, :]))
                nc.scalar.activation(ss[0:n, :], ss[0:n, :], ACT.Exp, scale=-0.5).then_inc(g_r, 1)
                outs = (KTl[:, :, 0:n], RR[:, :, 0, 0:n], RR[:, :, 1, 0:n],
                        QdT[:, ti, :, 0:n] if t < NT else WQ[:, :, 1, :])
                for k in range(4):
                    act.wait_ge(g_bt, 4 * t + k + 1)
                    nc.scalar.activation(outs[k], ps[:, 3 + k, :].rearrange("p (q t) -> p q t", q=PR)[:, :, 0:n],
                                         ACT.Copy).then_inc(g_ev, 1)

            def gate(t):
                n, _ = tile_tokens(t)
                act.wait_ge(o_mm, t + 1)
                if t < NT:
                    src = ps[0:n, 4:6, 0:PR * HD]
                else:
                    src = ps[0:n, 4:5, 0:2 * PR * HD]
                nc.scalar.activation(sqt[0:n, 0:DW].rearrange("p (a b) -> p a b", a=src.shape[1]), src, ACT.Square).then_inc(o_sq, 1)
                act.wait_ge(o_ss, t + 1)
                ac.step(nc.scalar.activation(ss[0:n, 0:H], ss[0:n, 0:H], ACT.Ln, bias=eps[0:n, :], scale=1.0 / HD))
                nc.scalar.activation(ss[0:n, 0:H], ss[0:n, 0:H], ACT.Exp, scale=-0.5).then_inc(o_r, 1)

            act.wait_ge(st_h, 16 * (4 + DB))
            for half in range(2):
                for ti in range(HT):
                    prep(half * HT + ti)
                for ti in range(HT):
                    t = half * HT + ti
                    act.wait_ge(uw_mm, 2 * t + 1)
                    nc.scalar.activation(Vb[:, ti, :], ps[:, 0, :], ACT.Copy).then_inc(uw_ev, 1)
                    act.wait_ge(uw_mm, 2 * t + 2)
                    nc.scalar.activation(WT[:, ti, :, :], ps[:, 1, :].rearrange("p (q t) -> p q t", q=PR), ACT.Copy).then_inc(uw_ev, 1)
                    gate(t)
            prep(NT)
            act.wait_ge(sp_mm, 1)
            nc.scalar.activation(NTs[:, :, :], ps[0:NS, 0, 0:H * C].rearrange("p (s c) -> p s c", c=C), ACT.Copy).then_inc(sp_act, 1)
            act.wait_ge(sp_mm, 4)
            nc.scalar.activation(Vb[0:NS, 0, :], ps[0:NS, 0, :], ACT.Copy).then_inc(sp_act, 1)
            nc.scalar.activation(WQ[:, :, 0, :], ps[:, 1, :].rearrange("p (q t) -> p q t", q=PR)[:, :, 0:NS], ACT.Copy).then_inc(sp_act, 1)
            act.wait_ge(sp_mm, 5)
            nc.scalar.activation(WSt[:, :, :, :], ps[:, 2, 0:PR * 2 * NS].rearrange("p (q w t) -> p q w t", q=PR, w=2), ACT.Copy).then_inc(sp_act, 1)
            gate(NT)

            act.wait_ge(o_g, NT + 1)
            split_hi(Job(0, J_OUT))
            act.wait_ge(st_s, 16 * (2 + 2 * PR))
            for k in range(KT):
                src = zs[:, k, :] if k < PR else gl[:, k - PR, 0:TOK]
                nc.scalar.activation(op[0][:, k, :], src, ACT.Copy).then_inc(op_hi, 1)

            def norm_tail(phase, m, final, value):
                act.wait_ge(final, value)
                if m == 0 and phase == 1:
                    act.wait_ge(u_lo, FQ * KT)
                if m == 1 and phase == 1:
                    act.wait_ge(u_sq, FQ * KT)
                if m > 1:
                    act.wait_ge(ss_done, phase * (KT - 1) + m - 1)
                nc.scalar.activation((t2 if m else t3)[:, :], xT[:, m, :], ACT.Square).then_inc(sq_done, 1)
                if phase < 2:
                    nc.scalar.activation(hh[0][:, m, :], xT[:, m, :], ACT.Copy, scale=gains[:, phase + 1, m:m + 1]).then_inc(h_hi, 1)

            def stats(n):
                for c in range(NCH):
                    act.wait_ge(st_mm, 3 * n + c + 1)
                    nc.scalar.activation(rsb[:, c * CW:(c + 1) * CW], ps[:, 6 + c % 2, 0:CW], ACT.Ln, bias=eps[:, :],
                                         scale=1.0 / D).then_inc(st_ln, 1)
                act.wait_ge(st_ln, 3 * n + 3)
                nc.scalar.activation(rsb[:, :], rsb[:, :], ACT.Exp, scale=-0.5).then_inc(rs_done, 1)

            for m in range(KT):
                split_hi(Job(0, J_OUT + m + 1))
                norm_tail(0, m, pf, J_OUT + m + 1)
            for q in range(FQ):
                up, down = J_MLP + 2 * KT * q, J_MLP + 2 * KT * q + KT

                def hidden(job, j, q=q):
                    n = q * KT + j
                    split_hi(job.next())
                    if q == 0 and isinstance(j, int) and j == 0:
                        stats(0)
                    wait(act, mm, job.num(1))
                    if isinstance(j, int) and j == 0:
                        wait(act, pf, job.num())
                    wait(act, t_done, n)
                    nc.scalar.activation(tri3(t1[:, :]), acc(job.slot), ACT.Relu).then_inc(pf, 1)
                    wait(act, t_done, n + 1)
                    nc.scalar.activation(pick(uu[0], j), t2[:, :], ACT.Square).then_inc(u_hi, 1)
                jobs(act, up, KT, hidden)
                if q < FQ - 1:
                    jobs(act, down, KT, lambda job, j: split_hi(job.next()))
                else:
                    for m in range(KT):
                        split_hi(Job(0, down + m + 1))
                        norm_tail(1, m, pf, down + m + 1)
            for m in range(KT):
                split_hi(Job(0, J_GATE + 2 * m + 1), kts=PK)
                if m == 0:
                    stats(1)
                act.wait_ge(pf, J_GATE + 2 * m + 1)
                wait(act, x_new, m)
                nc.scalar.activation(gt[:, :], t1[:, :], ACT.Sigmoid).then_inc(gt_done, 1)
                if m < KT - 1:
                    split_hi(Job(0, J_GATE + 2 * m + 2))
                if m == 0:
                    act.wait_ge(p_cp, 6)
                    for k in range(PK):
                        nc.scalar.activation(pp[0][:, k, :], pT[:, k, :], ACT.Copy).then_inc(p_hi, 1)
                norm_tail(2, m, x_new, m + 1)
            act.wait_ge(y_mm, 1)
            nc.scalar.activation(ltok[0:NS, NT:NT + 1], ps[0:NS, 6, NT:NT + 1], ACT.Ln, bias=eps[0:NS, :], scale=1.0 / D)
            ac.step(nc.scalar.activation(ltok[:, 0:NT], ps[:, 6, 0:NT], ACT.Ln, bias=eps[:, :], scale=1.0 / D))
            ac.step(nc.scalar.activation(rtok[:, 0:NT + 1], ltok[:, 0:NT + 1], ACT.Exp, scale=-0.5))
            for i in range(NT + 1):
                n, _ = tile_tokens(i)
                act.wait_ge(y_tr, i + 1)
                nc.scalar.activation(yrow[0:n, i, :].rearrange("p (a b) -> p a b", a=2), ps[0:n, 2 * (i % 3):2 * (i % 3) + 2, :],
                                     ACT.Copy, scale=rtok[0:n, i:i + 1]).then_inc(y_cp, 1)

        @block.tensor
        def _(pe):
            def multiply(job, rhs, kts=KT, m=P, before=None):
                wait(pe, w_lod, job.num(1))
                wait(pe, pf, job.num(-1))
                hi, lo = w_hi[job.slot], w_lo[job.slot]
                for k in range(kts):
                    if before:
                        before(k)
                    for n, (w, x) in enumerate(((hi, rhs[0]), (hi, rhs[1]), (lo, rhs[0]))):
                        for c in range(NCH):
                            last = nc.tensor.matmul(ps[0:m, 3 * job.slot + c, 0:CW], w[:, k, 0:m],
                                                    x[:, k, c * CW:(c + 1) * CW], start=(k == 0 and n == 0),
                                                    stop=(k == kts - 1 and n == 2))
                last.then_inc(mm, 1)

            pe.wait_ge(ld_i, 16)
            for i in range(NT + 1):
                n, _ = tile_tokens(i)
                pe.wait_ge(ld_x[i], 16)
                for g in range(2):
                    if 2 * i + g >= 6:
                        pe.wait_ge(x_cp, 2 * i + g - 5)
                    for k in range(4):
                        last = nc.tensor.transpose(ps[:, (2 * i + g) % 6, k * P:k * P + n],
                                                   xin[0:n, i, (4 * g + k) * P:(4 * g + k + 1) * P], ident[0:n, 0:n])
                    last.then_inc(x_tr, 1)
            pe.wait_ge(ld_h, 16 * 16)
            for rows, n, col in ((vrow, NV, 0), (srow, SC * QT, 64), (drow, DWC * CT, 128)):
                last = nc.tensor.transpose(ps[:, 7, col:col + n], rows[:, :], ident[0:n, 0:n])
            last.then_inc(vec_tr, 1)
            nq = DB * QH
            for m in range(QT):
                last = nc.tensor.transpose(ps[:, 6, m * nq:(m + 1) * nq], hq[:, m * P:(m + 1) * P], ident[0:nq, 0:nq])
            last.then_inc(hs_tr, 1)
            nh = 4 * HIST
            for g in range(2):
                if g:
                    pe.wait_ge(hs_cp, 1)
                else:
                    pe.wait_ge(vec_cp, 3)
                for m in range(CT):
                    last = nc.tensor.transpose(ps[:, 7 - g, m * nh:(m + 1) * nh], hc[:, g, m * P:(m + 1) * P], ident[0:nh, 0:nh])
                last.then_inc(hs_tr, 1)
            pe.wait_ge(x_cp, 2 * (NT + 1))
            pe.wait_ge(ld_c, 16 * (len(CONSTS) - 1))
            for i in range(NT + 1):
                n, _ = tile_tokens(i)
                pe.wait_ge(x_dg, i + 1)
                bank, col = 3 + i // 4, (i % 4) * P
                last = nc.tensor.matmul(ps[:, bank, col:col + n], ones[0:n, :], dg(i)[0:n, 0:n], start=True, stop=True)
                if i in (3, 7, 8):
                    last.then_inc(x_bc, 1)

            def mixer_rows(k):
                pe.wait_ge(h_lo, k + 1)

            multiply(Job(0, J_AB), hm, m=2 * H, before=mixer_rows)
            pe.wait_ge(x_rs, 3)
            for j in range(QT):
                multiply(Job(0, J_QKV + j), hm)
                if j == 0:
                    pe.wait_ge(pf, J_AB + 1)
                    for i in range(NT + 1):
                        n, t0 = tile_tokens(i)
                        last = nc.tensor.transpose(ps[0:n, 7, i * 2 * H:(i + 1) * 2 * H], t3[0:2 * H, t0:t0 + n], ident[0:2 * H, 0:2 * H])
                    last.then_inc(ab_tr, 1)
            for j in range(2 * CT):
                multiply(Job(0, J_GLU + j), hm)
            for j in range(PR):
                multiply(Job(0, J_Z + j), hm)

            pe.wait_ge(pf, J_OUT)
            for m in range(CT):
                last = nc.tensor.transpose(ps[0:HIST, 6, m * P:(m + 1) * P], gl[:, m, SEQ - HIST:SEQ], ident[:, :])
            last.then_inc(hist_tr, 1)
            for m in range(CT):
                last = nc.tensor.transpose(ps[0:NS, 7, m * P:(m + 1) * P], gl[:, m, SEQ:TOK], ident[:, :])
            last.then_inc(hist_tr, 1)
            for g in range(3):
                for k in range(4):
                    last = nc.tensor.transpose(ps[0:QH + DB * QH, g, k * P:(k + 1) * P], tail[:, 4 * g + k, :], ident[:, :])
                last.then_inc(hist_tr, 1)

            for p in range(CT):
                if p == 0:
                    pe.wait_ge(hist_cp, 5)
                pe.wait_ge(cv_acc, p + 1)
                for c in range(NCH):
                    last = nc.tensor.matmul(ps[:, c, 0:CW], consts["bd64"][:, :], t1[:, c * CW:(c + 1) * CW], start=True, stop=True)
                last.then_inc(cv_mm, 1)
                pe.wait_ge(cv_sq, p + 1)
                for c in range(NCH):
                    last = nc.tensor.matmul(ps[:, 3 + c, 0:CW], consts["bd64"][:, :], t2[:, c * CW:(c + 1) * CW], start=True, stop=True)
                last.then_inc(cv_var, 1)

            pe.wait_ge(cv_r, CT)
            pe.wait_ge(cv_c, CT)
            pe.wait_ge(gs_dve, 9)
            nt = NT * H
            gf = gg[:, :, :].rearrange("p t h -> p (t h)")
            nc.tensor.matmul(ps[:, 0, 0:nt], consts["uinc"][:, :], gf[:, 0:nt], start=True, stop=True)
            nc.tensor.matmul(ps[:, 0, nt:nt + H], consts["uinc4"][:, :], gf[:, nt:nt + H], start=True, stop=True)
            nc.tensor.matmul(ps[:, 1, 0:nt], consts["sgt"][:, :], gf[:, 0:nt], start=True, stop=True)
            nc.tensor.matmul(ps[:, 1, nt:nt + H], consts["sgt4"][:, :], gf[:, nt:nt + H], start=True, stop=True)
            nc.tensor.matmul(ps[:, 2, 0:NT * CPT * H], ones[:, :], gr[:, :, :, :].rearrange("p t b h -> p (t b h)"), start=True, stop=True)
            nc.tensor.matmul(ps[:, 3, 0:DB * H], ones[0:NS, :], grs[:, :, :].rearrange("p b h -> p (b h)"), start=True, stop=True)\
              .then_inc(gs_mm, 1)
            pe.wait_ge(gs_act, 10)

            def prep(t):
                n, t0 = tile_tokens(t)
                pe.wait_ge(d_ug, t + 1)
                if t:
                    pe.wait_ge(g_ev, 4 * t)
                for g in range(2):
                    last = nc.tensor.matmul(ps[0:n, 6 + g, :].rearrange("p (s c) -> p s c", c=P)[:, :, 0:n],
                                            consts["sgt" if t < NT else "sgt4"][0:n, 0:n],
                                            ug[0:n, 4 * g:4 * g + 4, 0:n], start=True, stop=True)
                last.then_inc(d_mm, 1)
                if t:
                    pe.wait_ge(g_lq, t)
                for g in range(3):
                    for k in range(4):
                        last = nc.tensor.transpose(ps[0:n, g, k * P:(k + 1) * P], qkvT[:, 4 * g + k, t0:t0 + n], ident[:, :])
                    last.then_inc(g_tok, 1)
                for k in range(4):
                    pe.wait_ge(g_big, 7 * t + k + 1)
                    if k == 3:
                        pe.wait_ge(d_exp, (CPT * t if t < NT else CPT * NT) + n // C)
                    for q in range(PR):
                        last = nc.tensor.transpose(ps[:, 3 + k, q * P:q * P + n], tk[k][0:n, q * P:(q + 1) * P], ident[0:n, 0:n])
                    last.then_inc(g_bt, 1)
                pe.wait_ge(g_ev, 4 * t + 4)
                pe.wait_ge(g_big, 7 * t + 7)
                for s in range(H):
                    par, q = divmod(s, PR)
                    rows = slice(par * HD, (par + 1) * HD)
                    last = nc.tensor.matmul(ps[0:n, s // 2, (s % 2) * 256:(s % 2) * 256 + 256].rearrange("p (w c) -> p w c", w=2)[:, :, 0:n],
                                            KTl[rows, q, 0:n], RR[rows, q, :, 0:n], start=True, stop=True)
                last.then_inc(g_aq, 1)

            def transpose_out(t):
                n, _ = tile_tokens(t)
                pe.wait_ge(o_n, t + 1)
                for q in range(PR):
                    last = nc.tensor.transpose(ps[:, 7, q * P:q * P + n], onr[0:n, q * P:(q + 1) * P], ident[0:n, 0:n])
                last.then_inc(o_tr, 1)

            for half in range(2):
                for ti in range(HT):
                    prep(half * HT + ti)
                pe.wait_ge(tt_ld, 16 * HT * CPT * (half + 1))
                pe.wait_ge(g_lq, HT * (half + 1))
                for ti in range(HT):
                    t = half * HT + ti
                    if ti:
                        pe.wait_ge(uw_ev, 2 * t)
                    for h in range(H):
                        s = (h % 2) * PR + h // 2
                        last = nc.tensor.matmul(ps[:, 0, h * HD:(h + 1) * HD], Tbd[:, ti, s, :], Vb[:, ti, h * HD:(h + 1) * HD], start=True, stop=True)
                    last.then_inc(uw_mm, 1)
                    for h in range(H):
                        s, par, q = (h % 2) * PR + h // 2, h % 2, h // 2
                        last = nc.tensor.matmul(ps[par * HD:(par + 1) * HD, 1, q * P:(q + 1) * P], Kbe[:, ti, h * HD:(h + 1) * HD],
                                                Tbd[:, ti, s, :], start=True, stop=True)
                    last.then_inc(uw_mm, 1)
                    pe.wait_ge(uw_ev, 2 * t + 2)
                    for b in range(CPT):
                        n = t * CPT + b
                        r = slice(b * C, (b + 1) * C)
                        pe.wait_ge(s_up, n + 1)
                        for w, src in ((2, WT), (4, QdT)):
                            if w == 4 and b == 0 and t:
                                pe.wait_ge(o_n, t)
                            for h in range(H):
                                par, q = h % 2, h // 2
                                rows = slice(par * HD, (par + 1) * HD)
                                last = nc.tensor.matmul(ps[r, w + par, q * HD:(q + 1) * HD], src[rows, ti, q, r], S[rows, q, :],
                                                        start=(w == 2 or q == 0), stop=(w == 2), skip_group_check=True)
                            if w == 2:
                                last.then_inc(ws_mm, 1)
                        pe.wait_ge(vn_d, n + 1)
                        for h in range(H):
                            par, q = h % 2, h // 2
                            last = nc.tensor.matmul(ps[par * HD:(par + 1) * HD, 6, q * HD:(q + 1) * HD], Kd[r, ti, h * HD:(h + 1) * HD],
                                                    Vn[r, h * HD:(h + 1) * HD], start=True, stop=True, skip_group_check=True)
                        last.then_inc(ds_mm, 1)
                        for h in range(H):
                            s, par, q = (h % 2) * PR + h // 2, h % 2, h // 2
                            last = nc.tensor.matmul(ps[r, 4 + par, q * HD:(q + 1) * HD], LQ[r, ti, s, 1, :], Vn[r, h * HD:(h + 1) * HD],
                                                    start=False, stop=True, skip_group_check=True)
                        if b == CPT - 1:
                            last.then_inc(o_mm, 1)
                    transpose_out(t)
                pe.wait_ge(o_g, HT * (half + 1))

            prep(NT)
            pe.wait_ge(sp_dve, 1)
            for s in range(H):
                last = nc.tensor.transpose(ps[0:NS, 0, s * C:(s + 1) * C], Ns[:, s, :], ident[0:NS, 0:NS])
            last.then_inc(sp_mm, 1)
            pe.wait_ge(sp_act, 1)
            for s in range(H):
                last = nc.tensor.matmul(ps[0:NS, 1, s * C:(s + 1) * C], NTs[:, s, :], Ns[:, s, :], start=True, stop=True)
            last.then_inc(sp_mm, 1)
            pe.wait_ge(sp_dve, 2)
            for s in range(H):
                last = nc.tensor.matmul(ps[0:NS, 2, s * C:(s + 1) * C], NTs[:, s, :], Ms[:, s, :], start=True, stop=True)
            last.then_inc(sp_mm, 1)
            pe.wait_ge(sp_dve, 3)
            for h in range(H):
                s = (h % 2) * PR + h // 2
                nc.tensor.matmul(ps[0:NS, 0, h * HD:(h + 1) * HD], Ts[:, s, :], Vb[0:NS, 0, h * HD:(h + 1) * HD], start=True, stop=True)
            for h in range(H):
                s, par, q = (h % 2) * PR + h // 2, h % 2, h // 2
                last = nc.tensor.matmul(ps[par * HD:(par + 1) * HD, 1, q * P:q * P + NS], Kbe[0:NS, 0, h * HD:(h + 1) * HD],
                                        Ts[:, s, :], start=True, stop=True)
            last.then_inc(sp_mm, 1)
            pe.wait_ge(sp_act, 3)
            pe.wait_ge(ld_s, 16 * 2 * PR)
            for par in range(2):
                rows = slice(par * HD, (par + 1) * HD)
                for q in range(PR):
                    for b in range(DB):
                        cols = slice(b * DS, (b + 1) * DS)
                        last = nc.tensor.matmul(ps[rows, 2, q * 2 * NS:(q + 1) * 2 * NS].rearrange("p (w t) -> p w t", w=2)[:, :, cols],
                                                S0[rows, q, b, :], WQ[rows, q, :, cols], start=True, stop=True)
            last.then_inc(sp_mm, 1)
            pe.wait_ge(sp_act, 4)
            for q in range(PR):
                last = nc.tensor.transpose(ps[0:NS, 3, q * P:(q + 1) * P], WSt[:, q, 0, :], ident[:, :])
            last.then_inc(sp_mm, 1)
            for q in range(PR):
                nc.tensor.matmul(ps[0:NS, 4, q * P:(q + 1) * P], WSt[:, q, 1, :], ident[:, :], start=(q == 0), stop=False, skip_group_check=True)
            pe.wait_ge(sp_dve, 4)
            for h in range(H):
                s = (h % 2) * PR + h // 2
                last = nc.tensor.matmul(ps[0:NS, 4, h * HD:(h + 1) * HD], LQ[0:NS, 0, s, 1, :], Vn[0:NS, h * HD:(h + 1) * HD],
                                        start=False, stop=True, skip_group_check=True)
            last.then_inc(o_mm, 1)
            pe.wait_ge(sp_dve, 5)
            for h in range(H):
                par, q = h % 2, h // 2
                last = nc.tensor.matmul(ps[par * HD:(par + 1) * HD, q, :], Kd[0:NS, 0, h * HD:(h + 1) * HD],
                                        VnM[:, h, :, :].rearrange("p b e -> p (b e)"), start=True, stop=True)
            last.then_inc(sp_mm, 1)
            transpose_out(NT)

            pe.wait_ge(o_g, NT + 1)
            pe.wait_ge(sp_dve, 13)
            for m in range(KT):
                multiply(Job(0, J_OUT + m), op, before=(lambda k: pe.wait_ge(op_lo, k + 1)) if m == 0 else None)

            def stat(n):
                pe.wait_ge(ss_done, (n + 1) * (KT - 1))
                for c in range(NCH):
                    if c == 2:
                        pe.wait_ge(st_ln, 3 * n + 1)
                    nc.tensor.matmul(ps[:, 6 + c % 2, 0:CW], ones[:, :], t3[:, c * CW:(c + 1) * CW], start=True, stop=True).then_inc(st_mm, 1)

            for q in range(FQ):
                up, down = J_MLP + 2 * KT * q, J_MLP + 2 * KT * q + KT

                def hidden(job, j, q=q):
                    first = q == 0 and isinstance(j, int) and j == 0
                    multiply(job, hh, before=(lambda k: pe.wait_ge(h_lo, KT + k + 1)) if first else None)
                    if first:
                        stat(0)
                jobs(pe, up, KT, hidden)

                def out(job, j, q=q):
                    first = isinstance(j, int) and j == 0
                    multiply(job, uu, before=(lambda k: pe.wait_ge(u_lo, q * KT + k + 1)) if first else None)
                jobs(pe, down, KT, out)

            multiply(Job(0, J_GATE), hh, before=lambda k: pe.wait_ge(h_lo, 2 * KT + k + 1))
            stat(1)
            pe.wait_ge(ld_p, 16 * (NT + 1))
            n_done = 0
            for k in range(PK):
                for g in range(3):
                    if n_done >= 2:
                        pe.wait_ge(p_cp, n_done - 1)
                    else:
                        pe.wait_ge(st_ln, 6)
                    for i in (range(4 * g, 4 * g + 4) if g < 2 else [NT]):
                        n, t0 = tile_tokens(i)
                        last = nc.tensor.transpose(ps[:, 6 + n_done % 2, (i % 4) * P:(i % 4) * P + n], prow[0:n, i, k * P:(k + 1) * P], ident[0:n, 0:n])
                    last.then_inc(p_tr, 1)
                    n_done += 1
            for m in range(KT):
                if m:
                    multiply(Job(0, J_GATE + 2 * m), hh)
                multiply(Job(0, J_GATE + 2 * m + 1), pp, kts=PK, before=(lambda k: pe.wait_ge(p_lo, k + 1)) if m == 0 else None)
            pe.wait_ge(ss_done, 3 * (KT - 1))
            for i in range(NT + 1):
                n, t0 = tile_tokens(i)
                last = nc.tensor.matmul(ps[0:n, 6, i:i + 1], t3[:, t0:t0 + n], ones[:, 0:1], start=True, stop=True)
            last.then_inc(y_mm, 1)
            pe.wait_ge(pf, J_END)
            pe.wait_ge(xg_done, KT)
            for i in range(NT + 1):
                n, t0 = tile_tokens(i)
                if i >= 3:
                    pe.wait_ge(y_cp, i - 2)
                for m in range(KT):
                    last = nc.tensor.transpose(ps[0:n, 2 * (i % 3) + m // 4, (m % 4) * P:(m % 4 + 1) * P], xT[:, m, t0:t0 + n], ident[:, :])
                last.then_inc(y_tr, 1)

        @block.vector
        def _(dve):
            dc = Chain(dve, dch)
            step = dc.step

            def split_lo(job, kts=KT, cols=P):
                wait(dve, w_hid, job.num(1))
                nc.vector.tensor_tensor(w_lo[job.slot][:, 0:kts, 0:cols], w_raw[job.slot][:, 0:kts, 0:cols],
                                        w_hi[job.slot][:, 0:kts, 0:cols].bitcast(F32), ALU.subtract).then_inc(w_lod, 1)

            nc.vector.memset(rtok[:, :], 1.0).then_inc(init, 1)
            nc.vector.memset(eps[:, :], EPS).then_inc(init, 1)
            nc.vector.memset(ab[:, :, :], 0.0).then_inc(init, 1)
            dve.wait_ge(vec_tr, 1)
            nc.vector.tensor_copy(vec[:, :], ps[:, 7, 0:NV]).then_inc(vec_cp, 1)
            nc.vector.tensor_copy(wsh[:, :, :].rearrange("p j m -> p (j m)"), ps[:, 7, 64:64 + SC * QT]).then_inc(vec_cp, 1)
            nc.vector.tensor_copy(wdw[:, :, :].rearrange("p j m -> p (j m)"), ps[:, 7, 128:128 + DWC * CT]).then_inc(vec_cp, 1)
            dve.wait_ge(hs_tr, 1)
            nc.vector.tensor_copy(raws[:, :, :, 0:QH], ps[:, 6, 0:QT * DB * QH].rearrange("p (m b r) -> p m b r", m=QT, b=DB)).then_inc(hs_cp, 1)
            for g in range(2):
                dve.wait_ge(hs_tr, 2 + g)
                for m in range(CT):
                    last = nc.vector.tensor_copy(gls[:, m, 4 * g:4 * g + 4, 0:HIST],
                                                 ps[:, 7 - g, m * 4 * HIST:(m + 1) * 4 * HIST].rearrange("p (b r) -> p b r", b=4))
                last.then_inc(hs_cp, 1)
            dve.wait_ge(x_ln, 1)
            for i in range(NT + 1):
                nc.vector.tensor_scalar(dg(i), ident[:, :], rtok[:, i:i + 1], None, ALU.mult).then_inc(x_dg, 1)
            split_lo(Job(0, J_AB), cols=2 * H)
            dve.wait_ge(vec_cp, 3)
            for k in range(KT):
                dve.wait_ge(h_hi, k + 1)
                nc.vector.scalar_tensor_tensor(out=hm[1][:, k, :], in0=xT0[:, k, :], scalar=gains[:, 0, k:k + 1],
                                               in1=hm[0][:, k, :].bitcast(F32), op0=ALU.mult, op1=ALU.subtract).then_inc(h_lo, 1)
            split_lo(Job(0, 1))
            dve.wait_ge(x_rs, 3)
            dve.wait_ge(mm, J_AB + 1)
            dve.wait_ge(x_sq, NT + 1)
            nc.vector.tensor_tensor(tri3(t3[0:2 * H, :]), acc(0, 2 * H), tri3(rsb[0:2 * H, :]), ALU.mult).then_inc(pf, 1)

            for j in range(QT):
                job = Job(0, J_QKV + j)
                split_lo(job.next())
                if j == 0:
                    dve.wait_ge(ab_tr, 1)
                    nc.vector.tensor_copy(ab[:, 0:NT, :], ps[:, 7, 0:NT * 2 * H].rearrange("p (t h) -> p t h", h=2 * H))
                    nc.vector.tensor_copy(ab[0:NS, NT, :], ps[0:NS, 7, NT * 2 * H:(NT + 1) * 2 * H]).then_inc(ab_cp, 1)
                dve.wait_ge(mm, job.num(1))
                nc.vector.tensor_tensor(tri3(t1[:, :]), acc(job.slot), tri3(rsb[:, :]), ALU.mult).then_inc(pf, 1)
                dve.wait_ge(pf, job.num(1))
                nc.vector.tensor_copy(tail[:, j, 0:QH], t1[:, SEQ - QH:SEQ])
                step(nc.vector.tensor_copy(raws[:, j, :, QH:QH + DS], t1[:, SEQ:TOK].rearrange("p (b t) -> p b t", b=DB)))
                nc.vector.tensor_copy(tail[:, j, QH:].rearrange("p (b r) -> p b r", b=DB), raws[:, j, :, DS:DS + QH])
                y = (t2, t3)[j % 2]
                wait(dve, silu_done, j - 1)
                ys = y[:, SEQ:TOK].rearrange("p (b t) -> p b t", b=DB)
                nc.vector.tensor_scalar(ys, raws[:, j, :, 0:DS], wsh[:, 0, j:j + 1], None, ALU.mult)
                step(nc.vector.tensor_scalar(y[:, 0:SEQ], t1[:, 0:SEQ], wsh[:, SC - 1, j:j + 1], None, ALU.mult))
                for k in range(1, SC):
                    nc.vector.scalar_tensor_tensor(out=ys, in0=raws[:, j, :, k:k + DS], scalar=wsh[:, k, j:j + 1], in1=ys,
                                                   op0=ALU.mult, op1=ALU.add)
                    ins = nc.vector.scalar_tensor_tensor(out=y[:, k:SEQ], in0=t1[:, 0:SEQ - k], scalar=wsh[:, SC - 1 - k, j:j + 1],
                                                         in1=y[:, k:SEQ], op0=ALU.mult, op1=ALU.add)
                    if k < SC - 1:
                        step(ins)
                    else:
                        ins.then_inc(y_done, 1)
            dve.wait_ge(y_done, QT)
            dve.wait_ge(st_x, 16)
            for p in range(CT):
                jb, ja = Job(0, J_GLU + 2 * p), Job(0, J_GLU + 2 * p + 1)
                split_lo(jb.next())
                dve.wait_ge(mm, jb.num(1))
                if p:
                    dve.wait_ge(sg_done, p)
                else:
                    dve.wait_ge(silu_done, QT)
                nc.vector.tensor_tensor(tri3(t3[:, :]), acc(jb.slot), tri3(rsb[:, :]), ALU.mult).then_inc(pf, 1)
                split_lo(ja.next())
                dve.wait_ge(mm, ja.num(1))
                dve.wait_ge(sgr_done, p + 1)
                nc.vector.tensor_tensor(tri3(gl[:, p, :]), acc(ja.slot), tri3(t2[:, :]), ALU.mult).then_inc(pf, 1)
                dve.wait_ge(pf, ja.num(1))
                nc.vector.tensor_copy(gls[:, p, :, HIST:], gl[:, p, SEQ:TOK].rearrange("p (b t) -> p b t", b=DB))
            for j in range(PR):
                job = Job(0, J_Z + j)
                if j < PR - 1:
                    split_lo(job.next())
                dve.wait_ge(mm, job.num(1))
                if j >= 2:
                    dve.wait_ge(z_done, j - 1)
                nc.vector.tensor_tensor(tri3((t1, t2)[j % 2][:, :]), acc(job.slot), tri3(rsb[:, :]), ALU.mult).then_inc(pf, 1)

            dve.wait_ge(z_done, PR)
            for p in range(CT):
                if p:
                    dve.wait_ge(cv_out, p)
                step(nc.vector.tensor_scalar(t1[:, 0:SEQ], gl[:, p, 0:SEQ], wdw[:, HIST, p:p + 1], cvp[:, 0, p:p + 1], ALU.mult, ALU.add))
                for k in range(1, DWC):
                    step(nc.vector.scalar_tensor_tensor(out=t1[:, k:SEQ], in0=gl[:, p, 0:SEQ - k], scalar=wdw[:, HIST - k, p:p + 1],
                                                        in1=t1[:, k:SEQ], op0=ALU.mult, op1=ALU.add))
                for t in range(DS):
                    prd = t3[:, t * DB * DWC:(t + 1) * DB * DWC].rearrange("p (b j) -> p b j", b=DB)
                    last = nc.vector.tensor_tensor(prd, gls[:, p, :, t:t + DWC], bc(wdw[:, :, p], 1, DB), ALU.mult)
                step(last)
                smp = t1[:, SEQ:TOK].rearrange("p (b t) -> p t b", b=DB)
                step(nc.vector.tensor_reduce(smp, t3[:, 0:NS * DWC].rearrange("p (t b j) -> p t b j", t=DS, b=DB), AX, ALU.add))
                nc.vector.tensor_scalar(t1[:, SEQ:TOK], t1[:, SEQ:TOK], cvp[:, 0, p:p + 1], None, ALU.add).then_inc(cv_acc, 1)
                dve.wait_ge(cv_mm, p + 1)
                nc.vector.tensor_tensor(tri3(t1[:, :]), tri3(t1[:, :]), acc(0), ALU.subtract).then_inc(cv_c, 1)
                dve.wait_ge(cv_r, p + 1)
                nc.vector.tensor_tensor(t1[:, :], t1[:, :], t2[:, :], ALU.mult).then_inc(cv_n, 1)

            g_n = [0]

            def small(ins):
                ins.then_inc(gs_dve, 1)
                g_n[0] += 1
                dve.wait_ge(gs_dve, g_n[0])

            small(nc.vector.tensor_tensor(sm[0][:, :, :], ab[:, :, H:2 * H], bc(hp[:, 1, :], 1, NT + 1), ALU.add))
            small(nc.vector.scalar_tensor_tensor(out=sm[1][:, :, :], in0=sm[0][:, :, :], scalar=-1.0, in1=sm[0][:, :, :],
                                                 op0=ALU.mult, op1=ALU.max))
            small(nc.vector.tensor_scalar(sm[0][:, :, :], sm[0][:, :, :], 0.0, None, ALU.max))
            dve.wait_ge(gs_act, 4)
            small(nc.vector.tensor_scalar(beta[:, :, :], beta[:, :, :], 1.0, None, ALU.add))
            small(nc.vector.reciprocal(beta[:, :, :], beta[:, :, :]))
            small(nc.vector.tensor_tensor(sm[2][:, :, :], sm[2][:, :, :], sm[0][:, :, :], ALU.add))
            small(nc.vector.scalar_tensor_tensor(out=gg[:, :, :], in0=sm[2][:, :, :], scalar=-1.0, in1=bc(hp[:, 0, :], 1, NT + 1),
                                                 op0=ALU.mult, op1=ALU.mult))
            small(nc.vector.tensor_tensor(gr[:, :, :, :], bc(gg[:, 0:NT, :], 2, CPT), bc(bc(consts["blk"][:, :], 1, NT), 3, H), ALU.mult))
            small(nc.vector.tensor_tensor(grs[:, :, :], bc(gg[0:NS, NT, :], 1, DB), bc(consts["blk4"][0:NS, :], 2, H), ALU.mult))
            dve.wait_ge(gs_act, 10)

            def heads(t):
                return t.rearrange("p (h e) -> p h e", e=HD)

            def prep(t):
                n, _ = tile_tokens(t)
                ti = t % HT
                wait(dve, d_mm, t)
                tri = consts["uinc" if t < NT else "uinc4"][0:n, 0:n]
                for r in range(2):
                    last = nc.vector.tensor_tensor(ug[0:n, r * PR:(r + 1) * PR, 0:n],
                                                   bc(gg[0:n, t, :].rearrange("p (q r) -> p r q", r=2)[:, r, :], 2, n), bc(tri, 1, PR), ALU.mult)
                last.then_inc(d_ug, 1)
                dve.wait_ge(g_sq, t + 1)
                nc.vector.tensor_reduce(ss[0:n, :], sqt[0:n, :].rearrange("p (h e) -> p h e", e=HD), AX, ALU.add).then_inc(g_ss, 1)
                dve.wait_ge(d_exp, CPT * t + n // C)
                tr = consts["tri" if t < NT else "tri4"]
                nc.vector.tensor_tensor(Dm[0:n, :, :], Dm[0:n, :, :], bc(tr[0:n, :], 1, H), ALU.mult).then_inc(d_msk, 1)
                dve.wait_ge(g_r, t + 1)
                rq, rk = ss[0:n, 0:H], ss[0:n, H:2 * H]
                sc_ = [sc[0:n, k, :] for k in range(6)]
                nc.vector.tensor_tensor(sc_[0], rk, beta[0:n, t, :], ALU.mult)
                nc.vector.tensor_tensor(sc_[2], rk, ekd[0:n, t, :], ALU.mult)
                step(nc.vector.tensor_scalar(sc_[3], rq, HD ** -0.5, None, ALU.mult))
                nc.vector.tensor_tensor(sc_[1], sc_[0], egc[0:n, t, :], ALU.mult)
                step(nc.vector.tensor_tensor(sc_[4], sc_[3], egc[0:n, t, :], ALU.mult))
                dve.wait_ge(g_tok, 3 * t + 3)
                wait(dve, g_bt, 4 * t)
                for bank, out, f in ((1, tk[0], rk), (1, tk[1], sc_[0]), (0, tk[2], sc_[3]), (0, tk[3], sc_[4]),
                                     (1, Kbe[:, ti, :], sc_[1]), (1, Kd[:, ti, :], sc_[2]), (2, Vb[:, ti, :], beta[0:n, t, :])):
                    nc.vector.tensor_tensor(heads(out[0:n, :]), heads(ps[0:n, bank, :]), bc(f, 2, HD), ALU.mult).then_inc(g_big, 1)
                dve.wait_ge(d_msk, t + 1)
                dve.wait_ge(g_aq, t + 1)
                for b in range(n // C):
                    r = slice(b * C, (b + 1) * C)
                    last = nc.vector.tensor_tensor(LQ[r, ti, :, :, :], ps[r, 0:4, :].rearrange("p k (x w c) -> p (k x) w c", x=2, w=2)[:, :, :, r],
                                                   bc(Dm[r, :, :], 2, 2), ALU.mult)
                last.then_inc(g_lq, 1)

            def gate(t):
                n, t0 = tile_tokens(t)
                dve.wait_ge(o_sq, t + 1)
                nc.vector.tensor_reduce(ss[0:n, 0:H], sqt[0:n, 0:DW].rearrange("p (h e) -> p h e", e=HD), AX, ALU.add).then_inc(o_ss, 1)
                dve.wait_ge(o_r, t + 1)
                wait(dve, o_tr, t)
                if t < NT:
                    for r in range(2):
                        last = nc.vector.tensor_tensor(onr[0:n, :].rearrange("p (q r e) -> p r q e", r=2, e=HD)[:, r],
                                                       ps[0:n, 4 + r, 0:PR * HD].rearrange("p (q e) -> p q e", e=HD),
                                                       bc(ss[0:n, r * PR:(r + 1) * PR], 2, HD), ALU.mult)
                else:
                    last = nc.vector.tensor_tensor(heads(onr[0:n, :]), heads(ps[0:n, 4, :]), bc(ss[0:n, 0:H], 2, HD), ALU.mult)
                last.then_inc(o_n, 1)
                dve.wait_ge(o_tr, t + 1)
                nc.vector.scalar_tensor_tensor(out=zs[:, :, t0:t0 + n], in0=ps[:, 7, :].rearrange("p (q t) -> p q t", q=PR)[:, :, 0:n],
                                               scalar=g2, in1=zs[:, :, t0:t0 + n], op0=ALU.mult, op1=ALU.mult).then_inc(o_g, 1)

            dve.wait_ge(st_h, 16 * (4 + DB))
            nc.vector.memset(S[:, :, :], 0.0).then_inc(s_up, 1)
            for half in range(2):
                for ti in range(HT):
                    prep(half * HT + ti)
                Xm = Xp[:, :].rearrange("p (m c) -> p m c", c=C)
                Lm = Lp[:, :].rearrange("p (m c) -> p m c", c=C)
                step(nc.vector.memset(Xp[:, :], 0.0))
                step(nc.vector.memset(Xp[:, 0:C * C:C + 1], 1.0))
                dve.wait_ge(lt_ld, 16 * (half + 1))
                for c in range(1, C):
                    pr = prod[:, 0:c * c].rearrange("p (m j) -> p m j", j=c)
                    step(nc.vector.tensor_tensor(pr, Xm[:, 0:c, 0:c], bc(Lm[:, 0:c, c], 1, c), ALU.mult))
                    ins = nc.vector.tensor_reduce(Xm[:, 0:c, c], pr, AX, ALU.add, negate=True)
                    if c < C - 1:
                        step(ins)
                    else:
                        ins.then_inc(inv, 1)
                for ti in range(HT):
                    t = half * HT + ti
                    dve.wait_ge(uw_ev, 2 * t + 1)
                    for b in range(CPT):
                        n = t * CPT + b
                        r = slice(b * C, (b + 1) * C)
                        dve.wait_ge(ws_mm, n + 1)
                        for par in range(2):
                            pv = lambda x: x.rearrange("p (q r e) -> p r q e", r=2, e=HD)[:, par]
                            last = nc.vector.tensor_tensor(pv(Vn[r, :]), pv(Vb[r, ti, :]), ps[r, 2 + par, 0:PR * HD].rearrange("p (q e) -> p q e", e=HD), ALU.subtract)
                        last.then_inc(vn_d, 1)
                        dve.wait_ge(s_up, n + 1)
                        step(nc.vector.tensor_tensor(Sd[:, :, :], S[:, :, :], bc(gld[:, t, b, :], 2, HD), ALU.mult))
                        dve.wait_ge(ds_mm, n + 1)
                        nc.vector.tensor_tensor(S[:, :, :], Sd[:, :, :], ps[:, 6, 0:PR * HD].rearrange("p (q e) -> p q e", e=HD), ALU.add).then_inc(s_up, 1)
                    gate(t)
            prep(NT)
            dve.wait_ge(g_lq, NT + 1)
            nc.vector.tensor_tensor(Ns[:, :, :], LQ[0:NS, 0, :, 0, :], bc(consts["str4"][0:NS, :], 1, H), ALU.mult).then_inc(sp_dve, 1)
            dve.wait_ge(sp_mm, 2)
            nc.vector.tensor_tensor(Ms[:, :, :], ps[0:NS, 1, 0:H * C].rearrange("p (s c) -> p s c", c=C), bc(ident[0:NS, 0:C], 1, H), ALU.add).then_inc(sp_dve, 1)
            dve.wait_ge(sp_dve, 2)
            dve.wait_ge(sp_mm, 3)
            nc.vector.tensor_tensor(Ts[:, :, :], Ms[:, :, :], ps[0:NS, 2, 0:H * C].rearrange("p (s c) -> p s c", c=C), ALU.subtract).then_inc(sp_dve, 1)
            dve.wait_ge(sp_mm, 6)
            dve.wait_ge(sp_act, 2)
            nc.vector.tensor_tensor(Vn[0:NS, :], Vb[0:NS, 0, :], ps[0:NS, 3, :], ALU.subtract).then_inc(sp_dve, 1)
            dve.wait_ge(sp_dve, 4)
            nc.vector.tensor_tensor(VnM[:, :, :, :], bc(heads(Vn[0:NS, :]), 2, DB), bc(bc(consts["blk4"][0:NS, :], 1, H), 3, HD), ALU.mult).then_inc(sp_dve, 1)
            dve.wait_ge(sp_mm, 7)
            for q in range(PR):
                nc.vector.tensor_tensor(S0[:, q, :, :], S0[:, q, :, :], bc(glds[:, :, q], 2, HD), ALU.mult).then_inc(sp_dve, 1)
                dve.wait_ge(sp_dve, 6 + 2 * q)
                nc.vector.tensor_tensor(S0[:, q, :, :], S0[:, q, :, :], ps[:, q, :].rearrange("p (b e) -> p b e", e=HD), ALU.add).then_inc(sp_dve, 1)
            gate(NT)

            split_lo(Job(0, J_OUT))
            dve.wait_ge(o_g, NT + 1)
            for k in range(KT):
                dve.wait_ge(op_hi, k + 1)
                src = zs[:, k, :] if k < PR else gl[:, k - PR, :]
                nc.vector.tensor_tensor(op[1][:, k, :], src, op[0][:, k, :].bitcast(F32), ALU.subtract).then_inc(op_lo, 1)

            def low_rows(phase, m):
                dve.wait_ge(h_hi, (phase + 1) * KT + m + 1)
                nc.vector.scalar_tensor_tensor(out=hh[1][:, m, :], in0=xT[:, m, :], scalar=gains[:, phase + 1, m:m + 1],
                                               in1=hh[0][:, m, :].bitcast(F32), op0=ALU.mult, op1=ALU.subtract).then_inc(h_lo, 1)

            def add_rows(job, m):
                wait(dve, mm, job.num(1))
                nc.vector.tensor_tensor(tri3(pick(xT, m)), tri3(pick(xT, m)), acc(job.slot), ALU.add).then_inc(pf, 1)

            dve.wait_ge(ld_xT, 16)
            for m in range(KT):
                job = Job(0, J_OUT + m)
                split_lo(job.next())
                add_rows(job, m)
                low_rows(0, m)
            for q in range(FQ):
                up, down = J_MLP + 2 * KT * q, J_MLP + 2 * KT * q + KT

                def hidden(job, j, q=q):
                    n = q * KT + j
                    split_lo(job.next())
                    if q == 0 and isinstance(j, int) and j == 0:
                        dve.wait_ge(rs_done, 1)
                    wait(dve, pf, job.num(1))
                    wait(dve, u_sq, n)
                    wait(dve, u_hi, n)
                    nc.vector.tensor_tensor(t2[:, :], t1[:, :], rsb[:, :], ALU.mult).then_inc(t_done, 1)
                    wait(dve, u_sq, n + 1)
                    wait(dve, u_hi, n + 1)
                    nc.vector.tensor_tensor(pick(uu[1], j), t3[:, :], pick(uu[0], j).bitcast(F32), ALU.subtract).then_inc(u_lo, 1)
                jobs(dve, up, KT, hidden)

                def out(job, j, q=q, down=down):
                    split_lo(job.next())
                    add_rows(job, j)
                    if q == FQ - 1:
                        low_rows(1, j)
                if q < FQ - 1:
                    jobs(dve, down, KT, out)
                else:
                    for m in range(KT):
                        out(Job(0, down + m), m)
            for m in range(KT):
                jg, jp = Job(0, J_GATE + 2 * m), Job(0, J_GATE + 2 * m + 1)
                split_lo(jp, kts=PK)
                if m == 0:
                    dve.wait_ge(rs_done, 2)
                dve.wait_ge(mm, jg.num(1))
                wait(dve, gt_done, m)
                nc.vector.tensor_tensor(tri3(t1[:, :]), acc(jg.slot), tri3(rsb[:, :]), ALU.mult).then_inc(pf, 1)
                if m == 0:
                    for k in range(PK):
                        for g in range(3):
                            dve.wait_ge(p_tr, 3 * k + g + 1)
                            w = 512 if g < 2 else NS
                            nc.vector.tensor_copy(pT[:, k, g * 512:g * 512 + w], ps[:, 6 + (3 * k + g) % 2, 0:w]).then_inc(p_cp, 1)
                if m < KT - 1:
                    split_lo(jp.next())
                if m == 0:
                    for k in range(PK):
                        dve.wait_ge(p_hi, k + 1)
                        nc.vector.tensor_tensor(pp[1][:, k, :], pT[:, k, :], pp[0][:, k, :].bitcast(F32), ALU.subtract).then_inc(p_lo, 1)
                dve.wait_ge(mm, jp.num(1))
                dve.wait_ge(gt_done, m + 1)
                nc.vector.tensor_tensor(tri3(pg[:, :]), acc(jp.slot), tri3(gt[:, :]), ALU.mult).then_inc(pf, 1)
                dve.wait_ge(pf, jp.num(1))
                nc.vector.tensor_tensor(xT[:, m, :], xT[:, m, :], pg[:, :], ALU.add).then_inc(x_new, 1)
                dve.wait_ge(sq_done, 2 * KT + m + 1)
                dve.wait_ge(x_new, m + 1)
                nc.vector.tensor_scalar(xT[:, m, :], xT[:, m, :], gains[:, 3, m:m + 1], None, ALU.mult).then_inc(xg_done, 1)


def bc(ap, axis, n):
    ap = ap.unsqueeze(axis)
    shape = list(ap.shape)
    shape[axis] = n
    return ap.to_broadcast(shape)


_INS = ["x_prompt", "x_sample", "state_ssm", "state_qkv_conv", "state_conf_conv", "p_prompt", "p_sample", "g_mix", "w_in",
        "w_short", "a_log", "dt_bias", "g_o", "w_dw", "b_dw", "g_cln", "b_cln", "w_out", "g_mlp", "w_up", "w_down",
        "w_ple", "g_ple", "w_ple_gate", "g_final"]
_OUTS = [("y_p", (1, SEQ, D)), ("y_s", (DB, DS, D)), ("ssm_p", (1, 1, H, HD, HD)), ("qkv_p", (1, 1, QH, 3 * DW)),
         ("conf_p", (1, 1, HIST, CC)), ("ssm_s", (1, DB, H, HD, HD)), ("qkv_s", (1, DB, QH, 3 * DW)),
         ("conf_s", (1, DB, HIST, CC))]


def kernel(**inputs):
    import concourse.bacc as _bacc
    from concourse.bass_utils import run_bass_kernel_spmd as _run

    nc = _bacc.Bacc("TRN2", target_bir_lowering=False, num_devices=1)
    arrays, a, o = {}, {}, {}
    for name in _INS:
        arrays[f"in_{name}"] = np.ascontiguousarray(inputs[name])
    arrays["in_consts"] = shape_constants()
    for name, arr in arrays.items():
        a[name[3:]] = nc.dram_tensor(name, arr.shape, mybir.dt.from_np(arr.dtype), kind="ExternalInput").ap()
    for name, shape in _OUTS:
        o[name] = nc.dram_tensor(f"out_{name}", shape, F32, kind="ExternalOutput").ap()
    build(nc, a, o)
    r = _run(nc, [arrays], core_ids=[0])
    return tuple(r.results[0][f"out_{name}"] for name, _ in _OUTS)
```

```python
from contextlib import ExitStack

import numpy as np

import concourse.bass as bass
from concourse import mybir

F32 = mybir.dt.float32
F32R = mybir.dt.float32r
ALU = mybir.AluOpType
ACT = mybir.ActivationFunctionType
AX = mybir.AxisListType.X

P = 128
SEQ, DB, DS = 1024, 8, 4
NS = DB * DS
TOK = SEQ + NS
D = 1024
KT = D // P
NCH = 3
CW = TOK // NCH
H, HD = 8, 64
PR = H // 2
DW = H * HD
SC, DWC = 4, 31
CC = D - DW
CT = CC // P
C = 32
CPT = P // C
FF = 4 * D
FQ = FF // D
PLE = 256
PK = PLE // P
EPS = 1e-6
NT = SEQ // P
HIST, QH = DWC - 1, SC - 1
QT = 3 * DW // P
O_Z, O_B, O_GA, O_GB = 3 * DW, 4 * DW, 4 * DW + 2 * H, 4 * DW + 2 * H + CC

J_AB, J_GLU, J_Z, J_QKV, J_OUT = 0, 1, 9, 13, 25
J_MLP = J_OUT + KT
J_GATE = J_MLP + 2 * FQ * KT
J_END = J_GATE + 2 * KT

PTAPS = list(range(1, 11))
VTAPS = [0] + list(range(11, DWC))
PSTEP, VSTEP = 4, 8

CONSTS = [("ident", P), ("ones", P), ("bd64", P), ("uinc", P), ("sgt", P), ("uinc4", P), ("sgt4", P),
          ("blk", CPT), ("blk4", DB), ("tri", C), ("tri4", C), ("str4", C)]
NV = 4 * KT + 3 * CT + 1


def shape_constants():
    r, c = np.arange(P)[:, None], np.arange(P)[None, :]

    def inside(n):
        return r // n == c // n

    low = (r < NS) & (c < NS)
    parts = {
        "ident": r == c, "ones": r >= 0 * c, "bd64": inside(HD) / HD,
        "uinc": (r <= c) & inside(C), "sgt": (r > c) & inside(C),
        "uinc4": (r <= c) & inside(DS) & low, "sgt4": (r > c) & inside(DS) & low,
        "blk": r // C == c[:, :CPT], "blk4": (r // DS == c[:, :DB]) & (r < NS),
        "tri": r % C <= c[:, :C], "tri4": (r <= c[:, :C]) & (r // DS == c[:, :C] // DS),
        "str4": (r < c[:, :C]) & (r // DS == c[:, :C] // DS),
    }
    return np.concatenate([parts[n].astype(np.float32) for n, _ in CONSTS], axis=1)


class Job:

    def __init__(self, i, c):
        self.i, self.c, self.slot = i, c, c % 2

    def num(self, off=0):
        return 2 * self.i + (self.c + off) if not isinstance(self.i, int) else 2 * self.i + self.c + off

    def half(self, off=0):
        return self.i + (self.c + off) // 2

    def next(self):
        return Job(self.i, self.c + 1)


def wait(eng, sem, value):
    if isinstance(value, int) and value <= 0:
        return
    eng.wait_ge(sem, value)


def jobs(eng, first, n, body):
    for j in range(min(n, 2)):
        body(Job(0, first + j), j)
    if n > 2:
        with eng.Fori(0, (n - 2) // 2) as i:
            for u in range(2):
                body(Job(i, first + 2 + u), 2 * i + (2 + u))


class Chain:

    def __init__(self, eng, sem):
        self.eng, self.sem, self.n = eng, sem, 0

    def mark(self, ins):
        self.n += 1
        ins.then_inc(self.sem, 1)
        return self.n

    def step(self, ins):
        self.n += 1
        ins.then_inc(self.sem, 1)
        self.eng.wait_ge(self.sem, self.n)


def build(nc, a, o):
    ctx = ExitStack()
    with ctx:
        base = (nc.sbuf_base + 31) // 32 * 32
        LIM = nc.sbuf_base + nc.sbuf_bytes_remaining
        R1 = base
        WR = R1 + 67584
        TR = WR + 24576
        XR = TR + 4 * 4224
        PRS = XR + 33792 + 67584
        cur = {}

        def at(region, name, shape, dt=F32, off=None):
            if off is None:
                off = cur.get(region, 0)
            size = int(np.prod(shape[1:])) * 4
            size = (size + 31) // 32 * 32
            cur[region] = off + size
            t = nc.alloc_sbuf_tensor_at(name, shape, dt, offset=region + off)
            assert region + off + size <= LIM, name
            return t

        sem = lambda name: ctx.enter_context(nc.semaphore(name))

        ident = at(PRS, "ident", [P, P])
        ones = at(PRS, "ones", [P, P])
        vec = at(PRS, "vec", [P, NV])
        gains = vec[:, 0:4 * KT].rearrange("p (n k) -> p n k", k=KT)
        cvp = vec[:, 4 * KT:4 * KT + 3 * CT].rearrange("p (n k) -> p n k", k=CT)
        g2 = vec[:, NV - 1:NV]
        eps = at(PRS, "eps", [P, 1])
        rtok = at(PRS, "rtok", [P, 16])
        ltok = at(PRS, "ltok", [P, 16])
        grow = at(PRS, "grow", [HIST, CC])
        gsrow = at(PRS, "gsrow", [NS, CC])
        cns = at(PRS, "cns", [P, SEQ])
        sqt = at(PRS, "sqt", [P, DW], off=cur[PRS] - 4 * SEQ)
        Vn = at(PRS, "Vn", [P, DW])
        dec = cur[PRS]
        dV = at(PRS, "dV", [NS, DW], off=cur[PRS] - 4 * SEQ - 4 * CC)
        dKbe = at(PRS, "dKbe", [NS, DW], off=cur[PRS] - 2 * 4 * CC)
        cur[PRS] = dec
        dKd = at(PRS, "dKd", [NS, DW])
        LQd = at(PRS, "LQd", [NS, H, 2, C])
        WQ = at(PRS, "WQ", [P, PR, 2, NS])
        ss = at(PRS, "ss", [P, H])
        gds = at(PRS, "gds", [P, CT, NS])
        assert PRS + cur[PRS] <= LIM

        w_raw = [at(WR, f"w_raw{s}", [P, KT, P]) for s in range(2)]
        w_hi = [at(WR, f"w_hi{s}", [P, KT, P], F32R) for s in range(2)]
        w_lo = [at(WR, f"w_lo{s}", [P, KT, P], F32R) for s in range(2)]
        tmp = [at(TR, f"tmp{n}", [P, TOK]) for n in range(4)]
        rsb, t1, t2, t3 = tmp

        hm = [at(R1, f"hm_{n}", [P, KT, TOK], F32R, off=o_) for n, o_ in (("hi", 0), ("lo", 33792))]
        op = [at(R1, f"op_{n}", [P, KT, TOK], F32R, off=o_) for n, o_ in (("hi", 0), ("lo", 33792))]
        uu = [at(R1, f"u_{n}", [P, KT, TOK], F32R, off=o_) for n, o_ in (("hi", 0), ("lo", 33792))]
        pT = at(R1, "pT", [P, PK, TOK], off=0)
        pp = [at(R1, f"p_{n}", [P, PK, TOK], F32R) for n in ("hi", "lo")]
        prow = at(R1, "prow", [P, NT + 1, PLE])
        gt = at(R1, "gt", [P, TOK])
        pg = at(R1, "pg", [P, TOK])
        yrow = at(R1, "yrow", [P, NT + 1, D], off=0)
        hh = [at(XR, f"h_{n}", [P, KT, TOK], F32R, off=33792 * o_) for n, o_ in (("hi", 1), ("lo", 2))]
        xT = at(XR, "xT", [P, KT, TOK], off=0)

        xT0 = at(XR, "xT0", [P, KT, TOK], off=0)
        zs = at(XR, "zs", [P, PR, TOK], off=0)
        gl = at(XR, "gl", [P, CT, TOK])
        qkv0 = cur[XR]
        xin = at(XR, "xin", [P, NT + 1, D])
        hq = at(XR, "hq", [DB * QH, QT * P])
        hc = at(XR, "hc", [4 * HIST, 2, CC])
        assert cur[XR] <= qkv0 + QT * TOK * 4
        qkvT = at(XR, "qkvT", [P, QT, TOK], off=qkv0)
        slots = [at(XR, f"cv{n}", [P, TOK], off=qkv0 + n * TOK * 4) for n in range(QT)]
        accv, accp, prd = slots[8:12], slots[4:6], slots[6:8]
        cur[XR] = qkv0 + QT * TOK * 4
        gls = at(XR, "gls", [P, CT, DB, HIST + DS])
        raws = at(XR, "raws", [P, QT, DB, QH + DS])
        tail = at(XR, "tail", [P, QT, QH + DB * QH])
        consts = {}
        for name, w in CONSTS[2:]:
            consts[name] = at(XR, "c_" + name, [P, w])
        wsh = at(XR, "wsh", [P, SC, QT])
        wdw = at(XR, "wdw", [P, DWC, CT])
        ab = at(XR, "ab", [P, NT + 1, 2 * H])
        hp = at(XR, "hp", [P, 2, H])
        sm = [at(XR, f"sm{n}", [P, NT + 1, H]) for n in range(4)]
        beta = at(XR, "beta", [P, NT + 1, H])
        gg = at(XR, "gg", [P, NT + 1, H])
        egc = at(XR, "egc", [P, NT + 1, H])
        ekd = at(XR, "ekd", [P, NT + 1, H])
        gld = at(XR, "gld", [P, NT, CPT, PR])
        glds = at(XR, "glds", [P, DB, PR])
        assert cur[XR] <= 33792 + 67584, cur[XR]

        sqd = at(TR, "sqd", [P, D], off=3 * 4224)
        vrow = at(TR, "vrow", [NV, P], off=4224)
        srow = at(TR, "srow", [SC * QT, P])
        drow = at(TR, "drow", [DWC * CT, P])
        qrow = at(R1, "qrow", [QH + DB * QH, QT * P], off=0)

        sqk = at(R1, "sqk", [P, 2 * PR, TOK], off=8192)
        Vb = at(R1, "Vb", [P, NT, DW], off=0)
        Kbe = at(R1, "Kbe", [P, NT, DW])
        Kd = at(R1, "Kd", [P, NT, DW])
        QdT = at(R1, "QdT", [P, NT, PR, P])
        S = at(R1, "S", [P, PR, HD])
        Sd = at(R1, "Sd", [P, PR, HD])
        assert cur[R1] <= 67584
        LQ = at(TR, "LQ", [P, NT, H, 2, C], off=0)
        tk = [at(WR, f"tk{n}", [P, DW], off=2048 * n) for n in range(4)]
        KTl = at(WR, "KTl", [P, PR, P])
        RR = at(WR, "RR", [P, PR, 2, P])
        ug = at(WR, "ug", [P, H, P])
        Dm = [at(WR, f"Dm{n}", [P, H, C]) for n in range(2)]
        rn = at(WR, "rn", [P, NT + 1, 2 * H])
        scb = at(WR, "scb", [P, 5, NT + 1, H])
        gr = at(WR, "gr", [P, NT, CPT, H])
        grs = at(WR, "grs", [NS, DB, H])
        assert cur[WR] <= 24576, cur[WR]
        Lp = at(WR, "Lp", [P, 2, C * C], off=0)
        Xp = at(WR, "Xp", [P, 2, C * C])
        prod = at(WR, "prod", [P, 2, C * C])
        assert cur[WR] <= 24576, cur[WR]
        onr = at(WR, "onr", [P, DW], off=0)
        VnM = at(WR, "VnM", [NS, H, DB, HD], off=4096)
        Tbd = at(XR, "Tbd", [P, NT, H, P], off=qkv0)
        WT = at(XR, "WT", [P, 2, PR, P])
        S0 = at(XR, "S0", [P, PR, DB, HD])
        WSt = at(XR, "WSt", [P, PR, 2, NS])
        Ns = at(XR, "Ns", [NS, H, C])
        NTs = at(XR, "NTs", [NS, H, C])
        Ms = at(XR, "Ms", [NS, H, C])
        Ts = at(XR, "Ts", [NS, H, C])
        assert cur[XR] <= qkv0 + QT * TOK * 4

        ps = ctx.enter_context(nc.psum_tensor("ps", [P, 8, 512], F32))

        def acc(slot, m=P):
            return ps[0:m, 3 * slot:3 * slot + 3, 0:CW]

        def tri3(t):
            return t.rearrange("p (c n) -> p c n", c=NCH)

        xT_dram = nc.dram_tensor("xT_dram", [D, TOK], F32).ap().rearrange("(k p) t -> p k t", p=P)
        lt_dram = nc.dram_tensor("lt_dram", [2, P, C * C], F32).ap()
        tt_dram = nc.dram_tensor("tt_dram", [2, P, C * C], F32).ap()

        ld_x = [sem(f"ld_x{i}") for i in range(NT + 1)]
        ld_i = sem("ld_ident")
        ld_c = sem("ld_consts")
        init = sem("init_done")
        vec_tr = sem("vec_tr")
        vec_cp = sem("vec_cp")
        ld_h = sem("ld_h")
        x_sq = sem("x_sq")
        x_tr = sem("x_tr")
        x_cp = sem("x_cp")
        x_ln = sem("x_ln")
        x_dg = sem("x_dg")
        x_bc = sem("x_bc")
        x_rs = sem("x_rs")
        h_hi = sem("h_hi")
        h_lo = sem("h_lo")
        hs_tr = sem("hs_tr")
        hs_cp = sem("hs_cp")
        st_x = sem("st_x")
        w_dma = [sem(f"w_dma{s}") for s in range(2)]
        w_hid = sem("w_hi_done")
        w_lod = sem("w_lo_done")
        mm = sem("mm_done")
        pf = sem("psum_free")
        y_done = sem("conv_done")
        silu_done = sem("silu_done")
        raw_done = sem("raw_done")
        sg_in = sem("sg_in")
        sg_done = sem("sg_done")
        sgr_done = sem("sgr_done")
        z_in = sem("z_in")
        z_done = sem("z_done")
        dch = sem("dve_chain")
        ach = sem("act_chain")
        cv_prod = sem("cv_prod")
        cv_add = sem("cv_add")
        cv_acc = sem("cv_acc")
        cv_mm = sem("cv_mm")
        cv_c = sem("cv_centred")
        cv_sq = sem("cv_sq")
        cv_var = sem("cv_var")
        cv_r = sem("cv_r")
        cv_n = sem("cv_n")
        cv_out = sem("cv_out")
        hist_tr = sem("hist_tr")
        hist_cp = sem("hist_cp")
        st_h = sem("st_h")
        ab_tr, ab_cp = sem("ab_tr"), sem("ab_cp")
        gs_act, gs_dve, gs_mm = sem("gs_act"), sem("gs_dve"), sem("gs_mm")
        d_ug, d_mm, d_exp, d_msk = sem("d_ug"), sem("d_mm"), sem("d_exp"), sem("d_msk")
        n_sq, n_mm, n_r = sem("n_sq"), sem("n_mm"), sem("n_r")
        g_tok = sem("g_tok")
        g_big, g_bt, g_ev, g_aq, g_lq = (sem(n) for n in ("g_big", "g_bt", "g_ev", "g_aq", "g_lq"))
        tb0, lt_st, lt_ld, inv, tt_st = (sem(n) for n in ("tbd_zero", "lt_st", "lt_ld", "inv_done", "tt_st"))
        tt_ld = [sem(f"tt_ld{t}") for t in range(NT)]
        uw_mm, uw_ev = sem("uw_mm"), sem("uw_ev")
        ws_mm, vn_d, ds_mm, s_up, o_mm = (sem(n) for n in ("ws_mm", "vn_done", "ds_mm", "s_up", "o_mm"))
        o_sq, o_ss, o_r, o_n, o_tr, o_g = (sem(n) for n in ("o_sq", "o_ss", "o_r", "o_n", "o_tr", "o_gated"))
        st_s, ld_s = sem("st_s"), sem("ld_s")
        sp_mm, sp_dve, sp_act = sem("sample_mm"), sem("sample_dve"), sem("sample_act")
        op_hi, op_lo = sem("op_hi"), sem("op_lo")
        ld_xT = sem("ld_xT")
        x_new = sem("x_new")
        sq_done, ss_done = sem("sq_done"), sem("ss_done")
        st_mm, st_ln = sem("stat_mm"), sem("stat_ln")
        rs_done = sem("rs_done")
        r_done, t_done, u_hi, u_sq, u_lo = (sem(n) for n in ("relu_done", "t_done", "u_hi_done", "u_sq", "u_lo_done"))
        gt_in, gt_done, pg_done = sem("gt_in"), sem("gt_done"), sem("pg_done")
        ld_p, p_tr, p_cp, p_hi, p_lo = (sem(n) for n in ("ld_p", "p_tr", "p_cp", "p_hi_done", "p_lo_done"))
        xg_done, y_mm, y_r, y_tr, y_cp, st_y = (sem(n) for n in ("xg_done", "y_mm", "y_r", "y_tr", "y_cp", "st_y"))

        w_in, w_out = a["w_in"][0], a["w_out"][0]
        w_up, w_down = a["w_up"][0], a["w_down"][0]
        w_ple, w_gate = a["w_ple"][0], a["w_ple_gate"][0]

        def tile_tokens(i):
            return (P, i * P) if i < NT else (NS, SEQ)

        def dg(i):
            return t1[:, i * P:(i + 1) * P] if i < NT else t2[:, 0:P]

        def pick(t, m):
            return t[:, m, :] if isinstance(m, int) else t[:, bass.ds(m, 1), :].rearrange("p a t -> p (a t)")

        HT = NT // 2

        def load_inverses(eng, t, blocks):
            for b in blocks:
                src = tt_dram[t // HT].rearrange("(s t b) (m c) -> t b m s c", t=HT, b=CPT, c=C)[t % HT, b]
                eng.dma_start(Tbd[b * C:(b + 1) * C, t, :, b * C:(b + 1) * C], src).then_inc(tt_ld[t], 16)

        def exps(t):
            return 2 * CPT * t

        block = ctx.enter_context(nc.Block())

        @block.sync
        def _(sp):
            def load_w(job, src, kts=KT, cols=P):
                wait(sp, w_lod, job.num(-1))
                sp.dma_start(w_raw[job.slot][:, 0:kts, 0:cols], src.rearrange("(k p) c -> p k c", p=P))\
                  .then_inc(w_dma[job.slot], 16)

            cin = a["consts"]
            off = 0
            for name, w in CONSTS:
                dst = {"ident": ident, "ones": ones}.get(name) or consts[name]
                sp.dma_start(dst[:, :], cin[:, off:off + w]).then_inc(ld_i if off == 0 else ld_c, 16)
                off += w
                if name == "ident":
                    for i in range(2):
                        n, t0 = tile_tokens(i)
                        sp.dma_start(xin[0:n, i, :], a["x_prompt"][0, t0:t0 + n, :]).then_inc(ld_x[i], 16)
            for i in range(2, NT + 1):
                n, t0 = tile_tokens(i)
                src = a["x_prompt"][0, t0:t0 + n, :] if i < NT else a["x_sample"].rearrange("b t d -> (b t) d")
                sp.dma_start(xin[0:n, i, :], src).then_inc(ld_x[i], 16)
            load_w(Job(0, J_AB), w_in[:, O_B:O_B + 2 * H], cols=2 * H)
            load_w(Job(0, 1), w_in[:, O_GB:O_GB + P])
            sp.wait_ge(x_cp, 2 * (NT + 1))
            sp.dma_start(xT_dram, xT0[:, :, :]).then_inc(st_x, 16)
            for p in range(CT):
                if p:
                    load_w(Job(0, J_GLU + 2 * p), w_in[:, O_GB + p * P:O_GB + (p + 1) * P])
                load_w(Job(0, J_GLU + 2 * p + 1), w_in[:, O_GA + p * P:O_GA + (p + 1) * P])
            for j in range(PR):
                load_w(Job(0, J_Z + j), w_in[:, O_Z + j * P:O_Z + (j + 1) * P])
            for j in range(QT):
                load_w(Job(0, J_QKV + j), w_in[:, j * P:(j + 1) * P])
                if j == 0:
                    sp.dma_start(o["conf_s"][0, :, 0:HIST - DS, :], a["state_conf_conv"][0, :, DS:HIST, :]).then_inc(st_h, 16)
                    sp.wait_ge(hist_cp, 1)
                    sp.dma_start(o["conf_p"][0, 0], grow[0:HIST, :]).then_inc(st_h, 16)
                    sp.wait_ge(hist_cp, 2)
                    for b in range(DB):
                        sp.dma_start(o["conf_s"][0, b, HIST - DS:HIST, :], gsrow[b * DS:(b + 1) * DS, :]).then_inc(st_h, 16)
            sp.wait_ge(hist_cp, 5)
            sp.dma_start(o["qkv_p"][0, 0], qrow[0:QH, :]).then_inc(st_h, 16)
            sp.dma_start(o["qkv_s"][0].rearrange("b r c -> (b r) c"), qrow[QH:QH + DB * QH, :]).then_inc(st_h, 16)
            for t in range(NT):
                sp.wait_ge(g_lq, t + 1)
                dst = lt_dram[t // HT].rearrange("(s t b) (m c) -> t (b m) s c", t=HT, b=CPT, c=C)[t % HT]
                sp.dma_start(dst, LQ[:, t, :, 0, :]).then_inc(lt_st, 16)
            sp.wait_ge(g_lq, NT + 1)
            sp.wait_ge(lt_st, 16 * NT)
            for half in range(2):
                sp.dma_start(Lp[:, half, :], lt_dram[half]).then_inc(lt_ld, 16)
            for par in range(2):
                for q in range(PR):
                    sp.dma_start(S0[par * HD:(par + 1) * HD, q, :, :],
                                 a["state_ssm"][0, :, 2 * q + par].rearrange("b d e -> d b e")).then_inc(ld_s, 16)
            sp.wait_ge(inv, 1)
            for half in range(2):
                sp.dma_start(tt_dram[half], Xp[:, half, :]).then_inc(tt_st, 16)
            sp.wait_ge(tt_st, 32)
            sp.wait_ge(tb0, 1)
            for t in range(NT):
                load_inverses(sp, t, range(CPT // 2))
            sp.wait_ge(s_up, NT * CPT + 1)
            for par in range(2):
                sp.dma_start(o["ssm_p"][0, 0].rearrange("(q r) d e -> r d q e", r=2)[par],
                             S[par * HD:(par + 1) * HD, :, :]).then_inc(st_s, 16)
            sp.wait_ge(sp_dve, 13)
            for par in range(2):
                for q in range(PR):
                    sp.dma_start(o["ssm_s"][0, :, 2 * q + par].rearrange("b d e -> d b e"),
                                 S0[par * HD:(par + 1) * HD, q, :, :]).then_inc(st_s, 16)
            sp.wait_ge(o_g, NT + 1)
            for j in range(2):
                load_w(Job(0, J_OUT + j), w_out[:, j * P:(j + 1) * P])
            sp.wait_ge(op_lo, KT)
            sp.wait_ge(st_x, 16)
            sp.dma_start(xT[:, :, :], xT_dram).then_inc(ld_xT, 16)
            with sp.Fori(0, (KT - 2) // 2) as i:
                for u in range(2):
                    load_w(Job(i, J_OUT + 2 + u), w_out[:, bass.ds((2 * i + 2 + u) * P, P)])
            for q in range(FQ):
                up, down = J_MLP + 2 * KT * q, J_MLP + 2 * KT * q + KT
                with sp.Fori(0, KT // 2) as i:
                    for u in range(2):
                        load_w(Job(i, up + u), w_up[:, bass.ds((2 * i + u + q * KT) * P, P)])
                with sp.Fori(0, KT // 2) as i:
                    for u in range(2):
                        load_w(Job(i, down + u), w_down[q * D:(q + 1) * D, bass.ds((2 * i + u) * P, P)])
            for i in range(NT + 1):
                n, t0 = tile_tokens(i)
                src = a["p_prompt"][0, 0, t0:t0 + n, :] if i < NT else a["p_sample"][0].rearrange("b t d -> (b t) d")
                if i == 0:
                    sp.wait_ge(mm, J_GATE)
                sp.dma_start(prow[0:n, i, :], src).then_inc(ld_p, 16)
            for m in range(KT):
                load_w(Job(0, J_GATE + 2 * m), w_gate[:, m * P:(m + 1) * P])
                load_w(Job(0, J_GATE + 2 * m + 1), w_ple[:, m * P:(m + 1) * P], kts=PK)
            for i in range(NT + 1):
                n, t0 = tile_tokens(i)
                sp.wait_ge(y_cp, i + 1)
                dst = o["y_p"][0, t0:t0 + n, :] if i < NT else o["y_s"].rearrange("b t d -> (b t) d")
                sp.dma_start(dst, yrow[0:n, i, :]).then_inc(st_y, 16)
            sp.wait_ge(st_y, 16 * (NT + 1))
            sp.wait_ge(st_s, 16 * (2 + 2 * PR))
            sp.wait_ge(st_h, 16 * (2 + DB + 2))
            sp.wait_ge(st_x, 16)

        @block.gpsimd
        def _(pool):
            def taps(s):
                for n in range(PSTEP * s, PSTEP * (s + 1)):
                    p, k = divmod(n, len(PTAPS))
                    if p < CT:
                        pool.wait_ge(cv_prod, n + 1)
                        if k:
                            pool.wait_ge(cv_add, n)
                            s0 = PTAPS[k]
                            nc.gpsimd.tensor_tensor(accp[p % 2][:, s0:SEQ], accp[p % 2][:, s0:SEQ], prd[n % 2][:, s0:SEQ], ALU.add)\
                              .then_inc(cv_add, 1)
                        else:
                            pool.wait_ge(cv_add, n)
                            nc.gpsimd.memset(accp[p % 2][:, 0:1], 0.0).then_inc(cv_add, 1)

            for p in range(CT):
                if p:
                    taps(2 * p - 2)
                pool.wait_ge(sg_done, p + 1)
                if p:
                    pool.wait_ge(pf, J_GLU + 2 * p)
                nc.gpsimd.tensor_tensor(t2[:, :], t1[:, :], rsb[:, :], ALU.mult).then_inc(sgr_done, 1)
                if p:
                    taps(2 * p - 1)
            for s in range(2 * CT - 2, len(PTAPS) * CT // PSTEP):
                taps(s)

            pool.wait_ge(g_tok, NT + 1)
            nc.gpsimd.memset(Tbd[:, :, :, :], 0.0).then_inc(tb0, 1)

            def sum_squares(phase):
                for m in range(1, KT):
                    pool.wait_ge(sq_done, phase * KT + m + 1)
                    if m > 1:
                        pool.wait_ge(ss_done, phase * (KT - 1) + m - 1)
                    nc.gpsimd.tensor_tensor(t3[:, :], t3[:, :], t2[:, :], ALU.add).then_inc(ss_done, 1)

            sum_squares(0)
            for q in range(FQ):
                def hidden(job, j, q=q):
                    n = q * KT + j
                    wait(pool, t_done, n + 1)
                    if q or not isinstance(j, int) or j:
                        wait(pool, u_lo, n)
                    nc.gpsimd.tensor_tensor(t3[:, :], t2[:, :], t2[:, :], ALU.mult).then_inc(u_sq, 1)
                jobs(pool, J_MLP + 2 * KT * q, KT, hidden)
            sum_squares(1)
            sum_squares(2)

        @block.scalar
        def _(act):
            ac = Chain(act, ach)

            def split_hi(job, kts=KT, cols=P):
                wait(act, w_dma[job.slot], 16 * job.half() + 16)
                wait(act, mm, job.num(-1))
                nc.scalar.activation(w_hi[job.slot][:, 0:kts, 0:cols], w_raw[job.slot][:, 0:kts, 0:cols],
                                     ACT.Copy).then_inc(w_hid, 1)

            for n, (name, k) in enumerate((("g_mix", KT), ("g_mlp", KT), ("g_ple", KT), ("g_final", KT),
                                           ("b_dw", CT), ("g_cln", CT), ("b_cln", CT))):
                src = a[name] if name == "g_final" else a[name][0]
                r0 = n * KT if n < 4 else 4 * KT + (n - 4) * CT
                act.dma_start(vrow[r0:r0 + k, :], src.rearrange("(k p) -> k p", p=P)).then_inc(ld_h, 16)
            for par in range(2):
                act.dma_start(vrow[NV - 1:NV, par * HD:(par + 1) * HD], a["g_o"]).then_inc(ld_h, 16)
            act.dma_start(srow[:, :], a["w_short"][0].rearrange("j (m p) -> (j m) p", p=P)).then_inc(ld_h, 16)
            act.dma_start(drow[:, :], a["w_dw"][0].rearrange("j (m p) -> (j m) p", p=P)).then_inc(ld_h, 16)
            act.dma_start(hq[:, :], a["state_qkv_conv"][0].rearrange("b r c -> (b r) c")).then_inc(ld_h, 16)
            for g in range(2):
                act.dma_start(hc[:, g, :], a["state_conf_conv"][0, 4 * g:4 * g + 4].rearrange("b r c -> (b r) c")).then_inc(ld_h, 16)
            act.dma_start(hp[:, 0, :], a["a_log"].to_broadcast([P, H])).then_inc(ld_h, 16)
            act.dma_start(hp[:, 1, :], a["dt_bias"].to_broadcast([P, H])).then_inc(ld_h, 16)
            act.wait_ge(init, 3)
            for i in range(NT + 1):
                n, t0 = tile_tokens(i)
                act.wait_ge(ld_x[i], 16)
                if i:
                    act.wait_ge(x_sq, i)
                nc.scalar.activation(sqd[0:n, :], xin[0:n, i, :], ACT.Square, accum_out=rtok[0:n, i:i + 1]).then_inc(x_sq, 1)
                for g in range(2):
                    act.wait_ge(x_tr, 2 * i + g + 1)
                    nc.scalar.activation(xT0[:, 4 * g:4 * g + 4, t0:t0 + n],
                                         ps[:, (2 * i + g) % 6, :].rearrange("p (k t) -> p k t", k=4)[:, :, 0:n],
                                         ACT.Copy).then_inc(x_cp, 1)
            act.wait_ge(x_sq, NT + 1)
            ac.step(nc.scalar.activation(ltok[:, 0:NT + 1], rtok[:, 0:NT + 1], ACT.Ln, bias=eps[:, :], scale=1.0 / D))
            nc.scalar.activation(rtok[:, 0:NT + 1], ltok[:, 0:NT + 1], ACT.Exp, scale=-0.5).then_inc(x_ln, 1)
            split_hi(Job(0, J_AB), cols=2 * H)
            act.wait_ge(x_cp, 2 * (NT + 1))
            act.wait_ge(vec_cp, 3)
            for k in range(KT):
                nc.scalar.activation(hm[0][:, k, :], xT0[:, k, :], ACT.Copy, scale=gains[:, 0, k:k + 1]).then_inc(h_hi, 1)
            for g in range(3):
                act.wait_ge(x_bc, g + 1)
                w = 4 * P if g < 2 else NS
                nc.scalar.activation(rsb[:, g * 512:g * 512 + w], ps[:, 3 + g, 0:w], ACT.Copy).then_inc(x_rs, 1)
            split_hi(Job(0, 1))

            def taps(s):
                for n in range(PSTEP * s, PSTEP * (s + 1)):
                    p, k = divmod(n, len(PTAPS))
                    if p < CT:
                        s0 = PTAPS[k]
                        act.wait_ge(pf, J_GLU + 2 * p + 2)
                        if k == 0 and p >= 2:
                            act.wait_ge(cv_acc, p - 1)
                        if n > 2:
                            act.wait_ge(cv_add, n - 1)
                        dst = prd[n % 2] if k else accp[p % 2]
                        nc.scalar.activation(dst[:, s0:SEQ], gl[:, p, 0:SEQ - s0], ACT.Copy,
                                             scale=wdw[:, HIST - s0, p:p + 1]).then_inc(cv_prod, 1)

            for p in range(CT):
                split_hi(Job(0, J_GLU + 2 * p + 1))
                if p:
                    taps(2 * p - 2)
                act.wait_ge(pf, J_GLU + 2 * p + 1)
                if p:
                    act.wait_ge(sgr_done, p)
                nc.scalar.activation(t1[:, :], t3[:, :], ACT.Sigmoid).then_inc(sg_done, 1)
                split_hi(Job(0, J_GLU + 2 * p + 2))
                if p:
                    taps(2 * p - 1)
            act.wait_ge(st_x, 16)
            for j in range(PR):
                split_hi(Job(0, J_Z + j + 1))
                taps(2 * CT - 2 + j)
                if j == 1:
                    act.wait_ge(hist_tr, 1)
                    nc.scalar.activation(grow[0:HIST, :], ps[0:HIST, 6, :], ACT.Copy).then_inc(hist_cp, 1)
                    act.wait_ge(hist_tr, 2)
                    nc.scalar.activation(gsrow[0:NS, :], ps[0:NS, 7, :], ACT.Copy).then_inc(hist_cp, 1)
                act.wait_ge(pf, J_Z + j + 1)
                nc.scalar.activation(zs[:, j, :], (t1, t2)[j % 2][:, :], ACT.Silu).then_inc(z_done, 1)

            def channel_norm(n):
                p, var = divmod(n, 2)
                v = accv[p][:, 0:SEQ] if p < CT else gds[:, :, :].rearrange("p m t -> p (m t)")
                w = SEQ if p < CT else CT * NS
                if not var:
                    act.wait_ge(cv_c, p + 1)
                    nc.scalar.activation(cns[:, 0:w], v, ACT.Square).then_inc(cv_sq, 1)
                    return
                act.wait_ge(cv_var, p + 1)
                src = ps[:, 6:8, :] if p < CT else ps[:, 6, 0:w]
                dst = cns[:, :].rearrange("p (a b) -> p a b", a=2) if p < CT else cns[:, 0:w]
                ac.step(nc.scalar.activation(dst, src, ACT.Ln, bias=eps[:, :]))
                nc.scalar.activation(cns[:, 0:w], cns[:, 0:w], ACT.Exp, scale=-0.5).then_inc(cv_r, 1)
                act.wait_ge(cv_n, p + 1)
                for m in range(CT) if p == CT else [p]:
                    nc.scalar.activation(gl[:, m, SEQ:TOK] if p == CT else gl[:, m, 0:SEQ], gds[:, m, :] if p == CT else v,
                                         ACT.Silu, bias=cvp[:, 2, m:m + 1], scale=cvp[:, 1, m:m + 1]).then_inc(cv_out, 1)

            for j in range(QT):
                if j < QT - 1:
                    split_hi(Job(0, J_QKV + j + 1))
                if 2 <= j < 2 * CT + 4:
                    channel_norm(j - 2)
                act.wait_ge(y_done, j + 1)
                nc.scalar.activation(qkvT[:, j, :], (t2, t3)[j % 2][:, :], ACT.Silu).then_inc(silu_done, 1)
            for g in range(3):
                act.wait_ge(hist_tr, 3 + g)
                nc.scalar.activation(qrow[:, g * 512:(g + 1) * 512], ps[0:QH + DB * QH, g, :], ACT.Copy).then_inc(hist_cp, 1)

            a_n = [0]

            def small(out, in_, f, **kw):
                nc.scalar.activation(out, in_, f, **kw).then_inc(gs_act, 1)
                a_n[0] += 1
                act.wait_ge(gs_act, a_n[0])

            act.wait_ge(ab_cp, 1)
            small(beta[:, :, :], ab[:, :, 0:H], ACT.Exp, scale=-1.0)
            act.wait_ge(gs_dve, 3)
            small(sm[1][:, :, :], sm[1][:, :, :], ACT.Exp, scale=-1.0)
            small(sm[2][:, :, :], sm[1][:, :, :], ACT.Ln, bias=1.0)
            small(hp[:, 0, :], hp[:, 0, :], ACT.Exp)
            act.wait_ge(gs_mm, 1)
            nc.scalar.activation(egc[:, :, :], ps[:, 0, 0:(NT + 1) * H].rearrange("p (t h) -> p t h", h=H), ACT.Exp).then_inc(gs_act, 1)
            nc.scalar.activation(ekd[:, :, :], ps[:, 1, 0:(NT + 1) * H].rearrange("p (t h) -> p t h", h=H), ACT.Exp).then_inc(gs_act, 1)
            for par in range(2):
                rows = slice(par * HD, (par + 1) * HD)
                nc.scalar.activation(gld[rows, :, :, :].rearrange("p t b q -> p (t b) q"),
                                     ps[rows, 2, 0:NT * CPT * H].rearrange("p (t q r) -> p t q r", q=PR, r=2)[:, :, :, par],
                                     ACT.Exp).then_inc(gs_act, 1)
                nc.scalar.activation(glds[rows, :, :], ps[rows, 3, 0:DB * H].rearrange("p (t q r) -> p t q r", q=PR, r=2)[:, :, :, par],
                                     ACT.Exp).then_inc(gs_act, 1)

            act.wait_ge(mm, J_OUT)
            for j in range(0, 2 * PR, 2):
                nc.scalar.activation(sqk[:, j, :], qkvT[:, j, :], ACT.Square).then_inc(n_sq, 1)
            act.wait_ge(n_mm, 1)
            nc.scalar.activation(rn[0:NS, NT, :], ps[0:NS, 4, NT * 2 * H:(NT + 1) * 2 * H], ACT.Ln, bias=eps[0:NS, :], scale=float(HD))
            ac.step(nc.scalar.activation(rn[:, 0:NT, :], ps[:, 4, 0:NT * 2 * H].rearrange("p (t h) -> p t h", h=2 * H), ACT.Ln,
                                         bias=eps[:, :], scale=float(HD)))
            nc.scalar.activation(rn[:, :, :], rn[:, :, :], ACT.Exp, scale=-0.5).then_inc(n_r, 1)

            def decays(t, g):
                n, _ = tile_tokens(t)
                act.wait_ge(d_mm, 2 * t + g + 1)
                wait(act, g_lq, t - 1)
                for b in range(n // C):
                    r = slice(b * C, (b + 1) * C)
                    nc.scalar.activation(Dm[t % 2][r, 4 * g:4 * g + 4, :], ps[r, 7, :].rearrange("p (s c) -> p s c", c=P)[:, :, r],
                                         ACT.Exp).then_inc(d_exp, 1)

            def back(t):
                n, _ = tile_tokens(t)
                wait(act, g_aq, t)
                outs = (KTl[:, :, 0:n], RR[:, :, 0, 0:n], RR[:, :, 1, 0:n], QdT[:, t, :, 0:n] if t < NT else WQ[:, :, 1, :])
                for k in range(4):
                    act.wait_ge(g_bt, 4 * t + k + 1)
                    nc.scalar.activation(outs[k], ps[:, 3 + k, :].rearrange("p (q t) -> p q t", q=PR)[:, :, 0:n],
                                         ACT.Copy).then_inc(g_ev, 1)

            def o_banks(t):
                return ps[:, 4 - 4 * (t % 2):6 - 4 * (t % 2), 0:PR * HD] if t < NT else ps[0:NS, 4:5, 0:2 * PR * HD]

            def gate_square(t):
                n, _ = tile_tokens(t)
                act.wait_ge(o_mm, t + 1)
                nc.scalar.activation(sqt[0:n, 0:DW].rearrange("p (a b) -> p a b", a=1 if t == NT else 2), o_banks(t), ACT.Square).then_inc(o_sq, 1)

            def gate_rms(t):
                n, _ = tile_tokens(t)
                act.wait_ge(o_ss, t + 1)
                ac.step(nc.scalar.activation(ss[0:n, 0:H], ss[0:n, 0:H], ACT.Ln, bias=eps[0:n, :], scale=1.0 / HD))
                nc.scalar.activation(ss[0:n, 0:H], ss[0:n, 0:H], ACT.Exp, scale=-0.5).then_inc(o_r, 1)

            def inverse_times(t, w):
                act.wait_ge(uw_mm, 2 * t + w + 1)
                if w == 0:
                    nc.scalar.activation(Vb[:, t, :], ps[:, 7, :], ACT.Copy).then_inc(uw_ev, 1)
                else:
                    nc.scalar.activation(WT[:, t % 2, :, :], ps[:, 7, :].rearrange("p (q t) -> p q t", q=PR), ACT.Copy).then_inc(uw_ev, 1)

            act.wait_ge(st_h, 16 * (4 + DB))
            decays(0, 0)
            decays(0, 1)
            for t in range(NT + 1):
                back(t)
                if t < NT:
                    decays(t + 1, 0)
                    decays(t + 1, 1)
            act.wait_ge(sp_mm, 1)
            nc.scalar.activation(NTs[:, :, :], ps[0:NS, 0, 0:H * C].rearrange("p (s c) -> p s c", c=C), ACT.Copy).then_inc(sp_act, 1)
            act.wait_ge(sp_mm, 4)
            nc.scalar.activation(dV[:, :], ps[0:NS, 0, :], ACT.Copy).then_inc(sp_act, 1)
            nc.scalar.activation(WQ[:, :, 0, :], ps[:, 1, :].rearrange("p (q t) -> p q t", q=PR)[:, :, 0:NS], ACT.Copy).then_inc(sp_act, 1)
            act.wait_ge(sp_mm, 5)
            nc.scalar.activation(WSt[:, :, :, :], ps[:, 2, 0:PR * 2 * NS].rearrange("p (q w t) -> p q w t", q=PR, w=2), ACT.Copy).then_inc(sp_act, 1)
            act.wait_ge(tt_st, 32)
            act.wait_ge(tb0, 1)
            for t in range(NT):
                load_inverses(act, t, range(CPT // 2, CPT))
            for w in range(2):
                inverse_times(0, w)
            for t in range(NT):
                if t:
                    gate_square(t - 1)
                if t < NT - 1:
                    inverse_times(t + 1, 0)
                if t:
                    gate_rms(t - 1)
                if t < NT - 1:
                    inverse_times(t + 1, 1)
            for t in (NT - 1, NT):
                gate_square(t)
                gate_rms(t)

            act.wait_ge(o_g, NT + 1)
            split_hi(Job(0, J_OUT))
            act.wait_ge(st_s, 16 * (2 + 2 * PR))
            for k in range(KT):
                src = zs[:, k, :] if k < PR else gl[:, k - PR, 0:TOK]
                nc.scalar.activation(op[0][:, k, :], src, ACT.Copy).then_inc(op_hi, 1)

            def norm_tail(phase, m, final, value):
                act.wait_ge(final, value)
                if m == 0 and phase == 1:
                    act.wait_ge(u_lo, FQ * KT)
                if m == 1 and phase == 1:
                    act.wait_ge(u_sq, FQ * KT)
                if m > 1:
                    act.wait_ge(ss_done, phase * (KT - 1) + m - 1)
                nc.scalar.activation((t2 if m else t3)[:, :], xT[:, m, :], ACT.Square).then_inc(sq_done, 1)
                if phase < 2:
                    nc.scalar.activation(hh[0][:, m, :], xT[:, m, :], ACT.Copy, scale=gains[:, phase + 1, m:m + 1]).then_inc(h_hi, 1)

            def stats(n):
                for c in range(NCH):
                    act.wait_ge(st_mm, 3 * n + c + 1)
                    nc.scalar.activation(rsb[:, c * CW:(c + 1) * CW], ps[:, 6 + c % 2, 0:CW], ACT.Ln, bias=eps[:, :],
                                         scale=1.0 / D).then_inc(st_ln, 1)
                act.wait_ge(st_ln, 3 * n + 3)
                nc.scalar.activation(rsb[:, :], rsb[:, :], ACT.Exp, scale=-0.5).then_inc(rs_done, 1)

            for m in range(KT):
                split_hi(Job(0, J_OUT + m + 1))
                norm_tail(0, m, pf, J_OUT + m + 1)
            for q in range(FQ):
                up, down = J_MLP + 2 * KT * q, J_MLP + 2 * KT * q + KT

                def hidden(job, j, q=q):
                    n = q * KT + j
                    split_hi(job.next())
                    if q == 0 and isinstance(j, int) and j == 0:
                        stats(0)
                    wait(act, mm, job.num(1))
                    if isinstance(j, int) and j == 0:
                        wait(act, pf, job.num())
                    wait(act, t_done, n)
                    nc.scalar.activation(tri3(t1[:, :]), acc(job.slot), ACT.Relu).then_inc(pf, 1)
                    wait(act, t_done, n + 1)
                    nc.scalar.activation(pick(uu[0], j), t2[:, :], ACT.Square).then_inc(u_hi, 1)
                jobs(act, up, KT, hidden)
                if q < FQ - 1:
                    jobs(act, down, KT, lambda job, j: split_hi(job.next()))
                else:
                    for m in range(KT):
                        split_hi(Job(0, down + m + 1))
                        norm_tail(1, m, pf, down + m + 1)
            for m in range(KT):
                split_hi(Job(0, J_GATE + 2 * m + 1), kts=PK)
                if m == 0:
                    stats(1)
                act.wait_ge(pf, J_GATE + 2 * m + 1)
                wait(act, x_new, m)
                nc.scalar.activation(gt[:, :], t1[:, :], ACT.Sigmoid).then_inc(gt_done, 1)
                if m < KT - 1:
                    split_hi(Job(0, J_GATE + 2 * m + 2))
                if m == 0:
                    act.wait_ge(p_cp, 6)
                    for k in range(PK):
                        nc.scalar.activation(pp[0][:, k, :], pT[:, k, :], ACT.Copy).then_inc(p_hi, 1)
                norm_tail(2, m, x_new, m + 1)
            act.wait_ge(y_mm, 1)
            nc.scalar.activation(ltok[0:NS, NT:NT + 1], ps[0:NS, 6, NT:NT + 1], ACT.Ln, bias=eps[0:NS, :], scale=1.0 / D)
            ac.step(nc.scalar.activation(ltok[:, 0:NT], ps[:, 6, 0:NT], ACT.Ln, bias=eps[:, :], scale=1.0 / D))
            ac.step(nc.scalar.activation(rtok[:, 0:NT + 1], ltok[:, 0:NT + 1], ACT.Exp, scale=-0.5))
            for i in range(NT + 1):
                n, _ = tile_tokens(i)
                act.wait_ge(y_tr, i + 1)
                nc.scalar.activation(yrow[0:n, i, :].rearrange("p (a b) -> p a b", a=2), ps[0:n, 2 * (i % 3):2 * (i % 3) + 2, :],
                                     ACT.Copy, scale=rtok[0:n, i:i + 1]).then_inc(y_cp, 1)

        @block.tensor
        def _(pe):
            def multiply(job, rhs, kts=KT, m=P, before=None):
                wait(pe, w_lod, job.num(1))
                wait(pe, pf, job.num(-1))
                hi, lo = w_hi[job.slot], w_lo[job.slot]
                for k in range(kts):
                    if before:
                        before(k)
                    for n, (w, x) in enumerate(((hi, rhs[0]), (hi, rhs[1]), (lo, rhs[0]))):
                        for c in range(NCH):
                            last = nc.tensor.matmul(ps[0:m, 3 * job.slot + c, 0:CW], w[:, k, 0:m],
                                                    x[:, k, c * CW:(c + 1) * CW], start=(k == 0 and n == 0),
                                                    stop=(k == kts - 1 and n == 2))
                last.then_inc(mm, 1)

            pe.wait_ge(ld_i, 16)
            for i in range(NT + 1):
                n, _ = tile_tokens(i)
                pe.wait_ge(ld_x[i], 16)
                for g in range(2):
                    if 2 * i + g >= 6:
                        pe.wait_ge(x_cp, 2 * i + g - 5)
                    for k in range(4):
                        last = nc.tensor.transpose(ps[:, (2 * i + g) % 6, k * P:k * P + n],
                                                   xin[0:n, i, (4 * g + k) * P:(4 * g + k + 1) * P], ident[0:n, 0:n])
                    last.then_inc(x_tr, 1)
            pe.wait_ge(ld_h, 16 * 16)
            for rows, n, col in ((vrow, NV, 0), (srow, SC * QT, 64), (drow, DWC * CT, 128)):
                last = nc.tensor.transpose(ps[:, 7, col:col + n], rows[:, :], ident[0:n, 0:n])
            last.then_inc(vec_tr, 1)
            nq = DB * QH
            for m in range(QT):
                last = nc.tensor.transpose(ps[:, 6, m * nq:(m + 1) * nq], hq[:, m * P:(m + 1) * P], ident[0:nq, 0:nq])
            last.then_inc(hs_tr, 1)
            nh = 4 * HIST
            for g in range(2):
                if g:
                    pe.wait_ge(hs_cp, 1)
                else:
                    pe.wait_ge(vec_cp, 3)
                for m in range(CT):
                    last = nc.tensor.transpose(ps[:, 7 - g, m * nh:(m + 1) * nh], hc[:, g, m * P:(m + 1) * P], ident[0:nh, 0:nh])
                last.then_inc(hs_tr, 1)
            pe.wait_ge(x_cp, 2 * (NT + 1))
            pe.wait_ge(ld_c, 16 * (len(CONSTS) - 1))
            for i in range(NT + 1):
                n, _ = tile_tokens(i)
                pe.wait_ge(x_dg, i + 1)
                bank, col = 3 + i // 4, (i % 4) * P
                last = nc.tensor.matmul(ps[:, bank, col:col + n], ones[0:n, :], dg(i)[0:n, 0:n], start=True, stop=True)
                if i in (3, 7, 8):
                    last.then_inc(x_bc, 1)

            def mixer_rows(k):
                pe.wait_ge(h_lo, k + 1)

            multiply(Job(0, J_AB), hm, m=2 * H, before=mixer_rows)
            pe.wait_ge(x_rs, 3)
            for j in range(2 * CT):
                multiply(Job(0, J_GLU + j), hm)
                if j == 0:
                    pe.wait_ge(pf, J_AB + 1)
                    for i in range(NT + 1):
                        n, t0 = tile_tokens(i)
                        last = nc.tensor.transpose(ps[0:n, 7, i * 2 * H:(i + 1) * 2 * H], t3[0:2 * H, t0:t0 + n], ident[0:2 * H, 0:2 * H])
                    last.then_inc(ab_tr, 1)
            for j in range(PR):
                multiply(Job(0, J_Z + j), hm)
                if j == 0:
                    pe.wait_ge(pf, J_Z)
                    pe.wait_ge(ab_cp, 1)
                    for m in range(CT):
                        last = nc.tensor.transpose(ps[0:HIST, 6, m * P:(m + 1) * P], gl[:, m, SEQ - HIST:SEQ], ident[:, :])
                    last.then_inc(hist_tr, 1)
                    for m in range(CT):
                        last = nc.tensor.transpose(ps[0:NS, 7, m * P:(m + 1) * P], gl[:, m, SEQ:TOK], ident[:, :])
                    last.then_inc(hist_tr, 1)

            def channel_norm(n):
                p, var = divmod(n, 2)
                if var:
                    pe.wait_ge(cv_sq, p + 1)
                elif p:
                    pe.wait_ge(cv_r, p)
                    pe.wait_ge(cv_acc, CT) if p == CT else pe.wait_ge(cv_acc, p + 1)
                else:
                    pe.wait_ge(hist_cp, 2)
                    pe.wait_ge(cv_acc, 1)
                if p == CT:
                    src = cns[:, 0:CT * NS] if var else gds[:, :, :].rearrange("p m t -> p (m t)")
                    last = nc.tensor.matmul(ps[:, 6, 0:CT * NS], consts["bd64"][:, :], src, start=True, stop=True)
                else:
                    for c in range(2):
                        last = nc.tensor.matmul(ps[:, 6 + c, :], consts["bd64"][:, :], (cns if var else accv[p])[:, c * 512:(c + 1) * 512],
                                                start=True, stop=True)
                last.then_inc(cv_var if var else cv_mm, 1)

            for j in range(QT):
                multiply(Job(0, J_QKV + j), hm)
                if 1 <= j < 2 * CT + 3:
                    channel_norm(j - 1)
            pe.wait_ge(y_done, QT)
            for g in range(3):
                for k in range(4):
                    last = nc.tensor.transpose(ps[0:QH + DB * QH, g, k * P:(k + 1) * P], tail[:, 4 * g + k, :], ident[:, :])
                last.then_inc(hist_tr, 1)

            pe.wait_ge(hist_cp, 5)
            pe.wait_ge(cv_r, CT + 1)
            pe.wait_ge(gs_dve, 9)
            nt = NT * H
            gf = gg[:, :, :].rearrange("p t h -> p (t h)")
            nc.tensor.matmul(ps[:, 0, 0:nt], consts["uinc"][:, :], gf[:, 0:nt], start=True, stop=True)
            nc.tensor.matmul(ps[:, 0, nt:nt + H], consts["uinc4"][:, :], gf[:, nt:nt + H], start=True, stop=True)
            nc.tensor.matmul(ps[:, 1, 0:nt], consts["sgt"][:, :], gf[:, 0:nt], start=True, stop=True)
            nc.tensor.matmul(ps[:, 1, nt:nt + H], consts["sgt4"][:, :], gf[:, nt:nt + H], start=True, stop=True)
            nc.tensor.matmul(ps[:, 2, 0:NT * CPT * H], ones[:, :], gr[:, :, :, :].rearrange("p t b h -> p (t b h)"), start=True, stop=True)
            nc.tensor.matmul(ps[:, 3, 0:DB * H], ones[0:NS, :], grs[:, :, :].rearrange("p b h -> p (b h)"), start=True, stop=True)\
              .then_inc(gs_mm, 1)
            pe.wait_ge(gs_act, 10)

            for j in range(2 * PR):
                pe.wait_ge(n_sq, 2 * PR)
                for t in range(NT + 1):
                    n, t0 = tile_tokens(t)
                    last = nc.tensor.matmul(ps[0:n, 4, t * 2 * H + 2 * j:t * 2 * H + 2 * j + 2], sqk[:, j, t0:t0 + n],
                                            consts["bd64"][:, 0:P:HD], start=True, stop=True)
            last.then_inc(n_mm, 1)

            def decays(t, g):
                n, _ = tile_tokens(t)
                pe.wait_ge(d_ug, t + 1)
                wait(pe, d_exp, exps(t) + g * (n // C))
                nc.tensor.matmul(ps[0:n, 7, :].rearrange("p (s c) -> p s c", c=P)[:, :, 0:n],
                                 consts["sgt" if t < NT else "sgt4"][0:n, 0:n], ug[0:n, 4 * g:4 * g + 4, 0:n],
                                 start=True, stop=True).then_inc(d_mm, 1)

            def tokens(t):
                n, t0 = tile_tokens(t)
                wait(pe, g_big, 7 * t)
                for g in range(3):
                    for k in range(4):
                        last = nc.tensor.transpose(ps[0:n, g, k * P:(k + 1) * P], qkvT[:, 4 * g + k, t0:t0 + n], ident[:, :])
                last.then_inc(g_tok, 1)

            def back(t):
                n, _ = tile_tokens(t)
                wait(pe, g_lq, t)
                for k in range(4):
                    pe.wait_ge(g_big, 7 * t + k + 1)
                    for q in range(PR):
                        last = nc.tensor.transpose(ps[:, 3 + k, q * P:q * P + n], tk[k][0:n, q * P:(q + 1) * P], ident[0:n, 0:n])
                    last.then_inc(g_bt, 1)

            def pairs(t):
                n, _ = tile_tokens(t)
                pe.wait_ge(g_ev, 4 * t + 4)
                for s in range(H):
                    par, q = divmod(s, PR)
                    rows = slice(par * HD, (par + 1) * HD)
                    last = nc.tensor.matmul(ps[0:n, 3 + s // 2, (s % 2) * 256:(s % 2) * 256 + 256].rearrange("p (w c) -> p w c", w=2)[:, :, 0:n],
                                            KTl[rows, q, 0:n], RR[rows, q, :, 0:n], start=True, stop=True)
                last.then_inc(g_aq, 1)

            def transpose_out(t):
                n, _ = tile_tokens(t)
                pe.wait_ge(o_n, t + 1)
                for q in range(PR):
                    last = nc.tensor.transpose(ps[:, 7, q * P:q * P + n], onr[0:n, q * P:(q + 1) * P], ident[0:n, 0:n])
                last.then_inc(o_tr, 1)

            def inverse_times(t, w):
                if w:
                    pe.wait_ge(uw_ev, 2 * t + 1)
                else:
                    pe.wait_ge(tt_ld[t], 16 * CPT)
                    wait(pe, o_g, t - 2)
                for h in range(H):
                    q, par = h // 2, h % 2
                    T = Tbd[:, t, par * PR + q, :]
                    if w == 0:
                        last = nc.tensor.matmul(ps[:, 7, h * HD:(h + 1) * HD], T, Vb[:, t, h * HD:(h + 1) * HD], start=True, stop=True)
                    else:
                        last = nc.tensor.matmul(ps[par * HD:(par + 1) * HD, 7, q * P:(q + 1) * P], Kbe[:, t, h * HD:(h + 1) * HD], T,
                                                start=True, stop=True)
                last.then_inc(uw_mm, 1)

            def chunk(t, b):
                n, ob = t * CPT + b, 4 - 4 * (t % 2)
                r = slice(b * C, (b + 1) * C)
                if b == 0:
                    pe.wait_ge(uw_ev, 2 * t + 2)
                pe.wait_ge(s_up, n + 1)
                for w, src in ((2, WT[:, t % 2, :, :]), (ob, QdT[:, t, :, :])):
                    if w != 2 and b == 0 and t >= 2:
                        pe.wait_ge(o_n, t - 1)
                    for h in range(H):
                        par, q = h % 2, h // 2
                        rows = slice(par * HD, (par + 1) * HD)
                        last = nc.tensor.matmul(ps[r, w + par, q * HD:(q + 1) * HD], src[rows, q, r], S[rows, q, :],
                                                start=(w == 2 or q == 0), stop=(w == 2), skip_group_check=True)
                    if w == 2:
                        last.then_inc(ws_mm, 1)
                pe.wait_ge(vn_d, n + 1)
                for h in range(H):
                    par, q = h % 2, h // 2
                    last = nc.tensor.matmul(ps[par * HD:(par + 1) * HD, 6, q * HD:(q + 1) * HD], Kd[r, t, h * HD:(h + 1) * HD],
                                            Vn[r, h * HD:(h + 1) * HD], start=True, stop=True, skip_group_check=True)
                last.then_inc(ds_mm, 1)
                for h in range(H):
                    s, par, q = (h % 2) * PR + h // 2, h % 2, h // 2
                    last = nc.tensor.matmul(ps[r, ob + par, q * HD:(q + 1) * HD], LQ[r, t, s, 1, :], Vn[r, h * HD:(h + 1) * HD],
                                            start=False, stop=True, skip_group_check=True)
                if b == CPT - 1:
                    last.then_inc(o_mm, 1)

            decays(0, 0)
            tokens(0)
            decays(0, 1)
            for t in range(NT + 1):
                back(t)
                if t < NT:
                    tokens(t + 1)
                    decays(t + 1, 0)
                pairs(t)
                if t < NT:
                    decays(t + 1, 1)

            pe.wait_ge(sp_dve, 1)
            for s in range(H):
                last = nc.tensor.transpose(ps[0:NS, 0, s * C:(s + 1) * C], Ns[:, s, :], ident[0:NS, 0:NS])
            last.then_inc(sp_mm, 1)
            pe.wait_ge(sp_act, 1)
            for s in range(H):
                last = nc.tensor.matmul(ps[0:NS, 1, s * C:(s + 1) * C], NTs[:, s, :], Ns[:, s, :], start=True, stop=True)
            last.then_inc(sp_mm, 1)
            pe.wait_ge(sp_dve, 2)
            for s in range(H):
                last = nc.tensor.matmul(ps[0:NS, 2, s * C:(s + 1) * C], NTs[:, s, :], Ms[:, s, :], start=True, stop=True)
            last.then_inc(sp_mm, 1)
            pe.wait_ge(sp_dve, 3)
            for h in range(H):
                s = (h % 2) * PR + h // 2
                nc.tensor.matmul(ps[0:NS, 0, h * HD:(h + 1) * HD], Ts[:, s, :], dV[:, h * HD:(h + 1) * HD], start=True, stop=True)
            for h in range(H):
                s, par, q = (h % 2) * PR + h // 2, h % 2, h // 2
                last = nc.tensor.matmul(ps[par * HD:(par + 1) * HD, 1, q * P:q * P + NS], dKbe[:, h * HD:(h + 1) * HD],
                                        Ts[:, s, :], start=True, stop=True)
            last.then_inc(sp_mm, 1)
            pe.wait_ge(sp_act, 3)
            pe.wait_ge(ld_s, 16 * 2 * PR)
            for par in range(2):
                rows = slice(par * HD, (par + 1) * HD)
                for q in range(PR):
                    for b in range(DB):
                        cols = slice(b * DS, (b + 1) * DS)
                        last = nc.tensor.matmul(ps[rows, 2, q * 2 * NS:(q + 1) * 2 * NS].rearrange("p (w t) -> p w t", w=2)[:, :, cols],
                                                S0[rows, q, b, :], WQ[rows, q, :, cols], start=True, stop=True)
            last.then_inc(sp_mm, 1)
            pe.wait_ge(sp_act, 4)
            for q in range(PR):
                last = nc.tensor.transpose(ps[0:NS, 3, q * P:(q + 1) * P], WSt[:, q, 0, :], ident[:, :])
            last.then_inc(sp_mm, 1)

            for w in range(2):
                inverse_times(0, w)
            for t in range(NT):
                for b in range(CPT):
                    chunk(t, b)
                    if b < 2 and t < NT - 1:
                        inverse_times(t + 1, b)
                    if b == 2 and t:
                        if t < NT - 1:
                            pe.wait_ge(uw_ev, 2 * t + 4)
                        transpose_out(t - 1)
            transpose_out(NT - 1)

            pe.wait_ge(o_g, NT)
            for q in range(PR):
                nc.tensor.matmul(ps[0:NS, 4, q * P:(q + 1) * P], WSt[:, q, 1, :], ident[:, :], start=(q == 0), stop=False, skip_group_check=True)
            for h in range(H):
                s = (h % 2) * PR + h // 2
                last = nc.tensor.matmul(ps[0:NS, 4, h * HD:(h + 1) * HD], LQd[:, s, 1, :], dV[:, h * HD:(h + 1) * HD],
                                        start=False, stop=True, skip_group_check=True)
            last.then_inc(o_mm, 1)
            pe.wait_ge(sp_dve, 5)
            for h in range(H):
                par, q = h % 2, h // 2
                last = nc.tensor.matmul(ps[par * HD:(par + 1) * HD, q, :], dKd[:, h * HD:(h + 1) * HD],
                                        VnM[:, h, :, :].rearrange("p b e -> p (b e)"), start=True, stop=True)
            last.then_inc(sp_mm, 1)
            transpose_out(NT)

            pe.wait_ge(o_g, NT + 1)
            pe.wait_ge(sp_dve, 13)
            for m in range(KT):
                multiply(Job(0, J_OUT + m), op, before=(lambda k: pe.wait_ge(op_lo, k + 1)) if m == 0 else None)

            def stat(n):
                pe.wait_ge(ss_done, (n + 1) * (KT - 1))
                for c in range(NCH):
                    if c == 2:
                        pe.wait_ge(st_ln, 3 * n + 1)
                    nc.tensor.matmul(ps[:, 6 + c % 2, 0:CW], ones[:, :], t3[:, c * CW:(c + 1) * CW], start=True, stop=True).then_inc(st_mm, 1)

            for q in range(FQ):
                up, down = J_MLP + 2 * KT * q, J_MLP + 2 * KT * q + KT

                def hidden(job, j, q=q):
                    first = q == 0 and isinstance(j, int) and j == 0
                    multiply(job, hh, before=(lambda k: pe.wait_ge(h_lo, KT + k + 1)) if first else None)
                    if first:
                        stat(0)
                jobs(pe, up, KT, hidden)

                def out(job, j, q=q):
                    first = isinstance(j, int) and j == 0
                    multiply(job, uu, before=(lambda k: pe.wait_ge(u_lo, q * KT + k + 1)) if first else None)
                jobs(pe, down, KT, out)

            multiply(Job(0, J_GATE), hh, before=lambda k: pe.wait_ge(h_lo, 2 * KT + k + 1))
            stat(1)
            pe.wait_ge(ld_p, 16 * (NT + 1))
            n_done = 0
            for k in range(PK):
                for g in range(3):
                    if n_done >= 2:
                        pe.wait_ge(p_cp, n_done - 1)
                    else:
                        pe.wait_ge(st_ln, 6)
                    for i in (range(4 * g, 4 * g + 4) if g < 2 else [NT]):
                        n, t0 = tile_tokens(i)
                        last = nc.tensor.transpose(ps[:, 6 + n_done % 2, (i % 4) * P:(i % 4) * P + n], prow[0:n, i, k * P:(k + 1) * P], ident[0:n, 0:n])
                    last.then_inc(p_tr, 1)
                    n_done += 1
            for m in range(KT):
                if m:
                    multiply(Job(0, J_GATE + 2 * m), hh)
                multiply(Job(0, J_GATE + 2 * m + 1), pp, kts=PK, before=(lambda k: pe.wait_ge(p_lo, k + 1)) if m == 0 else None)
            pe.wait_ge(ss_done, 3 * (KT - 1))
            for i in range(NT + 1):
                n, t0 = tile_tokens(i)
                last = nc.tensor.matmul(ps[0:n, 6, i:i + 1], t3[:, t0:t0 + n], ones[:, 0:1], start=True, stop=True)
            last.then_inc(y_mm, 1)
            pe.wait_ge(pf, J_END)
            pe.wait_ge(xg_done, KT)
            for i in range(NT + 1):
                n, t0 = tile_tokens(i)
                if i >= 3:
                    pe.wait_ge(y_cp, i - 2)
                for m in range(KT):
                    last = nc.tensor.transpose(ps[0:n, 2 * (i % 3) + m // 4, (m % 4) * P:(m % 4 + 1) * P], xT[:, m, t0:t0 + n], ident[:, :])
                last.then_inc(y_tr, 1)

        @block.vector
        def _(dve):
            dc = Chain(dve, dch)
            step = dc.step

            def split_lo(job, kts=KT, cols=P):
                wait(dve, w_hid, job.num(1))
                nc.vector.tensor_tensor(w_lo[job.slot][:, 0:kts, 0:cols], w_raw[job.slot][:, 0:kts, 0:cols],
                                        w_hi[job.slot][:, 0:kts, 0:cols].bitcast(F32), ALU.subtract).then_inc(w_lod, 1)

            nc.vector.memset(rtok[:, :], 1.0).then_inc(init, 1)
            nc.vector.memset(eps[:, :], EPS).then_inc(init, 1)
            nc.vector.memset(ab[:, :, :], 0.0).then_inc(init, 1)
            dve.wait_ge(vec_tr, 1)
            nc.vector.tensor_copy(vec[:, :], ps[:, 7, 0:NV]).then_inc(vec_cp, 1)
            nc.vector.tensor_copy(wsh[:, :, :].rearrange("p j m -> p (j m)"), ps[:, 7, 64:64 + SC * QT]).then_inc(vec_cp, 1)
            nc.vector.tensor_copy(wdw[:, :, :].rearrange("p j m -> p (j m)"), ps[:, 7, 128:128 + DWC * CT]).then_inc(vec_cp, 1)
            dve.wait_ge(hs_tr, 1)
            nc.vector.tensor_copy(raws[:, :, :, 0:QH], ps[:, 6, 0:QT * DB * QH].rearrange("p (m b r) -> p m b r", m=QT, b=DB)).then_inc(hs_cp, 1)
            for g in range(2):
                dve.wait_ge(hs_tr, 2 + g)
                for m in range(CT):
                    last = nc.vector.tensor_copy(gls[:, m, 4 * g:4 * g + 4, 0:HIST],
                                                 ps[:, 7 - g, m * 4 * HIST:(m + 1) * 4 * HIST].rearrange("p (b r) -> p b r", b=4))
                last.then_inc(hs_cp, 1)
            dve.wait_ge(x_ln, 1)
            for i in range(NT + 1):
                nc.vector.tensor_scalar(dg(i), ident[:, :], rtok[:, i:i + 1], None, ALU.mult).then_inc(x_dg, 1)
            split_lo(Job(0, J_AB), cols=2 * H)
            dve.wait_ge(vec_cp, 3)
            for k in range(KT):
                dve.wait_ge(h_hi, k + 1)
                nc.vector.scalar_tensor_tensor(out=hm[1][:, k, :], in0=xT0[:, k, :], scalar=gains[:, 0, k:k + 1],
                                               in1=hm[0][:, k, :].bitcast(F32), op0=ALU.mult, op1=ALU.subtract).then_inc(h_lo, 1)
            split_lo(Job(0, 1))
            dve.wait_ge(x_rs, 3)
            dve.wait_ge(mm, J_AB + 1)
            dve.wait_ge(x_sq, NT + 1)
            nc.vector.tensor_tensor(tri3(t3[0:2 * H, :]), acc(0, 2 * H), tri3(rsb[0:2 * H, :]), ALU.mult).then_inc(pf, 1)

            mark = [0, 0]

            def taps(n0, n1):
                for n in range(n0, min(n1, CT * len(VTAPS))):
                    p, k = divmod(n, len(VTAPS))
                    s0 = VTAPS[k]
                    for u in range(2):
                        lo, hi = max(s0, u * SEQ // 2), (u + 1) * SEQ // 2
                        dst = accv[p][:, lo:hi]
                        w = wdw[:, HIST - s0, p:p + 1]
                        if k:
                            dve.wait_ge(dch, mark[u])
                            ins = nc.vector.scalar_tensor_tensor(out=dst, in0=gl[:, p, lo - s0:hi - s0], scalar=w, in1=dst, op0=ALU.mult, op1=ALU.add)
                        else:
                            ins = nc.vector.tensor_scalar(dst, gl[:, p, lo:hi], w, cvp[:, 0, p:p + 1], ALU.mult, ALU.add)
                        mark[u] = dc.mark(ins)
                    if k == len(VTAPS) - 1 and p < CT - 1:
                        finish(p)

            def finish(p):
                dve.wait_ge(dch, mark[1])
                dve.wait_ge(cv_add, len(PTAPS) * (p + 1))
                nc.vector.tensor_tensor(accv[p][:, 0:SEQ], accv[p][:, 0:SEQ], accp[p % 2][:, 0:SEQ], ALU.add).then_inc(cv_acc, 1)

            def decode_taps(p):
                for t in range(DS):
                    pr = t3[:, t * DB * DWC:(t + 1) * DB * DWC].rearrange("p (b j) -> p b j", b=DB)
                    last = nc.vector.tensor_tensor(pr, gls[:, p, :, t:t + DWC], bc(wdw[:, :, p], 1, DB), ALU.mult)
                step(last)
                step(nc.vector.tensor_reduce(gds[:, p, :].rearrange("p (b t) -> p t b", b=DB),
                                             t3[:, 0:NS * DWC].rearrange("p (t b j) -> p t b j", t=DS, b=DB), AX, ALU.add))
                step(nc.vector.tensor_scalar(gds[:, p, :], gds[:, p, :], cvp[:, 0, p:p + 1], None, ALU.add))

            def channel_norm(n):
                p, var = divmod(n, 2)
                if p < CT:
                    v = accv[p][:, 0:SEQ]
                    split, src, r = v.rearrange("p (a b) -> p a b", a=2), ps[:, 6:8, :], cns[:, :]
                else:
                    v = gds[:, :, :].rearrange("p m t -> p (m t)")
                    split, src, r = v, ps[:, 6, 0:CT * NS], cns[:, 0:CT * NS]
                if var:
                    dve.wait_ge(cv_r, p + 1)
                    nc.vector.tensor_tensor(v, v, r, ALU.mult).then_inc(cv_n, 1)
                else:
                    dve.wait_ge(cv_mm, p + 1)
                    nc.vector.tensor_tensor(split, split, src, ALU.subtract).then_inc(cv_c, 1)

            dve.wait_ge(st_x, 16)
            for p in range(CT):
                jb, ja = Job(0, J_GLU + 2 * p), Job(0, J_GLU + 2 * p + 1)
                split_lo(jb.next())
                if p == 0:
                    dve.wait_ge(ab_tr, 1)
                    nc.vector.tensor_copy(ab[:, 0:NT, :], ps[:, 7, 0:NT * 2 * H].rearrange("p (t h) -> p t h", h=2 * H))
                    nc.vector.tensor_copy(ab[0:NS, NT, :], ps[0:NS, 7, NT * 2 * H:(NT + 1) * 2 * H]).then_inc(ab_cp, 1)
                else:
                    taps(VSTEP * (2 * p - 2), VSTEP * (2 * p - 1))
                dve.wait_ge(mm, jb.num(1))
                if p:
                    dve.wait_ge(sg_done, p)
                nc.vector.tensor_tensor(tri3(t3[:, :]), acc(jb.slot), tri3(rsb[:, :]), ALU.mult).then_inc(pf, 1)
                split_lo(ja.next())
                if p:
                    taps(VSTEP * (2 * p - 1), VSTEP * 2 * p)
                dve.wait_ge(mm, ja.num(1))
                dve.wait_ge(sgr_done, p + 1)
                nc.vector.tensor_tensor(tri3(gl[:, p, :]), acc(ja.slot), tri3(t2[:, :]), ALU.mult).then_inc(pf, 1)
                dve.wait_ge(pf, ja.num(1))
                nc.vector.tensor_copy(gls[:, p, :, HIST:], gl[:, p, SEQ:TOK].rearrange("p (b t) -> p b t", b=DB))
            nslot = 2 * CT - 2
            dve.wait_ge(sg_done, CT)
            for j in range(PR):
                job = Job(0, J_Z + j)
                split_lo(job.next())
                decode_taps(j)
                taps(VSTEP * nslot, VSTEP * (nslot + 1))
                nslot += 1
                dve.wait_ge(mm, job.num(1))
                if j >= 2:
                    dve.wait_ge(z_done, j - 1)
                nc.vector.tensor_tensor(tri3((t1, t2)[j % 2][:, :]), acc(job.slot), tri3(rsb[:, :]), ALU.mult).then_inc(pf, 1)

            for j in range(QT):
                job = Job(0, J_QKV + j)
                if j < QT - 1:
                    split_lo(job.next())
                if j == 0:
                    taps(VSTEP * nslot, CT * len(VTAPS))
                if j == 1:
                    finish(CT - 1)
                if 2 <= j < 2 * CT + 4:
                    channel_norm(j - 2)
                dve.wait_ge(mm, job.num(1))
                nc.vector.tensor_tensor(tri3(t1[:, :]), acc(job.slot), tri3(rsb[:, :]), ALU.mult).then_inc(pf, 1)
                dve.wait_ge(pf, job.num(1))
                nc.vector.tensor_copy(tail[:, j, 0:QH], t1[:, SEQ - QH:SEQ])
                step(nc.vector.tensor_copy(raws[:, j, :, QH:QH + DS], t1[:, SEQ:TOK].rearrange("p (b t) -> p b t", b=DB)))
                nc.vector.tensor_copy(tail[:, j, QH:].rearrange("p (b r) -> p b r", b=DB), raws[:, j, :, DS:DS + QH])
                y = (t2, t3)[j % 2]
                wait(dve, silu_done, j - 1)
                if j < 2:
                    dve.wait_ge(z_done, PR)
                ys = y[:, SEQ:TOK].rearrange("p (b t) -> p b t", b=DB)
                nc.vector.tensor_scalar(ys, raws[:, j, :, 0:DS], wsh[:, 0, j:j + 1], None, ALU.mult)
                step(nc.vector.tensor_scalar(y[:, 0:SEQ], t1[:, 0:SEQ], wsh[:, SC - 1, j:j + 1], None, ALU.mult))
                for k in range(1, SC):
                    nc.vector.scalar_tensor_tensor(out=ys, in0=raws[:, j, :, k:k + DS], scalar=wsh[:, k, j:j + 1], in1=ys,
                                                   op0=ALU.mult, op1=ALU.add)
                    ins = nc.vector.scalar_tensor_tensor(out=y[:, k:SEQ], in0=t1[:, 0:SEQ - k], scalar=wsh[:, SC - 1 - k, j:j + 1],
                                                         in1=y[:, k:SEQ], op0=ALU.mult, op1=ALU.add)
                    if k < SC - 1:
                        step(ins)
                    else:
                        ins.then_inc(y_done, 1)

            dve.wait_ge(mm, J_OUT)
            dve.wait_ge(silu_done, QT)
            for j in range(1, 2 * PR, 2):
                nc.vector.tensor_tensor(sqk[:, j, :], qkvT[:, j, :], qkvT[:, j, :], ALU.mult).then_inc(n_sq, 1)
            step(nc.vector.memset(rn[:, :, :], 1.0))
            g_n = [0]

            def small(ins):
                ins.then_inc(gs_dve, 1)
                g_n[0] += 1
                dve.wait_ge(gs_dve, g_n[0])

            small(nc.vector.tensor_tensor(sm[0][:, :, :], ab[:, :, H:2 * H], bc(hp[:, 1, :], 1, NT + 1), ALU.add))
            small(nc.vector.scalar_tensor_tensor(out=sm[1][:, :, :], in0=sm[0][:, :, :], scalar=-1.0, in1=sm[0][:, :, :],
                                                 op0=ALU.mult, op1=ALU.max))
            small(nc.vector.tensor_scalar(sm[0][:, :, :], sm[0][:, :, :], 0.0, None, ALU.max))
            dve.wait_ge(gs_act, 4)
            small(nc.vector.tensor_scalar(beta[:, :, :], beta[:, :, :], 1.0, None, ALU.add))
            small(nc.vector.reciprocal(beta[:, :, :], beta[:, :, :]))
            small(nc.vector.tensor_tensor(sm[2][:, :, :], sm[2][:, :, :], sm[0][:, :, :], ALU.add))
            small(nc.vector.scalar_tensor_tensor(out=gg[:, :, :], in0=sm[2][:, :, :], scalar=-1.0, in1=bc(hp[:, 0, :], 1, NT + 1),
                                                 op0=ALU.mult, op1=ALU.mult))
            small(nc.vector.tensor_tensor(gr[:, :, :, :], bc(gg[:, 0:NT, :], 2, CPT), bc(bc(consts["blk"][:, :], 1, NT), 3, H), ALU.mult))
            small(nc.vector.tensor_tensor(grs[:, :, :], bc(gg[0:NS, NT, :], 1, DB), bc(consts["blk4"][0:NS, :], 2, H), ALU.mult))
            dve.wait_ge(gs_act, 10)

            def heads(t):
                return t.rearrange("p (h e) -> p h e", e=HD)

            def logits(t):
                n, _ = tile_tokens(t)
                wait(dve, d_mm, 2 * t)
                tri = consts["uinc" if t < NT else "uinc4"][0:n, 0:n]
                for r in range(2):
                    last = nc.vector.tensor_tensor(ug[0:n, r * PR:(r + 1) * PR, 0:n],
                                                   bc(gg[0:n, t, :].rearrange("p (q r) -> p r q", r=2)[:, r, :], 2, n), bc(tri, 1, PR), ALU.mult)
                last.then_inc(d_ug, 1)

            def scaled(t):
                n, _ = tile_tokens(t)
                dve.wait_ge(g_tok, t + 1)
                wait(dve, g_bt, 4 * t)
                outs = (Kbe[:, t, :], Kd[:, t, :], Vb[:, t, :]) if t < NT else (dKbe, dKd, dV)
                for bank, out, f in ((1, tk[0], rn[0:n, t, H:2 * H]), (1, tk[1], scb[0:n, 0, t, :]), (0, tk[2], scb[0:n, 3, t, :]),
                                     (0, tk[3], scb[0:n, 4, t, :]), (1, outs[0], scb[0:n, 1, t, :]), (1, outs[1], scb[0:n, 2, t, :]),
                                     (2, outs[2], beta[0:n, t, :])):
                    nc.vector.tensor_tensor(heads(out[0:n, :]), heads(ps[0:n, bank, :]), bc(f, 2, HD), ALU.mult).then_inc(g_big, 1)

            def decayed(t):
                n, _ = tile_tokens(t)
                D_ = Dm[t % 2]
                dve.wait_ge(d_exp, exps(t) + 2 * (n // C))
                tr = consts["tri" if t < NT else "tri4"]
                nc.vector.tensor_tensor(D_[0:n, :, :], D_[0:n, :, :], bc(tr[0:n, :], 1, H), ALU.mult).then_inc(d_msk, 1)
                dve.wait_ge(d_msk, t + 1)
                dve.wait_ge(g_aq, t + 1)
                for b in range(n // C):
                    r = slice(b * C, (b + 1) * C)
                    last = nc.vector.tensor_tensor(LQ[r, t, :, :, :] if t < NT else LQd[:, :, :, :],
                                                   ps[r, 3:7, :].rearrange("p k (x w c) -> p (k x) w c", x=2, w=2)[:, :, :, r],
                                                   bc(D_[r, :, :], 2, 2), ALU.mult)
                last.then_inc(g_lq, 1)

            def gate_sum(t):
                n, _ = tile_tokens(t)
                dve.wait_ge(o_sq, t + 1)
                nc.vector.tensor_reduce(ss[0:n, 0:H], sqt[0:n, 0:DW].rearrange("p (h e) -> p h e", e=HD), AX, ALU.add).then_inc(o_ss, 1)

            def gate_norm(t):
                n, _ = tile_tokens(t)
                dve.wait_ge(o_r, t + 1)
                wait(dve, o_tr, t)
                if t < NT:
                    for r in range(2):
                        last = nc.vector.tensor_tensor(onr[0:n, :].rearrange("p (q r e) -> p r q e", r=2, e=HD)[:, r],
                                                       ps[0:n, 4 - 4 * (t % 2) + r, 0:PR * HD].rearrange("p (q e) -> p q e", e=HD),
                                                       bc(ss[0:n, r * PR:(r + 1) * PR], 2, HD), ALU.mult)
                else:
                    last = nc.vector.tensor_tensor(heads(onr[0:n, :]), heads(ps[0:n, 4, :]), bc(ss[0:n, 0:H], 2, HD), ALU.mult)
                last.then_inc(o_n, 1)

            def gate_out(t):
                n, t0 = tile_tokens(t)
                dve.wait_ge(o_tr, t + 1)
                nc.vector.scalar_tensor_tensor(out=zs[:, :, t0:t0 + n], in0=ps[:, 7, :].rearrange("p (q t) -> p q t", q=PR)[:, :, 0:n],
                                               scalar=g2, in1=zs[:, :, t0:t0 + n], op0=ALU.mult, op1=ALU.mult).then_inc(o_g, 1)

            dve.wait_ge(st_h, 16 * (4 + DB))
            logits(0)
            dve.wait_ge(n_r, 1)
            rq, rk = rn[:, :, 0:H], rn[:, :, H:2 * H]
            nc.vector.tensor_tensor(scb[:, 0, :, :], rk, beta[:, :, :], ALU.mult)
            nc.vector.tensor_tensor(scb[:, 2, :, :], rk, ekd[:, :, :], ALU.mult)
            step(nc.vector.tensor_scalar(scb[:, 3, :, :], rq, HD ** -0.5, None, ALU.mult))
            nc.vector.tensor_tensor(scb[:, 1, :, :], scb[:, 0, :, :], egc[:, :, :], ALU.mult)
            step(nc.vector.tensor_tensor(scb[:, 4, :, :], scb[:, 3, :, :], egc[:, :, :], ALU.mult))
            nc.vector.memset(S[:, :, :], 0.0).then_inc(s_up, 1)
            scaled(0)
            for t in range(NT + 1):
                if t < NT:
                    logits(t + 1)
                    scaled(t + 1)
                decayed(t)

            def decode_step(n):
                if n == 0:
                    dve.wait_ge(g_lq, NT + 1)
                    nc.vector.tensor_tensor(Ns[:, :, :], LQd[:, :, 0, :], bc(consts["str4"][0:NS, :], 1, H), ALU.mult).then_inc(sp_dve, 1)
                elif n == 1:
                    dve.wait_ge(sp_mm, 2)
                    nc.vector.tensor_tensor(Ms[:, :, :], ps[0:NS, 1, 0:H * C].rearrange("p (s c) -> p s c", c=C),
                                            bc(ident[0:NS, 0:C], 1, H), ALU.add).then_inc(sp_dve, 1)
                elif n == 2:
                    dve.wait_ge(sp_dve, 2)
                    dve.wait_ge(sp_mm, 3)
                    nc.vector.tensor_tensor(Ts[:, :, :], Ms[:, :, :], ps[0:NS, 2, 0:H * C].rearrange("p (s c) -> p s c", c=C), ALU.subtract).then_inc(sp_dve, 1)
                else:
                    dve.wait_ge(sp_mm, 6)
                    dve.wait_ge(sp_act, 2)
                    nc.vector.tensor_tensor(dV[:, :], dV[:, :], ps[0:NS, 3, :], ALU.subtract).then_inc(sp_dve, 1)

            decode_step(0)
            Xm = Xp[:, :, :].rearrange("p g (m c) -> p g m c", c=C)
            Lm = Lp[:, :, :].rearrange("p g (m c) -> p g m c", c=C)
            step(nc.vector.memset(Xp[:, :, :], 0.0))
            step(nc.vector.memset(Xp[:, :, 0:C * C:C + 1], 1.0))
            dve.wait_ge(lt_ld, 32)
            for c in range(1, C):
                pr = prod[:, :, 0:c * c].rearrange("p g (m j) -> p g m j", j=c)
                step(nc.vector.tensor_tensor(pr, Xm[:, :, 0:c, 0:c], bc(Lm[:, :, 0:c, c], 2, c), ALU.mult))
                ins = nc.vector.tensor_reduce(Xm[:, :, 0:c, c], pr, AX, ALU.add, negate=True)
                if c < C - 1:
                    step(ins)
                else:
                    ins.then_inc(inv, 1)
                if c in (10, 14, 24):
                    decode_step({10: 1, 14: 2, 24: 3}[c])
            for t in range(NT):
                dve.wait_ge(uw_ev, 2 * t + 1)
                for b in range(CPT):
                    if t and b:
                        (gate_sum, gate_norm, gate_out)[b - 1](t - 1)
                    n = t * CPT + b
                    r = slice(b * C, (b + 1) * C)
                    dve.wait_ge(ws_mm, n + 1)
                    for par in range(2):
                        pv = lambda x: x.rearrange("p (q r e) -> p r q e", r=2, e=HD)[:, par]
                        last = nc.vector.tensor_tensor(pv(Vn[r, :]), pv(Vb[r, t, :]), ps[r, 2 + par, 0:PR * HD].rearrange("p (q e) -> p q e", e=HD), ALU.subtract)
                    last.then_inc(vn_d, 1)
                    dve.wait_ge(s_up, n + 1)
                    step(nc.vector.tensor_tensor(Sd[:, :, :], S[:, :, :], bc(gld[:, t, b, :], 2, HD), ALU.mult))
                    dve.wait_ge(ds_mm, n + 1)
                    nc.vector.tensor_tensor(S[:, :, :], Sd[:, :, :], ps[:, 6, 0:PR * HD].rearrange("p (q e) -> p q e", e=HD), ALU.add).then_inc(s_up, 1)
            gate_sum(NT - 1)
            gate_norm(NT - 1)
            gate_out(NT - 1)
            dve.wait_ge(sp_dve, 4)
            nc.vector.tensor_tensor(VnM[:, :, :, :], bc(heads(dV[:, :]), 2, DB), bc(bc(consts["blk4"][0:NS, :], 1, H), 3, HD), ALU.mult).then_inc(sp_dve, 1)
            dve.wait_ge(sp_mm, 7)
            for q in range(PR):
                nc.vector.tensor_tensor(S0[:, q, :, :], S0[:, q, :, :], bc(glds[:, :, q], 2, HD), ALU.mult).then_inc(sp_dve, 1)
                dve.wait_ge(sp_dve, 6 + 2 * q)
                nc.vector.tensor_tensor(S0[:, q, :, :], S0[:, q, :, :], ps[:, q, :].rearrange("p (b e) -> p b e", e=HD), ALU.add).then_inc(sp_dve, 1)
            gate_sum(NT)
            gate_norm(NT)
            gate_out(NT)

            split_lo(Job(0, J_OUT))
            dve.wait_ge(o_g, NT + 1)
            for k in range(KT):
                dve.wait_ge(op_hi, k + 1)
                src = zs[:, k, :] if k < PR else gl[:, k - PR, :]
                nc.vector.tensor_tensor(op[1][:, k, :], src, op[0][:, k, :].bitcast(F32), ALU.subtract).then_inc(op_lo, 1)

            def low_rows(phase, m):
                dve.wait_ge(h_hi, (phase + 1) * KT + m + 1)
                nc.vector.scalar_tensor_tensor(out=hh[1][:, m, :], in0=xT[:, m, :], scalar=gains[:, phase + 1, m:m + 1],
                                               in1=hh[0][:, m, :].bitcast(F32), op0=ALU.mult, op1=ALU.subtract).then_inc(h_lo, 1)

            def add_rows(job, m):
                wait(dve, mm, job.num(1))
                nc.vector.tensor_tensor(tri3(pick(xT, m)), tri3(pick(xT, m)), acc(job.slot), ALU.add).then_inc(pf, 1)

            dve.wait_ge(ld_xT, 16)
            for m in range(KT):
                job = Job(0, J_OUT + m)
                split_lo(job.next())
                add_rows(job, m)
                low_rows(0, m)
            for q in range(FQ):
                up, down = J_MLP + 2 * KT * q, J_MLP + 2 * KT * q + KT

                def hidden(job, j, q=q):
                    n = q * KT + j
                    split_lo(job.next())
                    if q == 0 and isinstance(j, int) and j == 0:
                        dve.wait_ge(rs_done, 1)
                    wait(dve, pf, job.num(1))
                    wait(dve, u_sq, n)
                    wait(dve, u_hi, n)
                    nc.vector.tensor_tensor(t2[:, :], t1[:, :], rsb[:, :], ALU.mult).then_inc(t_done, 1)
                    wait(dve, u_sq, n + 1)
                    wait(dve, u_hi, n + 1)
                    nc.vector.tensor_tensor(pick(uu[1], j), t3[:, :], pick(uu[0], j).bitcast(F32), ALU.subtract).then_inc(u_lo, 1)
                jobs(dve, up, KT, hidden)

                def out(job, j, q=q, down=down):
                    split_lo(job.next())
                    add_rows(job, j)
                    if q == FQ - 1:
                        low_rows(1, j)
                if q < FQ - 1:
                    jobs(dve, down, KT, out)
                else:
                    for m in range(KT):
                        out(Job(0, down + m), m)
            for m in range(KT):
                jg, jp = Job(0, J_GATE + 2 * m), Job(0, J_GATE + 2 * m + 1)
                split_lo(jp, kts=PK)
                if m == 0:
                    dve.wait_ge(rs_done, 2)
                dve.wait_ge(mm, jg.num(1))
                wait(dve, gt_done, m)
                nc.vector.tensor_tensor(tri3(t1[:, :]), acc(jg.slot), tri3(rsb[:, :]), ALU.mult).then_inc(pf, 1)
                if m == 0:
                    for k in range(PK):
                        for g in range(3):
                            dve.wait_ge(p_tr, 3 * k + g + 1)
                            w = 512 if g < 2 else NS
                            nc.vector.tensor_copy(pT[:, k, g * 512:g * 512 + w], ps[:, 6 + (3 * k + g) % 2, 0:w]).then_inc(p_cp, 1)
                if m < KT - 1:
                    split_lo(jp.next())
                if m == 0:
                    for k in range(PK):
                        dve.wait_ge(p_hi, k + 1)
                        nc.vector.tensor_tensor(pp[1][:, k, :], pT[:, k, :], pp[0][:, k, :].bitcast(F32), ALU.subtract).then_inc(p_lo, 1)
                dve.wait_ge(mm, jp.num(1))
                dve.wait_ge(gt_done, m + 1)
                nc.vector.tensor_tensor(tri3(pg[:, :]), acc(jp.slot), tri3(gt[:, :]), ALU.mult).then_inc(pf, 1)
                dve.wait_ge(pf, jp.num(1))
                nc.vector.tensor_tensor(xT[:, m, :], xT[:, m, :], pg[:, :], ALU.add).then_inc(x_new, 1)
                dve.wait_ge(sq_done, 2 * KT + m + 1)
                dve.wait_ge(x_new, m + 1)
                nc.vector.tensor_scalar(xT[:, m, :], xT[:, m, :], gains[:, 3, m:m + 1], None, ALU.mult).then_inc(xg_done, 1)


def bc(ap, axis, n):
    ap = ap.unsqueeze(axis)
    shape = list(ap.shape)
    shape[axis] = n
    return ap.to_broadcast(shape)


_INS = ["x_prompt", "x_sample", "state_ssm", "state_qkv_conv", "state_conf_conv", "p_prompt", "p_sample", "g_mix", "w_in",
        "w_short", "a_log", "dt_bias", "g_o", "w_dw", "b_dw", "g_cln", "b_cln", "w_out", "g_mlp", "w_up", "w_down",
        "w_ple", "g_ple", "w_ple_gate", "g_final"]
_OUTS = [("y_p", (1, SEQ, D)), ("y_s", (DB, DS, D)), ("ssm_p", (1, 1, H, HD, HD)), ("qkv_p", (1, 1, QH, 3 * DW)),
         ("conf_p", (1, 1, HIST, CC)), ("ssm_s", (1, DB, H, HD, HD)), ("qkv_s", (1, DB, QH, 3 * DW)),
         ("conf_s", (1, DB, HIST, CC))]


def kernel(**inputs):
    import concourse.bacc as _bacc
    from concourse.bass_utils import run_bass_kernel_spmd as _run

    nc = _bacc.Bacc("TRN2", target_bir_lowering=False, num_devices=1, dynamic_dma_scratch_size=1024)
    arrays, a, o = {}, {}, {}
    for name in _INS:
        arrays[f"in_{name}"] = np.ascontiguousarray(inputs[name])
    arrays["in_consts"] = shape_constants()
    for name, arr in arrays.items():
        a[name[3:]] = nc.dram_tensor(name, arr.shape, mybir.dt.from_np(arr.dtype), kind="ExternalInput").ap()
    for name, shape in _OUTS:
        o[name] = nc.dram_tensor(f"out_{name}", shape, F32, kind="ExternalOutput").ap()
    build(nc, a, o)
    r = _run(nc, [arrays], core_ids=[0])
    return tuple(r.results[0][f"out_{name}"] for name, _ in _OUTS)
```

```python
from contextlib import ExitStack

import numpy as np

import concourse.bass as bass
from concourse import mybir

F32 = mybir.dt.float32
F32R = mybir.dt.float32r
ALU = mybir.AluOpType
ACT = mybir.ActivationFunctionType
AX = mybir.AxisListType.X

P = 128
SEQ, DB, DS = 1024, 8, 4
NS = DB * DS
TOK = SEQ + NS
D = 1024
KT = D // P
NCH = 3
CW = TOK // NCH
H, HD = 8, 64
PR = H // 2
DW = H * HD
SC, DWC = 4, 31
CC = D - DW
CT = CC // P
C = 32
CPT = P // C
FF = 4 * D
FQ = FF // D
PLE = 256
PK = PLE // P
EPS = 1e-6
NT = SEQ // P
HIST, QH = DWC - 1, SC - 1
QT = 3 * DW // P
O_Z, O_B, O_GA, O_GB = 3 * DW, 4 * DW, 4 * DW + 2 * H, 4 * DW + 2 * H + CC

J_AB, J_GLU, J_Z, J_QKV, J_OUT = 0, 1, 9, 13, 25
J_MLP = J_OUT + KT
J_GATE = J_MLP + 2 * FQ * KT
J_END = J_GATE + 2 * KT

G_IN, G_TO, G_ALL, G_SEQ = 0, (NT + 1) * H, 2 * (NT + 1) * H, 2 * (NT + 1) * H + NT * CPT * H

PCOUNT = [9, 10, 12, 16]
PTAPS = [(p, k, k + 1) for p in range(CT) for k in range(PCOUNT[p])]
VTAPS = [(p, k, k + PCOUNT[p] if k else 0) for p in range(CT) for k in range(DWC - PCOUNT[p])]
PPLAN = [3] * (2 * CT - 2) + [4] * PR + [5, 3, 2, 1, 2]
VPLAN = [6] * (2 * CT - 2) + [5, 4, 4, 5] + [4, 4, 3, 3, 3, 3, 3]
assert sum(PPLAN) == len(PTAPS) and sum(VPLAN) == len(VTAPS) and len(PTAPS) + len(VTAPS) == CT * DWC

CONSTS = [("ident", P), ("ones", P), ("bd64", P), ("uinc", P), ("sgt", P), ("uinc4", P), ("sgt4", P),
          ("blk", CPT), ("blk4", DB), ("tri", C), ("tri4", C), ("str4", C)]
NV = 4 * KT + 3 * CT + 1


def shape_constants():
    r, c = np.arange(P)[:, None], np.arange(P)[None, :]

    def inside(n):
        return r // n == c // n

    low = (r < NS) & (c < NS)
    parts = {
        "ident": r == c, "ones": r >= 0 * c, "bd64": inside(HD) / HD,
        "uinc": (r <= c) & inside(C), "sgt": (r > c) & inside(C),
        "uinc4": (r <= c) & inside(DS) & low, "sgt4": (r > c) & inside(DS) & low,
        "blk": r // C == c[:, :CPT], "blk4": (r // DS == c[:, :DB]) & (r < NS),
        "tri": r % C <= c[:, :C], "tri4": (r <= c[:, :C]) & (r // DS == c[:, :C] // DS),
        "str4": (r < c[:, :C]) & (r // DS == c[:, :C] // DS),
    }
    return np.concatenate([parts[n].astype(np.float32) for n, _ in CONSTS], axis=1)


class Job:

    def __init__(self, i, c):
        self.i, self.c, self.slot = i, c, c % 2

    def num(self, off=0):
        return 2 * self.i + (self.c + off)

    def half(self):
        return self.i + self.c // 2

    def next(self):
        return Job(self.i, self.c + 1)


ORDER = list(range(KT // 2, KT)) + list(range(KT // 2))


def wait(eng, sem, value):
    if isinstance(value, int) and value <= 0:
        return
    eng.wait_ge(sem, value)


def jobs(eng, first, n, body):
    for j in range(min(n, 2)):
        body(Job(0, first + j), j)
    if n > 2:
        with eng.Fori(0, (n - 2) // 2) as i:
            for u in range(2):
                body(Job(i, first + 2 + u), 2 * i + (2 + u))


class Chain:

    def __init__(self, eng, sem):
        self.eng, self.sem, self.n = eng, sem, 0

    def mark(self, ins):
        self.n += 1
        ins.then_inc(self.sem, 1)
        return self.n

    def step(self, ins):
        self.eng.wait_ge(self.sem, self.mark(ins))


def build(nc, a, o):
    ctx = ExitStack()
    with ctx:
        base = (nc.sbuf_base + 31) // 32 * 32
        LIM = nc.sbuf_base + nc.sbuf_bytes_remaining
        R1 = base
        WR = R1 + 67584
        TR = WR + 24576
        XR = TR + 4 * 4224
        PRS = XR + 33792 + 67584
        cur = {}

        def at(region, name, shape, dt=F32, off=None):
            if off is None:
                off = cur.get(region, 0)
            size = int(np.prod(shape[1:])) * 4
            size = (size + 31) // 32 * 32
            cur[region] = off + size
            t = nc.alloc_sbuf_tensor_at(name, shape, dt, offset=region + off)
            assert region + off + size <= LIM, name
            return t

        sem = lambda name: ctx.enter_context(nc.semaphore(name))

        tmp = [at(TR, f"tmp{n}", [P, TOK]) for n in range(4)]
        rsb, t1, t2, t3 = tmp

        ident = at(PRS, "ident", [P, P])
        ones = at(PRS, "ones", [P, P])
        vec = at(PRS, "vec", [P, NV])
        gains = vec[:, 0:4 * KT].rearrange("p (n k) -> p n k", k=KT)
        cvp = vec[:, 4 * KT:4 * KT + 3 * CT].rearrange("p (n k) -> p n k", k=CT)
        g2 = vec[:, NV - 1:NV]
        eps = at(PRS, "eps", [P, 1])
        rtok = at(PRS, "rtok", [P, 16])
        ltok = at(PRS, "ltok", [P, 16])
        grow = at(PRS, "grow", [HIST, CC])
        gsrow = at(PRS, "gsrow", [NS, CC])
        cns = at(PRS, "cns", [P, SEQ])
        sqt = at(PRS, "sqt", [P, DW], off=cur[PRS] - 4 * SEQ)
        Vn = at(PRS, "Vn", [P, DW])
        dec = cur[PRS]
        qrow = at(PRS, "qrow", [QH + DB * QH, QT * P], off=cur[PRS] - 4 * SEQ)
        cur[PRS] = dec
        dV = at(PRS, "dV", [NS, DW], off=cur[PRS] - 4 * SEQ - 4 * CC)
        dKbe = at(PRS, "dKbe", [NS, DW], off=cur[PRS] - 2 * 4 * CC)
        cur[PRS] = dec
        prow = at(PRS, "prow", [P, NT + 1, PLE], off=dec - 4 * CC * 2 - 4 * SEQ)
        cur[PRS] = dec
        pT = [t1, at(PRS, "pT1", [P, TOK], off=dec + 1024)]
        cur[PRS] = dec
        dKd = at(PRS, "dKd", [NS, DW])
        LQd = at(PRS, "LQd", [NS, H, 2, C])
        WQ = at(PRS, "WQ", [P, PR, 2, NS])
        ss = at(PRS, "ss", [P, H])
        rn = at(PRS, "rn", [P, NT + 1, 2 * H])
        gr = at(PRS, "gr", [P, NT, CPT, H])
        grs = at(PRS, "grs", [NS, DB, H])
        gds = at(PRS, "gds", [P, CT, NS])
        assert PRS + cur[PRS] <= LIM

        w_raw = [at(WR, f"w_raw{s}", [P, KT, P]) for s in range(2)]
        w_hi = [at(WR, f"w_hi{s}", [P, KT, P], F32R) for s in range(2)]
        w_lo = [at(WR, f"w_lo{s}", [P, KT, P], F32R) for s in range(2)]
        hm = [at(R1, f"hm_{n}", [P, KT, TOK], F32R, off=o_) for n, o_ in (("hi", 0), ("lo", 33792))]
        op = [at(R1, f"op_{n}", [P, KT, TOK], F32R, off=o_) for n, o_ in (("hi", 0), ("lo", 33792))]
        uu = [at(R1, f"u_{n}", [P, KT, TOK], F32R, off=o_) for n, o_ in (("hi", 0), ("lo", 33792))]
        pp = [at(R1, f"p_{n}", [P, PK, TOK], F32R, off=o_) for n, o_ in (("hi", 0), ("lo", 8448))]
        gt = at(R1, "gt", [P, TOK])
        pg = at(R1, "pg", [P, TOK])
        yrow = at(R1, "yrow", [P, NT + 1, D], off=0)
        hh = [at(XR, f"h_{n}", [P, KT, TOK], F32R, off=33792 * o_) for n, o_ in (("hi", 1), ("lo", 2))]
        xT = at(XR, "xT", [P, KT, TOK], off=0)

        xT0 = at(XR, "xT0", [P, KT, TOK], off=0)
        zs = at(XR, "zs", [P, PR, TOK], off=0)
        gl = at(XR, "gl", [P, CT, TOK])
        qkv0 = cur[XR]
        xin = at(XR, "xin", [P, NT + 1, D])
        hq = at(XR, "hq", [DB * QH, QT * P])
        hc = at(XR, "hc", [4 * HIST, 2, CC])
        assert cur[XR] <= qkv0 + QT * TOK * 4
        qkvT = at(XR, "qkvT", [P, QT, TOK], off=qkv0)
        slots = [at(XR, f"cv{n}", [P, TOK], off=qkv0 + n * TOK * 4) for n in range(QT)]
        accv, accp, prd = slots[8:12], (slots[4], slots[7]), slots[5:7]

        def squares(j):
            return slots[(4, 4, 4, 8, 8, 9, 8, 9)[j]]
        cur[XR] = qkv0 + QT * TOK * 4
        gls = at(XR, "gls", [P, CT, DB, HIST + DS])
        raws = at(XR, "raws", [P, QT, DB, QH + DS])
        tail = at(XR, "tail", [P, QT, QH + DB * QH])
        consts = {}
        for name, w in CONSTS[2:]:
            consts[name] = at(XR, "c_" + name, [P, w])
        wsh = at(XR, "wsh", [P, SC, QT])
        wdw = at(XR, "wdw", [P, DWC, CT])
        ab = at(XR, "ab", [P, NT + 1, 2 * H])
        hp = at(XR, "hp", [P, 2, H])
        sm = [at(XR, f"sm{n}", [P, NT + 1, H]) for n in range(4)]
        beta = at(XR, "beta", [P, NT + 1, H])
        gg = at(XR, "gg", [P, NT + 1, H])
        egc = at(XR, "egc", [P, NT + 1, H])
        ekd = at(XR, "ekd", [P, NT + 1, H])
        gld = at(XR, "gld", [P, NT, CPT, PR])
        glds = at(XR, "glds", [P, DB, PR])
        assert cur[XR] <= 33792 + 67584, cur[XR]

        sqd = at(TR, "sqd", [P, D], off=3 * 4224)
        vrow = at(TR, "vrow", [NV, P], off=4224)
        srow = at(TR, "srow", [SC * QT, P])
        drow = at(TR, "drow", [DWC * CT, P])

        Vb = at(R1, "Vb", [P, NT, DW], off=0)
        Kbe = at(R1, "Kbe", [P, NT, DW])
        Kd = at(R1, "Kd", [P, NT, DW])
        QdT = at(R1, "QdT", [P, NT, PR, P])
        S = at(R1, "S", [P, PR, HD])
        Sd = at(R1, "Sd", [P, PR, HD])
        assert cur[R1] <= 67584
        LQ = at(TR, "LQ", [P, NT, H, 2, C], off=0)
        tk = [at(WR, f"tk{n}", [P, DW], off=2048 * n) for n in range(4)]
        KTl = at(WR, "KTl", [P, PR, P])
        RR = at(WR, "RR", [P, PR, 2, P])
        ug = at(WR, "ug", [P, H, P])
        Dm = [at(WR, f"Dm{n}", [P, H, C]) for n in range(2)]
        scb = at(WR, "scb", [P, 5, NT + 1, H])
        assert cur[WR] <= 24576, cur[WR]
        Xp = at(WR, "Xp", [P, 2, C * C], off=0)
        prod = at(WR, "prod", [P, 2, C * C])
        assert cur[WR] <= 24576, cur[WR]
        VnM = at(WR, "VnM", [NS, H, DB, HD], off=4096)
        NLP = NT - 2 * C * C // (H * P)
        Tbd = at(XR, "Tbd", [P, NT, H, P], off=qkv0)
        Lp = at(XR, "Lp", [P, 2, C * C], off=qkv0 + 4 * NLP * H * P)
        WT = at(XR, "WT", [P, 2, PR, P])
        S0 = at(XR, "S0", [P, PR, DB, HD])
        WSt = at(XR, "WSt", [P, PR, 2, NS])
        Ns = at(XR, "Ns", [NS, H, C])
        NTs = at(XR, "NTs", [NS, H, C])
        onr = at(XR, "onr", [P, DW], off=cur[XR] - 2 * H * C * 4)
        Ms = at(XR, "Ms", [NS, H, C])
        Ts = at(XR, "Ts", [NS, H, C])
        assert cur[XR] <= qkv0 + QT * TOK * 4

        ps = ctx.enter_context(nc.psum_tensor("ps", [P, 8, 512], F32))

        def acc(slot, m=P):
            return ps[0:m, 3 * slot:3 * slot + 3, 0:CW]

        def tri3(t):
            return t.rearrange("p (c n) -> p c n", c=NCH)

        xT_dram = nc.dram_tensor("xT_dram", [D, TOK], F32).ap().rearrange("(k p) t -> p k t", p=P)
        lt_dram = nc.dram_tensor("lt_dram", [2, P, C * C], F32).ap()
        tt_dram = nc.dram_tensor("tt_dram", [2, P, C * C], F32).ap()

        ld_x = [sem(f"ld_x{i}") for i in range(NT + 1)]
        ld_i = sem("ld_ident")
        ld_c = sem("ld_consts")
        init = sem("init_done")
        vec_tr = sem("vec_tr")
        vec_cp = sem("vec_cp")
        ld_h = sem("ld_h")
        x_sq = sem("x_sq")
        x_tr = sem("x_tr")
        x_cp = sem("x_cp")
        x_cp2 = sem("x_cp2")
        x_ln = sem("x_ln")
        x_dg = sem("x_dg")
        x_bc = sem("x_bc")
        x_rs = sem("x_rs")
        h_hi = sem("h_hi")
        h_lo = sem("h_lo")
        hs_tr = sem("hs_tr")
        hs_cp = sem("hs_cp")
        st_x = sem("st_x")
        w_dma = [sem(f"w_dma{s}") for s in range(2)]
        w_hid = sem("w_hi_done")
        w_lod = sem("w_lo_done")
        mm = sem("mm_done")
        pf = sem("psum_free")
        y_done = sem("conv_done")
        silu_done = sem("silu_done")
        sg_done = sem("sg_done")
        sgr_done = sem("sgr_done")
        z_done = sem("z_done")
        dch = sem("dve_chain")
        ach = sem("act_chain")
        cv_prod = sem("cv_prod")
        cv_add = sem("cv_add")
        cv_acc = sem("cv_acc")
        cv_mm = sem("cv_mm")
        cv_c = sem("cv_centred")
        cv_sq = sem("cv_sq")
        cv_var = sem("cv_var")
        cv_r = sem("cv_r")
        cv_n = sem("cv_n")
        cv_out = sem("cv_out")
        hist_tr = sem("hist_tr")
        hist_cp = sem("hist_cp")
        st_h = sem("st_h")
        ab_tr, ab_cp = sem("ab_tr"), sem("ab_cp")
        gs_act, gs_dve, gs_mm = sem("gs_act"), sem("gs_dve"), sem("gs_mm")
        d_ug, d_mm, d_exp, d_msk = sem("d_ug"), sem("d_mm"), sem("d_exp"), sem("d_msk")
        n_sq, n_mm, n_cp, n_r = sem("n_sq"), sem("n_mm"), sem("n_cp"), sem("n_r")
        g_qk, g_tok = sem("g_qk"), sem("g_tok")
        g_big, g_bt, g_ev, g_aq, g_lq = (sem(n) for n in ("g_big", "g_bt", "g_ev", "g_aq", "g_lq"))
        tb0, lt_st, lt_ld, inv = (sem(n) for n in ("tbd_zero", "lt_st", "lt_ld", "inv_done"))
        tt_st = [sem(f"tt_st{n}") for n in range(2)]
        tt_ld = [sem(f"tt_ld{t}") for t in range(NT)]
        uw_mm, uw_ev = sem("uw_mm"), sem("uw_ev")
        ws_mm, vn_d, ds_mm, s_up = ([sem(f"{n}{par}") for par in range(2)]
                                        for n in ("ws_mm", "vn_done", "ds_mm", "state_updated"))
        sd, o_mm = sem("state_decayed"), sem("o_mm")
        o_sq, o_ss, o_r, o_n, o_tr, o_g = (sem(n) for n in ("o_sq", "o_ss", "o_r", "o_n", "o_tr", "o_gated"))
        st_s, ld_s = sem("st_s"), sem("ld_s")
        sp_mm, sp_dve, sp_act = sem("sample_mm"), sem("sample_dve"), sem("sample_act")
        sp_vm, sp_g, sp_ds, sp_up, st_p = (sem(n) for n in ("sample_v_masked", "sample_decayed", "sample_ds", "sample_updated", "st_p"))
        op_hi, op_lo = sem("op_hi"), sem("op_lo")
        ld_xT = [sem(f"ld_xT{n}") for n in range(2)]
        x_new = sem("x_new")
        sq_done, ss_done = sem("sq_done"), sem("ss_done")
        st_mm, st_ln = sem("stat_mm"), sem("stat_ln")
        rs_done = sem("rs_done")
        t_done, u_hi, u_sq, u_lo = (sem(n) for n in ("t_done", "u_hi_done", "u_sq", "u_lo_done"))
        gt_done = sem("gt_done")
        ld_p, p_tr, p_cp, p_hi, p_lo = (sem(n) for n in ("ld_p", "p_tr", "p_cp", "p_hi_done", "p_lo_done"))
        xg_done, y_mm, y_tr, y_cp, st_y = (sem(n) for n in ("xg_done", "y_mm", "y_tr", "y_cp", "st_y"))

        w_in, w_out = a["w_in"][0], a["w_out"][0]
        w_up, w_down = a["w_up"][0], a["w_down"][0]
        w_ple, w_gate = a["w_ple"][0], a["w_ple_gate"][0]

        def tile_tokens(i):
            return (P, i * P) if i < NT else (NS, SEQ)

        def dg(i):
            return t1[:, i * P:(i + 1) * P] if i < NT else t2[:, 0:P]

        def pick(t, m):
            return t[:, m, :] if isinstance(m, int) else t[:, bass.ds(m, 1), :].rearrange("p a t -> p (a t)")

        HT = NT // 2

        def load_inverses(eng, t, blocks):
            if t % HT == 0:
                eng.wait_ge(tt_st[t // HT], 16)
            for b in blocks:
                src = tt_dram[t // HT].rearrange("(s t b) (m c) -> t b m s c", t=HT, b=CPT, c=C)[t % HT, b]
                eng.dma_start(Tbd[b * C:(b + 1) * C, t, :, b * C:(b + 1) * C], src).then_inc(tt_ld[t], 16)

        def exps(t):
            return 2 * CPT * t

        block = ctx.enter_context(nc.Block())

        @block.sync
        def _(sp):
            def load_w(job, src, kts=KT, cols=P):
                wait(sp, w_lod, job.num(-1))
                sp.dma_start(w_raw[job.slot][:, 0:kts, 0:cols], src.rearrange("(k p) c -> p k c", p=P))\
                  .then_inc(w_dma[job.slot], 16)

            cin = a["consts"]
            off = 0
            for name, w in CONSTS:
                dst = {"ident": ident, "ones": ones}.get(name) or consts[name]
                sp.dma_start(dst[:, :], cin[:, off:off + w]).then_inc(ld_i if off == 0 else ld_c, 16)
                off += w
                if name == "ident":
                    for i in range(2):
                        n, t0 = tile_tokens(i)
                        sp.dma_start(xin[0:n, i, :], a["x_prompt"][0, t0:t0 + n, :]).then_inc(ld_x[i], 16)
            for i in range(2, NT + 1):
                n, t0 = tile_tokens(i)
                src = a["x_prompt"][0, t0:t0 + n, :] if i < NT else a["x_sample"].rearrange("b t d -> (b t) d")
                sp.dma_start(xin[0:n, i, :], src).then_inc(ld_x[i], 16)
            load_w(Job(0, J_AB), w_in[:, O_B:O_B + 2 * H], cols=2 * H)
            load_w(Job(0, 1), w_in[:, O_GB:O_GB + P])
            sp.wait_ge(x_cp, NT + 1)
            sp.wait_ge(x_cp2, NT + 1)
            sp.dma_start(xT_dram, xT0[:, :, :]).then_inc(st_x, 16)
            for p in range(CT):
                if p:
                    load_w(Job(0, J_GLU + 2 * p), w_in[:, O_GB + p * P:O_GB + (p + 1) * P])
                load_w(Job(0, J_GLU + 2 * p + 1), w_in[:, O_GA + p * P:O_GA + (p + 1) * P])
            for j in range(PR):
                load_w(Job(0, J_Z + j), w_in[:, O_Z + j * P:O_Z + (j + 1) * P])
            for j in range(QT):
                load_w(Job(0, J_QKV + j), w_in[:, j * P:(j + 1) * P])
                if j == 0:
                    sp.dma_start(o["conf_s"][0, :, 0:HIST - DS, :], a["state_conf_conv"][0, :, DS:HIST, :]).then_inc(st_h, 16)
                    sp.wait_ge(hist_cp, 1)
                    sp.dma_start(o["conf_p"][0, 0], grow[0:HIST, :]).then_inc(st_h, 16)
                    sp.wait_ge(hist_cp, 2)
                    for b in range(DB):
                        sp.dma_start(o["conf_s"][0, b, HIST - DS:HIST, :], gsrow[b * DS:(b + 1) * DS, :]).then_inc(st_h, 16)
            sp.wait_ge(hist_cp, 5)
            sp.dma_start(o["qkv_p"][0, 0], qrow[0:QH, :]).then_inc(st_h, 16)
            sp.dma_start(o["qkv_s"][0].rearrange("b r c -> (b r) c"), qrow[QH:QH + DB * QH, :]).then_inc(st_h, 16)
            for t in range(NT):
                sp.wait_ge(g_lq, t + 1)
                dst = lt_dram[t // HT].rearrange("(s t b) (m c) -> t (b m) s c", t=HT, b=CPT, c=C)[t % HT]
                sp.dma_start(dst, LQ[:, t, :, 0, :]).then_inc(lt_st, 16)
            sp.wait_ge(g_tok, NT + 1)
            sp.wait_ge(lt_st, 16 * NT)
            for half in range(2):
                sp.dma_start(Lp[:, half, :], lt_dram[half]).then_inc(lt_ld, 16)
            sp.wait_ge(lt_ld, 32)
            for par in range(2):
                for q in range(PR):
                    sp.dma_start(S0[par * HD:(par + 1) * HD, q, :, :],
                                 a["state_ssm"][0, :, 2 * q + par].rearrange("b d e -> d b e")).then_inc(ld_s, 16)
            sp.wait_ge(inv, 1)
            for half in range(2):
                sp.dma_start(tt_dram[half], Xp[:, half, :]).then_inc(tt_st[half], 16)
            sp.wait_ge(tb0, 2)
            for t in range(NT):
                load_inverses(sp, t, range(CPT // 2))
            sp.wait_ge(sp_ds, PR)
            for j in range(2):
                load_w(Job(0, J_OUT + j), w_out[:, ORDER[j] * P:(ORDER[j] + 1) * P])
            sp.wait_ge(sp_up, PR)
            for par in range(2):
                for q in range(PR):
                    sp.dma_start(o["ssm_s"][0, :, 2 * q + par].rearrange("b d e -> d b e"),
                                 S0[par * HD:(par + 1) * HD, q, :, :]).then_inc(st_s, 16)
            for par in range(2):
                sp.wait_ge(s_up[par], NT * CPT + 1)
            for par in range(2):
                sp.dma_start(o["ssm_p"][0, 0].rearrange("(q r) d e -> r d q e", r=2)[par],
                             S[par * HD:(par + 1) * HD, :, :]).then_inc(st_p, 16)
            sp.wait_ge(st_x, 16)
            for n in range(2):
                sp.wait_ge(op_lo, KT // 2 * (n + 1))
                rows = slice(ORDER[4 * n], ORDER[4 * n] + KT // 2)
                sp.dma_start(xT[:, rows, :], xT_dram[:, rows, :]).then_inc(ld_xT[n], 16)
            for j in range(2, KT):
                load_w(Job(0, J_OUT + j), w_out[:, ORDER[j] * P:(ORDER[j] + 1) * P])
            for i in range(NT + 1):
                n, t0 = tile_tokens(i)
                src = a["p_prompt"][0, 0, t0:t0 + n, :] if i < NT else a["p_sample"][0].rearrange("b t d -> (b t) d")
                sp.dma_start(prow[0:n, i, :], src).then_inc(ld_p, 16)
            for q in range(FQ):
                up, down = J_MLP + 2 * KT * q, J_MLP + 2 * KT * q + KT
                with sp.Fori(0, KT // 2) as i:
                    for u in range(2):
                        load_w(Job(i, up + u), w_up[:, bass.ds((2 * i + u + q * KT) * P, P)])
                with sp.Fori(0, KT // 2) as i:
                    for u in range(2):
                        load_w(Job(i, down + u), w_down[q * D:(q + 1) * D, bass.ds((2 * i + u) * P, P)])
            for m in range(KT):
                load_w(Job(0, J_GATE + 2 * m), w_gate[:, m * P:(m + 1) * P])
                load_w(Job(0, J_GATE + 2 * m + 1), w_ple[:, m * P:(m + 1) * P], kts=PK)
            for i in range(NT + 1):
                n, t0 = tile_tokens(i)
                sp.wait_ge(y_cp, i + 1)
                dst = o["y_p"][0, t0:t0 + n, :] if i < NT else o["y_s"].rearrange("b t d -> (b t) d")
                sp.dma_start(dst, yrow[0:n, i, :]).then_inc(st_y, 16)
            sp.wait_ge(st_y, 16 * (NT + 1))
            sp.wait_ge(st_p, 32)
            sp.wait_ge(st_s, 16 * 2 * PR)
            sp.wait_ge(st_h, 16 * (2 + DB + 2))
            sp.wait_ge(st_x, 16)

        @block.gpsimd
        def _(pool):
            def taps(s):
                for n in range(sum(PPLAN[:s]), sum(PPLAN[:s + 1])):
                    p, k, s0 = PTAPS[n]
                    pool.wait_ge(cv_prod, n + 1)
                    wait(pool, cv_add, n)
                    if k:
                        nc.gpsimd.tensor_tensor(accp[p % 2][:, s0:SEQ], accp[p % 2][:, s0:SEQ], prd[n % 2][:, s0:SEQ], ALU.add)\
                          .then_inc(cv_add, 1)
                    else:
                        nc.gpsimd.memset(accp[p % 2][:, 0:1], 0.0).then_inc(cv_add, 1)

            for p in range(CT):
                if p:
                    taps(2 * p - 2)
                pool.wait_ge(sg_done, p + 1)
                if p:
                    pool.wait_ge(pf, J_GLU + 2 * p)
                nc.gpsimd.tensor_tensor(t2[:, :], t1[:, :], rsb[:, :], ALU.mult).then_inc(sgr_done, 1)
                if p:
                    taps(2 * p - 1)
            for s in range(2 * CT - 2, 2 * CT - 2 + PR):
                taps(s)
            for j in range(1, QT):
                job = Job(0, J_QKV + j)
                pool.wait_ge(w_lod, J_QKV + j)
                wait(pool, w_hid, job.num(1))
                nc.gpsimd.tensor_tensor(w_lo[job.slot][:, :, :], w_raw[job.slot][:, :, :], w_hi[job.slot][:, :, :].bitcast(F32),
                                        ALU.subtract).then_inc(w_lod, 1)
                if 2 * CT - 2 + PR + j - 1 < len(PPLAN):
                    taps(2 * CT - 2 + PR + j - 1)

            def logits(t):
                n, _ = tile_tokens(t)
                wait(pool, d_mm, 2 * t)
                tri = consts["uinc" if t < NT else "uinc4"][0:n, 0:n]
                for r in range(2):
                    last = nc.gpsimd.tensor_tensor(ug[0:n, r * PR:(r + 1) * PR, 0:n],
                                                   bc(gg[0:n, t, :].rearrange("p (q r) -> p r q", r=2)[:, r, :], 2, n), bc(tri, 1, PR), ALU.mult)
                last.then_inc(d_ug, 1)

            pool.wait_ge(gs_dve, 9)
            pool.wait_ge(mm, J_OUT)
            for t in range(NT + 1):
                logits(t)

            pool.wait_ge(g_tok, NT + 1)
            nc.gpsimd.memset(Tbd[:, 0:NLP, :, :], 0.0).then_inc(tb0, 1)
            pool.wait_ge(inv, 1)
            nc.gpsimd.memset(Tbd[:, NLP:NT, :, :], 0.0).then_inc(tb0, 1)

            pool.wait_ge(sp_mm, 5)
            for q in range(PR):
                nc.gpsimd.tensor_tensor(S0[:, q, :, :], S0[:, q, :, :], bc(glds[:, :, q], 2, HD), ALU.mult).then_inc(sp_g, 1)
            pool.wait_ge(sp_dve, 4)
            for half in range(2):
                pool.wait_ge(tt_st[half], 16)
            nc.gpsimd.tensor_tensor(VnM[:, :, :, :], bc(dV[:, :].rearrange("p (h e) -> p h e", e=HD), 2, DB),
                                    bc(bc(consts["blk4"][0:NS, :], 1, H), 3, HD), ALU.mult).then_inc(sp_vm, 1)

            for n in range(NT * CPT):
                for par in range(2):
                    pool.wait_ge(s_up[par], n + 1)
                nc.gpsimd.tensor_tensor(Sd[:, :, :], S[:, :, :], bc(gld[:, n // CPT, n % CPT, :], 2, HD), ALU.mult).then_inc(sd, 1)

            def sum_squares(phase):
                for m in range(1, KT):
                    pool.wait_ge(sq_done, phase * KT + m + 1)
                    if m > 1:
                        pool.wait_ge(ss_done, phase * (KT - 1) + m - 1)
                    nc.gpsimd.tensor_tensor(t3[:, :], t3[:, :], t2[:, :], ALU.add).then_inc(ss_done, 1)

            sum_squares(0)
            for q in range(FQ):
                def hidden(job, j, q=q):
                    n = q * KT + j
                    wait(pool, t_done, n + 1)
                    if q or not isinstance(j, int) or j:
                        wait(pool, u_lo, n)
                    nc.gpsimd.tensor_tensor(t3[:, :], t2[:, :], t2[:, :], ALU.mult).then_inc(u_sq, 1)
                jobs(pool, J_MLP + 2 * KT * q, KT, hidden)
            sum_squares(1)
            sum_squares(2)

        @block.scalar
        def _(act):
            ac = Chain(act, ach)

            def split_hi(job, kts=KT, cols=P):
                wait(act, w_dma[job.slot], 16 * job.half() + 16)
                wait(act, mm, job.num(-1))
                nc.scalar.activation(w_hi[job.slot][:, 0:kts, 0:cols], w_raw[job.slot][:, 0:kts, 0:cols],
                                     ACT.Copy).then_inc(w_hid, 1)

            for n, (name, k) in enumerate((("g_mix", KT), ("g_mlp", KT), ("g_ple", KT), ("g_final", KT),
                                           ("b_dw", CT), ("g_cln", CT), ("b_cln", CT))):
                src = a[name] if name == "g_final" else a[name][0]
                r0 = n * KT if n < 4 else 4 * KT + (n - 4) * CT
                act.dma_start(vrow[r0:r0 + k, :], src.rearrange("(k p) -> k p", p=P)).then_inc(ld_h, 16)
            for par in range(2):
                act.dma_start(vrow[NV - 1:NV, par * HD:(par + 1) * HD], a["g_o"]).then_inc(ld_h, 16)
            act.dma_start(srow[:, :], a["w_short"][0].rearrange("j (m p) -> (j m) p", p=P)).then_inc(ld_h, 16)
            act.dma_start(drow[:, :], a["w_dw"][0].rearrange("j (m p) -> (j m) p", p=P)).then_inc(ld_h, 16)
            act.dma_start(hq[:, :], a["state_qkv_conv"][0].rearrange("b r c -> (b r) c")).then_inc(ld_h, 16)
            for g in range(2):
                act.dma_start(hc[:, g, :], a["state_conf_conv"][0, 4 * g:4 * g + 4].rearrange("b r c -> (b r) c")).then_inc(ld_h, 16)
            act.dma_start(hp[:, 0, :], a["a_log"].to_broadcast([P, H])).then_inc(ld_h, 16)
            act.dma_start(hp[:, 1, :], a["dt_bias"].to_broadcast([P, H])).then_inc(ld_h, 16)
            act.wait_ge(init, 4)
            for i in range(NT + 1):
                n, t0 = tile_tokens(i)
                act.wait_ge(ld_x[i], 16)
                if i:
                    act.wait_ge(x_sq, i)
                nc.scalar.activation(sqd[0:n, :], xin[0:n, i, :], ACT.Square, accum_out=rtok[0:n, i:i + 1]).then_inc(x_sq, 1)
                act.wait_ge(x_tr, 2 * i + 1)
                nc.scalar.activation(xT0[:, 0:4, t0:t0 + n], ps[:, (2 * i) % 6, :].rearrange("p (k t) -> p k t", k=4)[:, :, 0:n],
                                     ACT.Copy).then_inc(x_cp, 1)
            act.wait_ge(x_sq, NT + 1)
            ac.step(nc.scalar.activation(ltok[:, 0:NT + 1], rtok[:, 0:NT + 1], ACT.Ln, bias=eps[:, :], scale=1.0 / D))
            nc.scalar.activation(rtok[:, 0:NT + 1], ltok[:, 0:NT + 1], ACT.Exp, scale=-0.5).then_inc(x_ln, 1)
            split_hi(Job(0, J_AB), cols=2 * H)
            act.wait_ge(x_cp, NT + 1)
            act.wait_ge(x_cp2, NT + 1)
            act.wait_ge(vec_cp, 3)
            for k in range(KT):
                nc.scalar.activation(hm[0][:, k, :], xT0[:, k, :], ACT.Copy, scale=gains[:, 0, k:k + 1]).then_inc(h_hi, 1)
            for g in range(3):
                act.wait_ge(x_bc, g + 1)
                w = 4 * P if g < 2 else NS
                nc.scalar.activation(rsb[:, g * 512:g * 512 + w], ps[:, 3 + g, 0:w], ACT.Copy).then_inc(x_rs, 1)
            split_hi(Job(0, 1))

            a_n = [0]

            def small(out, in_, f, **kw):
                nc.scalar.activation(out, in_, f, **kw).then_inc(gs_act, 1)
                a_n[0] += 1
                act.wait_ge(gs_act, a_n[0])

            def decays_a():
                act.wait_ge(ab_cp, 1)
                small(beta[:, :, :], ab[:, :, 0:H], ACT.Exp, scale=-1.0)
                act.wait_ge(gs_dve, 3)
                small(sm[1][:, :, :], sm[1][:, :, :], ACT.Exp, scale=-1.0)
                small(sm[2][:, :, :], sm[1][:, :, :], ACT.Ln, bias=1.0)
                small(hp[:, 0, :], hp[:, 0, :], ACT.Exp)

            def decays_b():
                act.wait_ge(gs_mm, 1)
                nc.scalar.activation(egc[:, :, :], ps[:, 7, G_IN:G_TO].rearrange("p (t h) -> p t h", h=H), ACT.Exp).then_inc(gs_act, 1)
                nc.scalar.activation(ekd[:, :, :], ps[:, 7, G_TO:G_ALL].rearrange("p (t h) -> p t h", h=H), ACT.Exp).then_inc(gs_act, 1)
                for par in range(2):
                    rows = slice(par * HD, (par + 1) * HD)
                    nc.scalar.activation(gld[rows, :, :, :].rearrange("p t b q -> p (t b) q"),
                                         ps[rows, 7, G_ALL:G_SEQ].rearrange("p (t q r) -> p t q r", q=PR, r=2)[:, :, :, par],
                                         ACT.Exp).then_inc(gs_act, 1)
                    nc.scalar.activation(glds[rows, :, :], ps[rows, 7, G_SEQ:G_SEQ + DB * H].rearrange("p (t q r) -> p t q r", q=PR, r=2)[:, :, :, par],
                                         ACT.Exp).then_inc(gs_act, 1)

            def taps(s):
                for n in range(sum(PPLAN[:s]), sum(PPLAN[:s + 1])):
                    p, k, s0 = PTAPS[n]
                    act.wait_ge(pf, J_GLU + 2 * p + 2)
                    if k == 0 and p >= 2:
                        act.wait_ge(cv_acc, p - 1)
                    if n > 2:
                        act.wait_ge(cv_add, n - 1)
                    dst = prd[n % 2] if k else accp[p % 2]
                    nc.scalar.activation(dst[:, s0:SEQ], gl[:, p, 0:SEQ - s0], ACT.Copy,
                                         scale=wdw[:, HIST - s0, p:p + 1]).then_inc(cv_prod, 1)

            for p in range(CT):
                split_hi(Job(0, J_GLU + 2 * p + 1))
                if p:
                    taps(2 * p - 2)
                act.wait_ge(pf, J_GLU + 2 * p + 1)
                if p:
                    act.wait_ge(sgr_done, p)
                nc.scalar.activation(t1[:, :], t3[:, :], ACT.Sigmoid).then_inc(sg_done, 1)
                split_hi(Job(0, J_GLU + 2 * p + 2))
                if p:
                    taps(2 * p - 1)
                if p < 2:
                    (decays_a, decays_b)[p]()
            act.wait_ge(st_x, 16)
            for j in range(PR):
                split_hi(Job(0, J_Z + j + 1))
                taps(2 * CT - 2 + j)
                if j == 1:
                    act.wait_ge(hist_tr, 1)
                    nc.scalar.activation(grow[0:HIST, :], ps[0:HIST, 6, :], ACT.Copy).then_inc(hist_cp, 1)
                    act.wait_ge(hist_tr, 2)
                    nc.scalar.activation(gsrow[0:NS, :], ps[0:NS, 7, :], ACT.Copy).then_inc(hist_cp, 1)
                act.wait_ge(pf, J_Z + j + 1)
                nc.scalar.activation(zs[:, j, :], (t1, t2)[j % 2][:, :], ACT.Silu).then_inc(z_done, 1)

            def channel_norm(n, out=False):
                p, var = divmod(n, 2)
                v = accv[p][:, 0:SEQ] if p < CT else gds[:, :, :].rearrange("p m t -> p (m t)")
                w = SEQ if p < CT else CT * NS
                if not var:
                    act.wait_ge(cv_c, p + 1)
                    nc.scalar.activation(cns[:, 0:w], v, ACT.Square).then_inc(cv_sq, 1)
                    return
                if out:
                    act.wait_ge(cv_n, p + 1)
                    for m in range(CT) if p == CT else [p]:
                        nc.scalar.activation(gl[:, m, SEQ:TOK] if p == CT else gl[:, m, 0:SEQ], gds[:, m, :] if p == CT else v,
                                             ACT.Silu, bias=cvp[:, 2, m:m + 1], scale=cvp[:, 1, m:m + 1]).then_inc(cv_out, 1)
                    return
                act.wait_ge(cv_var, p + 1)
                src = ps[:, 6:8, :] if p < CT else ps[:, 6, 0:w]
                dst = cns[:, :].rearrange("p (a b) -> p a b", a=2) if p < CT else cns[:, 0:w]
                ac.step(nc.scalar.activation(dst, src, ACT.Ln, bias=eps[:, :]))
                nc.scalar.activation(cns[:, 0:w], cns[:, 0:w], ACT.Exp, scale=-0.5).then_inc(cv_r, 1)

            for j in range(QT + 1):
                if j < QT - 1:
                    split_hi(Job(0, J_QKV + j + 1))
                if j == 0:
                    taps(2 * CT - 2 + PR)
                if j == QT - 1:
                    ac.step(nc.scalar.activation(rn[:, :, :], rn[:, :, :], ACT.Ln, bias=eps[:, :], scale=float(HD)))
                    nc.scalar.activation(rn[:, :, :], rn[:, :, :], ACT.Exp, scale=-0.5).then_inc(n_r, 1)
                if 2 <= j < 2 * CT + 4:
                    channel_norm(j - 2)
                if 2 <= j < 2 * PR + 2:
                    act.wait_ge(n_mm, j - 1)
                    c = 2 * (j - 2)
                    nc.scalar.activation(rn[0:NS, NT, c:c + 2], ps[0:NS, 7, NT * 2 * H + c:NT * 2 * H + c + 2], ACT.Copy)
                    nc.scalar.activation(rn[:, 0:NT, c:c + 2], ps[:, 7, 0:NT * 2 * H].rearrange("p (t h) -> p t h", h=2 * H)[:, :, c:c + 2],
                                         ACT.Copy).then_inc(n_cp, 1)
                if j == 0:
                    continue
                c = j - 1
                act.wait_ge(y_done, c + 1)
                nc.scalar.activation(qkvT[:, c, :], (t2, t3)[c % 2][:, :], ACT.Silu).then_inc(silu_done, 1)
                if c < 2 * PR:
                    act.wait_ge(silu_done, c + 1)
                    wait(act, n_mm, (0, 1, 2, 0, 4, 0, 5, 6)[c])
                    if c == 0:
                        act.wait_ge(cv_acc, 3)
                    nc.scalar.activation(squares(c)[:, :], qkvT[:, c, :], ACT.Square).then_inc(n_sq, 1)
                if 2 <= j < 2 * CT + 4 and j % 2:
                    channel_norm(j - 2, out=True)
                if 2 * CT - 2 + PR + j < len(PPLAN):
                    taps(2 * CT - 2 + PR + j)
            def decays(t, g):
                n, _ = tile_tokens(t)
                act.wait_ge(d_mm, 2 * t + g + 1)
                wait(act, g_lq, t - 1)
                for b in range(n // C):
                    r = slice(b * C, (b + 1) * C)
                    nc.scalar.activation(Dm[t % 2][r, 4 * g:4 * g + 4, :], ps[r, 7, :].rearrange("p (s c) -> p s c", c=P)[:, :, r],
                                         ACT.Exp).then_inc(d_exp, 1)

            def back(t):
                n, _ = tile_tokens(t)
                wait(act, g_aq, t)
                outs = (KTl[:, :, 0:n], RR[:, :, 0, 0:n], RR[:, :, 1, 0:n], QdT[:, t, :, 0:n] if t < NT else WQ[:, :, 1, :])
                for k in range(4):
                    act.wait_ge(g_bt, 4 * t + k + 1)
                    nc.scalar.activation(outs[k], ps[:, 3 + k, :].rearrange("p (q t) -> p q t", q=PR)[:, :, 0:n],
                                         ACT.Copy).then_inc(g_ev, 1)

            def o_banks(t):
                return ps[:, 4 - 4 * (t % 2):6 - 4 * (t % 2), 0:PR * HD] if t < NT else ps[0:NS, 4:5, 0:2 * PR * HD]

            def gate_square(t):
                n, _ = tile_tokens(t)
                act.wait_ge(o_mm, t + 1)
                nc.scalar.activation(sqt[0:n, 0:DW].rearrange("p (a b) -> p a b", a=1 if t == NT else 2), o_banks(t), ACT.Square).then_inc(o_sq, 1)

            def gate_rms(t):
                n, _ = tile_tokens(t)
                act.wait_ge(o_ss, t + 1)
                ac.step(nc.scalar.activation(ss[0:n, 0:H], ss[0:n, 0:H], ACT.Ln, bias=eps[0:n, :], scale=1.0 / HD))
                nc.scalar.activation(ss[0:n, 0:H], ss[0:n, 0:H], ACT.Exp, scale=-0.5).then_inc(o_r, 1)

            def inverse_times(t, w):
                act.wait_ge(uw_mm, 2 * t + w + 1)
                if w == 0:
                    nc.scalar.activation(Vb[:, t, :], ps[:, 7, :], ACT.Copy).then_inc(uw_ev, 1)
                else:
                    nc.scalar.activation(WT[:, t % 2, :, :], ps[:, 7, :].rearrange("p (q t) -> p q t", q=PR), ACT.Copy).then_inc(uw_ev, 1)

            decays(0, 0)
            decays(0, 1)
            for g in range(3):
                act.wait_ge(hist_tr, 3 + g)
                nc.scalar.activation(qrow[:, g * 512:(g + 1) * 512], ps[0:QH + DB * QH, 3 + g, :], ACT.Copy).then_inc(hist_cp, 1)

            for t in range(NT + 1):
                back(t)
                if t < NT:
                    decays(t + 1, 0)
                    decays(t + 1, 1)
            act.wait_ge(sp_mm, 1)
            nc.scalar.activation(NTs[:, :, :], ps[0:NS, 0, 0:H * C].rearrange("p (s c) -> p s c", c=C), ACT.Copy).then_inc(sp_act, 1)
            act.wait_ge(sp_mm, 4)
            nc.scalar.activation(dV[:, :], ps[0:NS, 0, :], ACT.Copy).then_inc(sp_act, 1)
            nc.scalar.activation(WQ[:, :, 0, :], ps[:, 1, :].rearrange("p (q t) -> p q t", q=PR)[:, :, 0:NS], ACT.Copy).then_inc(sp_act, 1)
            act.wait_ge(sp_mm, 5)
            nc.scalar.activation(WSt[:, :, :, :], ps[:, 2, 0:PR * 2 * NS].rearrange("p (q w t) -> p q w t", q=PR, w=2), ACT.Copy).then_inc(sp_act, 1)
            act.wait_ge(tb0, 2)
            for t in range(NT):
                load_inverses(act, t, range(CPT // 2, CPT))
            act.wait_ge(st_h, 16 * (4 + DB))
            for w in range(2):
                inverse_times(0, w)
            for t in range(NT):
                if t:
                    gate_square(t - 1)
                if t < NT - 1:
                    inverse_times(t + 1, 0)
                if t:
                    gate_rms(t - 1)
                if t < NT - 1:
                    inverse_times(t + 1, 1)
            split_hi(Job(0, J_OUT))

            def operand_hi(k):
                src = zs[:, k, :] if k < PR else gl[:, k - PR, 0:TOK]
                nc.scalar.activation(op[0][:, k, :], src, ACT.Copy).then_inc(op_hi, 1)

            gate_square(NT - 1)
            act.wait_ge(cv_out, 2 * CT)
            operand_hi(ORDER[0])
            gate_rms(NT - 1)
            gate_square(NT)
            operand_hi(ORDER[1])
            gate_rms(NT)
            act.wait_ge(st_p, 32)
            operand_hi(ORDER[2])
            operand_hi(ORDER[3])
            act.wait_ge(o_g, NT + 1)
            for k in ORDER[4:]:
                operand_hi(k)

            def norm_tail(phase, i, m, final, value):
                act.wait_ge(final, value)
                if m == 0 and phase == 1:
                    act.wait_ge(u_lo, FQ * KT)
                if m == 1 and phase == 1:
                    act.wait_ge(u_sq, FQ * KT)
                if i > 1:
                    act.wait_ge(ss_done, phase * (KT - 1) + i - 1)
                nc.scalar.activation((t2 if i else t3)[:, :], xT[:, m, :], ACT.Square).then_inc(sq_done, 1)
                if phase < 2:
                    nc.scalar.activation(hh[0][:, m, :], xT[:, m, :], ACT.Copy, scale=gains[:, phase + 1, m:m + 1]).then_inc(h_hi, 1)

            def stats(n):
                for c in range(NCH):
                    act.wait_ge(st_mm, 3 * n + c + 1)
                    nc.scalar.activation(rsb[:, c * CW:(c + 1) * CW], ps[:, 6 + c % 2, 0:CW], ACT.Ln, bias=eps[:, :],
                                         scale=1.0 / D).then_inc(st_ln, 1)
                act.wait_ge(st_ln, 3 * n + 3)
                nc.scalar.activation(rsb[:, :], rsb[:, :], ACT.Exp, scale=-0.5).then_inc(rs_done, 1)

            for m in range(KT):
                split_hi(Job(0, J_OUT + m + 1))
                norm_tail(0, m, ORDER[m], pf, J_OUT + m + 1)
            for q in range(FQ):
                up, down = J_MLP + 2 * KT * q, J_MLP + 2 * KT * q + KT

                def hidden(job, j, q=q):
                    n = q * KT + j
                    split_hi(job.next())
                    if q == 0 and isinstance(j, int) and j == 0:
                        stats(0)
                    wait(act, mm, job.num(1))
                    if isinstance(j, int) and j == 0:
                        wait(act, pf, job.num())
                    wait(act, t_done, n)
                    nc.scalar.activation(tri3(t1[:, :]), acc(job.slot), ACT.Relu).then_inc(pf, 1)
                    wait(act, t_done, n + 1)
                    nc.scalar.activation(pick(uu[0], j), t2[:, :], ACT.Square).then_inc(u_hi, 1)
                jobs(act, up, KT, hidden)
                if q < FQ - 1:
                    jobs(act, down, KT, lambda job, j: split_hi(job.next()))
                else:
                    for m in range(KT):
                        split_hi(Job(0, down + m + 1))
                        norm_tail(1, m, m, pf, down + m + 1)
            act.wait_ge(mm, J_GATE)
            act.wait_ge(p_cp, 3 * PK)
            for k in range(PK):
                nc.scalar.activation(pp[0][:, k, :], pT[k][:, :], ACT.Copy).then_inc(p_hi, 1)
            for m in range(KT):
                split_hi(Job(0, J_GATE + 2 * m + 1), kts=PK)
                if m == 0:
                    stats(1)
                if m < KT - 1:
                    split_hi(Job(0, J_GATE + 2 * m + 2))
                act.wait_ge(pf, J_GATE + 2 * m + 1)
                wait(act, x_new, m)
                nc.scalar.activation(gt[:, :], t1[:, :], ACT.Sigmoid).then_inc(gt_done, 1)
                norm_tail(2, m, m, x_new, m + 1)
            act.wait_ge(y_mm, 1)
            nc.scalar.activation(ltok[0:NS, NT:NT + 1], ps[0:NS, 6, NT:NT + 1], ACT.Ln, bias=eps[0:NS, :], scale=1.0 / D)
            ac.step(nc.scalar.activation(ltok[:, 0:NT], ps[:, 6, 0:NT], ACT.Ln, bias=eps[:, :], scale=1.0 / D))
            ac.step(nc.scalar.activation(rtok[:, 0:NT + 1], ltok[:, 0:NT + 1], ACT.Exp, scale=-0.5))
            for i in range(NT + 1):
                n, _ = tile_tokens(i)
                act.wait_ge(y_tr, i + 1)
                nc.scalar.activation(yrow[0:n, i, :].rearrange("p (a b) -> p a b", a=2), ps[0:n, 2 * (i % 3):2 * (i % 3) + 2, :],
                                     ACT.Copy, scale=rtok[0:n, i:i + 1]).then_inc(y_cp, 1)

        @block.tensor
        def _(pe):
            def multiply(job, rhs, kts=KT, m=P, before=None, order=range(KT)):
                wait(pe, w_lod, job.num(1))
                wait(pe, pf, job.num(-1))
                hi, lo = w_hi[job.slot], w_lo[job.slot]
                for i, k in enumerate(order[:kts]):
                    if before:
                        before(i)
                    for n, (w, x) in enumerate(((hi, rhs[0]), (hi, rhs[1]), (lo, rhs[0]))):
                        for c in range(NCH):
                            last = nc.tensor.matmul(ps[0:m, 3 * job.slot + c, 0:CW], w[:, k, 0:m],
                                                    x[:, k, c * CW:(c + 1) * CW], start=(i == 0 and n == 0),
                                                    stop=(i == kts - 1 and n == 2))
                last.then_inc(mm, 1)

            pe.wait_ge(ld_i, 16)
            for i in range(NT + 1):
                n, _ = tile_tokens(i)
                pe.wait_ge(ld_x[i], 16)
                for g in range(2):
                    wait(pe, (x_cp, x_cp2)[g], i - 2)
                    for k in range(4):
                        last = nc.tensor.transpose(ps[:, (2 * i + g) % 6, k * P:k * P + n],
                                                   xin[0:n, i, (4 * g + k) * P:(4 * g + k + 1) * P], ident[0:n, 0:n])
                    last.then_inc(x_tr, 1)
            pe.wait_ge(ld_h, 16 * 16)
            for rows, n, col in ((vrow, NV, 0), (srow, SC * QT, 64), (drow, DWC * CT, 128)):
                last = nc.tensor.transpose(ps[:, 7, col:col + n], rows[:, :], ident[0:n, 0:n])
            last.then_inc(vec_tr, 1)
            nq = DB * QH
            for m in range(QT):
                last = nc.tensor.transpose(ps[:, 6, m * nq:(m + 1) * nq], hq[:, m * P:(m + 1) * P], ident[0:nq, 0:nq])
            last.then_inc(hs_tr, 1)
            nh = 4 * HIST
            for g in range(2):
                if g:
                    pe.wait_ge(hs_cp, 1)
                else:
                    pe.wait_ge(vec_cp, 3)
                for m in range(CT):
                    last = nc.tensor.transpose(ps[:, 7 - g, m * nh:(m + 1) * nh], hc[:, g, m * P:(m + 1) * P], ident[0:nh, 0:nh])
                last.then_inc(hs_tr, 1)
            pe.wait_ge(x_cp, NT + 1)
            pe.wait_ge(x_cp2, NT + 1)
            pe.wait_ge(ld_c, 16 * (len(CONSTS) - 1))
            for i in range(NT + 1):
                n, _ = tile_tokens(i)
                pe.wait_ge(x_dg, i + 1)
                bank, col = 3 + i // 4, (i % 4) * P
                last = nc.tensor.matmul(ps[:, bank, col:col + n], ones[0:n, :], dg(i)[0:n, 0:n], start=True, stop=True)
                if i in (3, 7, 8):
                    last.then_inc(x_bc, 1)

            def mixer_rows(k):
                pe.wait_ge(h_lo, k + 1)

            multiply(Job(0, J_AB), hm, m=2 * H, before=mixer_rows)
            pe.wait_ge(x_rs, 3)
            for j in range(2 * CT):
                multiply(Job(0, J_GLU + j), hm)
                if j == 0:
                    pe.wait_ge(pf, J_AB + 1)
                    for i in range(NT + 1):
                        n, t0 = tile_tokens(i)
                        last = nc.tensor.transpose(ps[0:n, 7, i * 2 * H:(i + 1) * 2 * H], t3[0:2 * H, t0:t0 + n], ident[0:2 * H, 0:2 * H])
                    last.then_inc(ab_tr, 1)
                if j == 2:
                    pe.wait_ge(ab_cp, 1)
                    pe.wait_ge(gs_dve, 9)
                    nt = NT * H
                    gf = gg[:, :, :].rearrange("p t h -> p (t h)")
                    nc.tensor.matmul(ps[:, 7, G_IN:G_IN + nt], consts["uinc"][:, :], gf[:, 0:nt], start=True, stop=True)
                    nc.tensor.matmul(ps[:, 7, G_IN + nt:G_TO], consts["uinc4"][:, :], gf[:, nt:nt + H], start=True, stop=True)
                    nc.tensor.matmul(ps[:, 7, G_TO:G_TO + nt], consts["sgt"][:, :], gf[:, 0:nt], start=True, stop=True)
                    nc.tensor.matmul(ps[:, 7, G_TO + nt:G_ALL], consts["sgt4"][:, :], gf[:, nt:nt + H], start=True, stop=True)
                    nc.tensor.matmul(ps[:, 7, G_ALL:G_SEQ], ones[:, :], gr[:, :, :, :].rearrange("p t b h -> p (t b h)"), start=True, stop=True)
                    nc.tensor.matmul(ps[:, 7, G_SEQ:G_SEQ + DB * H], ones[0:NS, :], grs[:, :, :].rearrange("p b h -> p (b h)"), start=True, stop=True)\
                      .then_inc(gs_mm, 1)
            for j in range(PR):
                multiply(Job(0, J_Z + j), hm)
                if j == 0:
                    pe.wait_ge(pf, J_Z)
                    pe.wait_ge(gs_act, 10)
                    for m in range(CT):
                        last = nc.tensor.transpose(ps[0:HIST, 6, m * P:(m + 1) * P], gl[:, m, SEQ - HIST:SEQ], ident[:, :])
                    last.then_inc(hist_tr, 1)
                    for m in range(CT):
                        last = nc.tensor.transpose(ps[0:NS, 7, m * P:(m + 1) * P], gl[:, m, SEQ:TOK], ident[:, :])
                    last.then_inc(hist_tr, 1)

            def channel_norm(n):
                p, var = divmod(n, 2)
                if var:
                    pe.wait_ge(cv_sq, p + 1)
                else:
                    pe.wait_ge(cv_acc, min(p + 1, CT))
                    if p:
                        pe.wait_ge(cv_r, p)
                    else:
                        pe.wait_ge(hist_cp, 2)
                wait(pe, n_cp, min(n, 2 * PR))
                if p == CT:
                    src = cns[:, 0:CT * NS] if var else gds[:, :, :].rearrange("p m t -> p (m t)")
                    last = nc.tensor.matmul(ps[:, 6, 0:CT * NS], consts["bd64"][:, :], src, start=True, stop=True)
                else:
                    for c in range(2):
                        last = nc.tensor.matmul(ps[:, 6 + c, :], consts["bd64"][:, :], (cns if var else accv[p])[:, c * 512:(c + 1) * 512],
                                                start=True, stop=True)
                last.then_inc(cv_var if var else cv_mm, 1)

            def head_squares(j):
                pe.wait_ge(n_sq, j + 1)
                p, var = divmod(j, 2)
                pe.wait_ge(cv_r if var else cv_c, p + 1)
                for t in range(NT + 1):
                    n, t0 = tile_tokens(t)
                    c = t * 2 * H + 2 * j
                    last = nc.tensor.matmul(ps[0:n, 7, c:c + 2], squares(j)[:, t0:t0 + n], consts["bd64"][:, 0:P:HD], start=True, stop=True)
                last.then_inc(n_mm, 1)

            for j in range(QT):
                squares_beside = lambda k, j=j: head_squares(j - 2) if k == KT - 1 and 2 <= j < 2 * PR + 2 else None
                multiply(Job(0, J_QKV + j), hm, before=squares_beside)
                if 1 <= j < 2 * CT + 3:
                    channel_norm(j - 1)
            pe.wait_ge(cv_r, CT + 1)
            def decays(t, g):
                n, _ = tile_tokens(t)
                pe.wait_ge(d_ug, t + 1)
                wait(pe, d_exp, exps(t) + g * (n // C))
                nc.tensor.matmul(ps[0:n, 7, :].rearrange("p (s c) -> p s c", c=P)[:, :, 0:n],
                                 consts["sgt" if t < NT else "sgt4"][0:n, 0:n], ug[0:n, 4 * g:4 * g + 4, 0:n],
                                 start=True, stop=True).then_inc(d_mm, 1)

            def tokens(t):
                n, t0 = tile_tokens(t)
                wait(pe, g_big, 7 * t)
                for g in range(3):
                    if t == 0:
                        pe.wait_ge(silu_done, PR * (g + 1))
                    for k in range(4):
                        last = nc.tensor.transpose(ps[0:n, g, k * P:(k + 1) * P], qkvT[:, 4 * g + k, t0:t0 + n], ident[:, :])
                    if g:
                        last.then_inc((g_qk, g_tok)[g - 1], 1)

            def back(t):
                n, _ = tile_tokens(t)
                wait(pe, g_lq, t)
                for k in range(4):
                    pe.wait_ge(g_big, 7 * t + k + 1)
                    for q in range(PR):
                        last = nc.tensor.transpose(ps[:, 3 + k, q * P:q * P + n], tk[k][0:n, q * P:(q + 1) * P], ident[0:n, 0:n])
                    last.then_inc(g_bt, 1)

            def pairs(t):
                n, _ = tile_tokens(t)
                pe.wait_ge(g_ev, 4 * t + 4)
                for s in range(H):
                    par, q = divmod(s, PR)
                    rows = slice(par * HD, (par + 1) * HD)
                    last = nc.tensor.matmul(ps[0:n, 3 + s // 2, (s % 2) * 256:(s % 2) * 256 + 256].rearrange("p (w c) -> p w c", w=2)[:, :, 0:n],
                                            KTl[rows, q, 0:n], RR[rows, q, :, 0:n], start=True, stop=True)
                last.then_inc(g_aq, 1)

            def transpose_out(t):
                n, _ = tile_tokens(t)
                pe.wait_ge(o_n, t + 1)
                for q in range(PR):
                    last = nc.tensor.transpose(ps[:, 7, q * P:q * P + n], onr[0:n, q * P:(q + 1) * P], ident[0:n, 0:n])
                last.then_inc(o_tr, 1)

            def inverse_times(t, w):
                if w:
                    pe.wait_ge(uw_ev, 2 * t + 1)
                else:
                    pe.wait_ge(tt_ld[t], 16 * CPT)
                    wait(pe, o_g, t - 2)
                    wait(pe, sp_up, min(t - 2, PR))
                for h in range(H):
                    q, par = h // 2, h % 2
                    T = Tbd[:, t, par * PR + q, :]
                    if w == 0:
                        last = nc.tensor.matmul(ps[:, 7, h * HD:(h + 1) * HD], T, Vb[:, t, h * HD:(h + 1) * HD], start=True, stop=True)
                    else:
                        last = nc.tensor.matmul(ps[par * HD:(par + 1) * HD, 7, q * P:(q + 1) * P], Kbe[:, t, h * HD:(h + 1) * HD], T,
                                                start=True, stop=True)
                last.then_inc(uw_mm, 1)

            def chunk(t, b):
                n, ob = t * CPT + b, 4 - 4 * (t % 2)
                r = slice(b * C, (b + 1) * C)
                if b == 0:
                    pe.wait_ge(uw_ev, 2 * t + 2)
                def state_product(par, bank, src, first):
                    rows = slice(par * HD, (par + 1) * HD)
                    for q in range(PR):
                        last = nc.tensor.matmul(ps[r, bank + par, q * HD:(q + 1) * HD], src[rows, q, r], S[rows, q, :],
                                                start=(first or q == 0), stop=first, skip_group_check=True)
                    return last

                for par in range(2):
                    pe.wait_ge(s_up[par], n + 1)
                    state_product(par, 2, WT[:, t % 2, :, :], True).then_inc(ws_mm[par], 1)
                if b == 0 and t >= 2:
                    pe.wait_ge(o_n, t - 1)
                for par in range(2):
                    state_product(par, ob, QdT[:, t, :, :], False)
                for par in range(2):
                    pe.wait_ge(vn_d[par], n + 1)
                    for q in range(PR):
                        h = 2 * q + par
                        last = nc.tensor.matmul(ps[par * HD:(par + 1) * HD, 6, q * HD:(q + 1) * HD], Kd[r, t, h * HD:(h + 1) * HD],
                                                Vn[r, h * HD:(h + 1) * HD], start=True, stop=True, skip_group_check=True)
                    last.then_inc(ds_mm[par], 1)
                for par in range(2):
                    for q in range(PR):
                        h = 2 * q + par
                        last = nc.tensor.matmul(ps[r, ob + par, q * HD:(q + 1) * HD], LQ[r, t, par * PR + q, 1, :], Vn[r, h * HD:(h + 1) * HD],
                                                start=False, stop=True, skip_group_check=True)
                if b == CPT - 1:
                    last.then_inc(o_mm, 1)

            decays(0, 0)
            pe.wait_ge(pf, J_OUT)
            tokens(0)
            decays(0, 1)
            pe.wait_ge(y_done, QT)
            for g in range(3):
                for k in range(4):
                    last = nc.tensor.transpose(ps[0:QH + DB * QH, 3 + g, k * P:(k + 1) * P], tail[:, 4 * g + k, :], ident[:, :])
                last.then_inc(hist_tr, 1)
            pe.wait_ge(hist_cp, 5)
            for t in range(NT + 1):
                back(t)
                if t < NT:
                    tokens(t + 1)
                    decays(t + 1, 0)
                pairs(t)
                if t < NT:
                    decays(t + 1, 1)

            pe.wait_ge(sp_dve, 1)
            for s in range(H):
                last = nc.tensor.transpose(ps[0:NS, 0, s * C:(s + 1) * C], Ns[:, s, :], ident[0:NS, 0:NS])
            last.then_inc(sp_mm, 1)
            pe.wait_ge(sp_act, 1)
            for s in range(H):
                last = nc.tensor.matmul(ps[0:NS, 1, s * C:(s + 1) * C], NTs[:, s, :], Ns[:, s, :], start=True, stop=True)
            last.then_inc(sp_mm, 1)
            pe.wait_ge(sp_dve, 2)
            for s in range(H):
                last = nc.tensor.matmul(ps[0:NS, 2, s * C:(s + 1) * C], NTs[:, s, :], Ms[:, s, :], start=True, stop=True)
            last.then_inc(sp_mm, 1)
            pe.wait_ge(sp_dve, 3)
            for h in range(H):
                s = (h % 2) * PR + h // 2
                nc.tensor.matmul(ps[0:NS, 0, h * HD:(h + 1) * HD], Ts[:, s, :], dV[:, h * HD:(h + 1) * HD], start=True, stop=True)
            for h in range(H):
                s, par, q = (h % 2) * PR + h // 2, h % 2, h // 2
                last = nc.tensor.matmul(ps[par * HD:(par + 1) * HD, 1, q * P:q * P + NS], dKbe[:, h * HD:(h + 1) * HD],
                                        Ts[:, s, :], start=True, stop=True)
            last.then_inc(sp_mm, 1)
            pe.wait_ge(sp_act, 3)
            pe.wait_ge(ld_s, 16 * 2 * PR)
            for par in range(2):
                rows = slice(par * HD, (par + 1) * HD)
                for q in range(PR):
                    for b in range(DB):
                        cols = slice(b * DS, (b + 1) * DS)
                        last = nc.tensor.matmul(ps[rows, 2, q * 2 * NS:(q + 1) * 2 * NS].rearrange("p (w t) -> p w t", w=2)[:, :, cols],
                                                S0[rows, q, b, :], WQ[rows, q, :, cols], start=True, stop=True)
            last.then_inc(sp_mm, 1)
            pe.wait_ge(sp_act, 4)
            for q in range(PR):
                last = nc.tensor.transpose(ps[0:NS, 3, q * P:(q + 1) * P], WSt[:, q, 0, :], ident[:, :])
            last.then_inc(sp_mm, 1)

            def sample_state(q):
                if q == 0:
                    pe.wait_ge(sp_vm, 1)
                pe.wait_ge(o_g, q + 1)
                for par in range(2):
                    h = 2 * q + par
                    last = nc.tensor.matmul(ps[par * HD:(par + 1) * HD, 7, :], dKd[:, h * HD:(h + 1) * HD],
                                            VnM[:, h, :, :].rearrange("p b e -> p (b e)"), start=True, stop=True)
                last.then_inc(sp_ds, 1)

            for w in range(2):
                inverse_times(0, w)
            for t in range(NT):
                for b in range(CPT):
                    chunk(t, b)
                    if b < 2 and t < NT - 1:
                        inverse_times(t + 1, b)
                    if b == 2 and t:
                        if t < NT - 1:
                            pe.wait_ge(uw_ev, 2 * t + 4)
                        transpose_out(t - 1)
                    if b == 3 and 1 <= t <= PR:
                        sample_state(t - 1)
            pe.wait_ge(o_n, NT - 1)
            for q in range(PR):
                nc.tensor.matmul(ps[0:NS, 4, q * P:(q + 1) * P], WSt[:, q, 1, :], ident[:, :], start=(q == 0), stop=False, skip_group_check=True)
            for h in range(H):
                s = (h % 2) * PR + h // 2
                last = nc.tensor.matmul(ps[0:NS, 4, h * HD:(h + 1) * HD], LQd[:, s, 1, :], dV[:, h * HD:(h + 1) * HD],
                                        start=False, stop=True, skip_group_check=True)
            last.then_inc(o_mm, 1)
            transpose_out(NT - 1)
            pe.wait_ge(o_g, NT)
            transpose_out(NT)

            pe.wait_ge(o_n, NT + 1)
            for i in range(KT):
                multiply(Job(0, J_OUT + i), op, order=ORDER, before=(lambda k: pe.wait_ge(op_lo, k + 1)) if i == 0 else None)

            def stat(n):
                pe.wait_ge(ss_done, (n + 1) * (KT - 1))
                for c in range(NCH):
                    if c == 2:
                        pe.wait_ge(st_ln, 3 * n + 1)
                    nc.tensor.matmul(ps[:, 6 + c % 2, 0:CW], ones[:, :], t3[:, c * CW:(c + 1) * CW], start=True, stop=True).then_inc(st_mm, 1)

            for q in range(FQ):
                up, down = J_MLP + 2 * KT * q, J_MLP + 2 * KT * q + KT

                def hidden(job, j, q=q):
                    first = q == 0 and isinstance(j, int) and j == 0
                    multiply(job, hh, before=(lambda k: pe.wait_ge(h_lo, KT + k + 1)) if first else None, order=ORDER if first else range(KT))
                    if first:
                        stat(0)
                jobs(pe, up, KT, hidden)

                def out(job, j, q=q):
                    first = isinstance(j, int) and j == 0
                    multiply(job, uu, before=(lambda k: pe.wait_ge(u_lo, q * KT + k + 1)) if first else None)
                if q < FQ - 1:
                    jobs(pe, down, KT, out)
                else:
                    pe.wait_ge(ld_p, 16 * (NT + 1))
                    for m in range(KT):
                        out(Job(0, down + m), m)
                        if m < 3 * PK:
                            k, g = divmod(m, 3)
                            if m >= 2:
                                pe.wait_ge(p_cp, m - 1)
                            else:
                                pe.wait_ge(st_ln, 3)
                            for i in (range(4 * g, 4 * g + 4) if g < 2 else [NT]):
                                n, t0 = tile_tokens(i)
                                last = nc.tensor.transpose(ps[:, 6 + m % 2, (i % 4) * P:(i % 4) * P + n], prow[0:n, i, k * P:(k + 1) * P], ident[0:n, 0:n])
                            last.then_inc(p_tr, 1)

            def gate_rows(k):
                pe.wait_ge(h_lo, 2 * KT + k + 1)
                if k == KT // 2:
                    pe.wait_ge(p_cp, 3 * PK)
                    stat(1)

            multiply(Job(0, J_GATE), hh, before=gate_rows)
            for m in range(KT):
                if m:
                    multiply(Job(0, J_GATE + 2 * m), hh)
                multiply(Job(0, J_GATE + 2 * m + 1), pp, kts=PK, before=(lambda k: pe.wait_ge(p_lo, k + 1)) if m == 0 else None)
            pe.wait_ge(ss_done, 3 * (KT - 1))
            for i in range(NT + 1):
                n, t0 = tile_tokens(i)
                last = nc.tensor.matmul(ps[0:n, 6, i:i + 1], t3[:, t0:t0 + n], ones[:, 0:1], start=True, stop=True)
            last.then_inc(y_mm, 1)
            pe.wait_ge(pf, J_END)
            pe.wait_ge(xg_done, KT)
            for i in range(NT + 1):
                n, t0 = tile_tokens(i)
                if i >= 3:
                    pe.wait_ge(y_cp, i - 2)
                for m in range(KT):
                    last = nc.tensor.transpose(ps[0:n, 2 * (i % 3) + m // 4, (m % 4) * P:(m % 4 + 1) * P], xT[:, m, t0:t0 + n], ident[:, :])
                last.then_inc(y_tr, 1)

        @block.vector
        def _(dve):
            dc = Chain(dve, dch)
            step = dc.step

            def split_lo(job, kts=KT, cols=P):
                wait(dve, w_hid, job.num(1))
                nc.vector.tensor_tensor(w_lo[job.slot][:, 0:kts, 0:cols], w_raw[job.slot][:, 0:kts, 0:cols],
                                        w_hi[job.slot][:, 0:kts, 0:cols].bitcast(F32), ALU.subtract).then_inc(w_lod, 1)

            nc.vector.memset(rtok[:, :], 1.0).then_inc(init, 1)
            nc.vector.memset(eps[:, :], EPS).then_inc(init, 1)
            nc.vector.memset(ab[:, :, :], 0.0).then_inc(init, 1)
            nc.vector.memset(rn[:, :, :], 1.0).then_inc(init, 1)
            for i in range(NT + 1):
                n, t0 = tile_tokens(i)
                dve.wait_ge(x_tr, 2 * i + 2)
                nc.vector.tensor_copy(xT0[:, 4:8, t0:t0 + n], ps[:, (2 * i + 1) % 6, :].rearrange("p (k t) -> p k t", k=4)[:, :, 0:n]).then_inc(x_cp2, 1)
            dve.wait_ge(vec_tr, 1)
            nc.vector.tensor_copy(vec[:, :], ps[:, 7, 0:NV]).then_inc(vec_cp, 1)
            nc.vector.tensor_copy(wsh[:, :, :].rearrange("p j m -> p (j m)"), ps[:, 7, 64:64 + SC * QT]).then_inc(vec_cp, 1)
            nc.vector.tensor_copy(wdw[:, :, :].rearrange("p j m -> p (j m)"), ps[:, 7, 128:128 + DWC * CT]).then_inc(vec_cp, 1)
            dve.wait_ge(hs_tr, 1)
            nc.vector.tensor_copy(raws[:, :, :, 0:QH], ps[:, 6, 0:QT * DB * QH].rearrange("p (m b r) -> p m b r", m=QT, b=DB)).then_inc(hs_cp, 1)
            for g in range(2):
                dve.wait_ge(hs_tr, 2 + g)
                for m in range(CT):
                    last = nc.vector.tensor_copy(gls[:, m, 4 * g:4 * g + 4, 0:HIST],
                                                 ps[:, 7 - g, m * 4 * HIST:(m + 1) * 4 * HIST].rearrange("p (b r) -> p b r", b=4))
                last.then_inc(hs_cp, 1)
            dve.wait_ge(x_ln, 1)
            for i in range(NT + 1):
                nc.vector.tensor_scalar(dg(i), ident[:, :], rtok[:, i:i + 1], None, ALU.mult).then_inc(x_dg, 1)
            split_lo(Job(0, J_AB), cols=2 * H)
            dve.wait_ge(vec_cp, 3)
            for k in range(KT):
                dve.wait_ge(h_hi, k + 1)
                nc.vector.scalar_tensor_tensor(out=hm[1][:, k, :], in0=xT0[:, k, :], scalar=gains[:, 0, k:k + 1],
                                               in1=hm[0][:, k, :].bitcast(F32), op0=ALU.mult, op1=ALU.subtract).then_inc(h_lo, 1)
            split_lo(Job(0, 1))
            dve.wait_ge(x_rs, 3)
            dve.wait_ge(mm, J_AB + 1)
            dve.wait_ge(x_sq, NT + 1)
            nc.vector.tensor_tensor(tri3(t3[0:2 * H, :]), acc(0, 2 * H), tri3(rsb[0:2 * H, :]), ALU.mult).then_inc(pf, 1)

            g_n = [0]

            def small(ins):
                ins.then_inc(gs_dve, 1)
                g_n[0] += 1
                dve.wait_ge(gs_dve, g_n[0])

            mark = [0, 0]

            def taps(s):
                for n in range(sum(VPLAN[:s]), sum(VPLAN[:s + 1])):
                    p, k, s0 = VTAPS[n]
                    for u in range(2):
                        lo, hi = max(s0, u * SEQ // 2), (u + 1) * SEQ // 2
                        dst = accv[p][:, lo:hi]
                        w = wdw[:, HIST - s0, p:p + 1]
                        if k:
                            dve.wait_ge(dch, mark[u])
                            ins = nc.vector.scalar_tensor_tensor(out=dst, in0=gl[:, p, lo - s0:hi - s0], scalar=w, in1=dst, op0=ALU.mult, op1=ALU.add)
                        else:
                            ins = nc.vector.tensor_scalar(dst, gl[:, p, lo:hi], w, cvp[:, 0, p:p + 1], ALU.mult, ALU.add)
                        mark[u] = dc.mark(ins)
                    if k == DWC - PCOUNT[p] - 1:
                        finish(p)

            def finish(p):
                dve.wait_ge(dch, mark[1])
                dve.wait_ge(cv_add, sum(PCOUNT[:p + 1]))
                nc.vector.tensor_tensor(accv[p][:, 0:SEQ], accv[p][:, 0:SEQ], accp[p % 2][:, 0:SEQ], ALU.add).then_inc(cv_acc, 1)

            def decode_taps(p):
                for t in range(DS):
                    pr = t3[:, t * DB * DWC:(t + 1) * DB * DWC].rearrange("p (b j) -> p b j", b=DB)
                    last = nc.vector.tensor_tensor(pr, gls[:, p, :, t:t + DWC], bc(wdw[:, :, p], 1, DB), ALU.mult)
                step(last)
                step(nc.vector.tensor_reduce(gds[:, p, :].rearrange("p (b t) -> p t b", b=DB),
                                             t3[:, 0:NS * DWC].rearrange("p (t b j) -> p t b j", t=DS, b=DB), AX, ALU.add))
                step(nc.vector.tensor_scalar(gds[:, p, :], gds[:, p, :], cvp[:, 0, p:p + 1], None, ALU.add))

            def channel_norm(n):
                p, var = divmod(n, 2)
                if p < CT:
                    v = accv[p][:, 0:SEQ]
                    split, src, r = v.rearrange("p (a b) -> p a b", a=2), ps[:, 6:8, :], cns[:, :]
                else:
                    v = gds[:, :, :].rearrange("p m t -> p (m t)")
                    split, src, r = v, ps[:, 6, 0:CT * NS], cns[:, 0:CT * NS]
                if var:
                    dve.wait_ge(cv_r, p + 1)
                    nc.vector.tensor_tensor(v, v, r, ALU.mult).then_inc(cv_n, 1)
                else:
                    dve.wait_ge(cv_mm, p + 1)
                    nc.vector.tensor_tensor(split, split, src, ALU.subtract).then_inc(cv_c, 1)

            dve.wait_ge(st_x, 16)
            for p in range(CT):
                jb, ja = Job(0, J_GLU + 2 * p), Job(0, J_GLU + 2 * p + 1)
                split_lo(jb.next())
                if p == 0:
                    dve.wait_ge(ab_tr, 1)
                    nc.vector.tensor_copy(ab[:, 0:NT, :], ps[:, 7, 0:NT * 2 * H].rearrange("p (t h) -> p t h", h=2 * H))
                    nc.vector.tensor_copy(ab[0:NS, NT, :], ps[0:NS, 7, NT * 2 * H:(NT + 1) * 2 * H]).then_inc(ab_cp, 1)
                    dve.wait_ge(ab_cp, 1)
                    small(nc.vector.tensor_tensor(sm[0][:, :, :], ab[:, :, H:2 * H], bc(hp[:, 1, :], 1, NT + 1), ALU.add))
                    small(nc.vector.scalar_tensor_tensor(out=sm[1][:, :, :], in0=sm[0][:, :, :], scalar=-1.0, in1=sm[0][:, :, :],
                                                         op0=ALU.mult, op1=ALU.max))
                    small(nc.vector.tensor_scalar(sm[0][:, :, :], sm[0][:, :, :], 0.0, None, ALU.max))
                else:
                    taps(2 * p - 2)
                dve.wait_ge(mm, jb.num(1))
                if p:
                    dve.wait_ge(sg_done, p)
                nc.vector.tensor_tensor(tri3(t3[:, :]), acc(jb.slot), tri3(rsb[:, :]), ALU.mult).then_inc(pf, 1)
                split_lo(ja.next())
                if p:
                    taps(2 * p - 1)
                dve.wait_ge(mm, ja.num(1))
                dve.wait_ge(sgr_done, p + 1)
                nc.vector.tensor_tensor(tri3(gl[:, p, :]), acc(ja.slot), tri3(t2[:, :]), ALU.mult).then_inc(pf, 1)
                dve.wait_ge(pf, ja.num(1))
                nc.vector.tensor_copy(gls[:, p, :, HIST:], gl[:, p, SEQ:TOK].rearrange("p (b t) -> p b t", b=DB))
                if p == 0:
                    dve.wait_ge(gs_act, 4)
                    small(nc.vector.tensor_scalar(beta[:, :, :], beta[:, :, :], 1.0, None, ALU.add))
                    small(nc.vector.reciprocal(beta[:, :, :], beta[:, :, :]))
                    small(nc.vector.tensor_tensor(sm[2][:, :, :], sm[2][:, :, :], sm[0][:, :, :], ALU.add))
                    small(nc.vector.scalar_tensor_tensor(out=gg[:, :, :], in0=sm[2][:, :, :], scalar=-1.0, in1=bc(hp[:, 0, :], 1, NT + 1),
                                                         op0=ALU.mult, op1=ALU.mult))
                    small(nc.vector.tensor_tensor(gr[:, :, :, :], bc(gg[:, 0:NT, :], 2, CPT), bc(bc(consts["blk"][:, :], 1, NT), 3, H), ALU.mult))
                    small(nc.vector.tensor_tensor(grs[:, :, :], bc(gg[0:NS, NT, :], 1, DB), bc(consts["blk4"][0:NS, :], 2, H), ALU.mult))
            dve.wait_ge(sg_done, CT)
            for j in range(PR):
                job = Job(0, J_Z + j)
                split_lo(job.next())
                decode_taps(j)
                taps(2 * CT - 2 + j)
                dve.wait_ge(mm, job.num(1))
                if j >= 2:
                    dve.wait_ge(z_done, j - 1)
                nc.vector.tensor_tensor(tri3((t1, t2)[j % 2][:, :]), acc(job.slot), tri3(rsb[:, :]), ALU.mult).then_inc(pf, 1)

            for w in range(QT + 1):
                if w:
                    j, job = w - 1, Job(0, J_QKV + w - 1)
                    dve.wait_ge(mm, job.num(1))
                    if j:
                        dve.wait_ge(y_done, j)
                    else:
                        dve.wait_ge(z_done, PR)
                    nc.vector.tensor_tensor(tri3(t1[:, :]), acc(job.slot), tri3(rsb[:, :]), ALU.mult).then_inc(pf, 1)
                if 2 <= w < 2 * CT + 4 and w % 2 == 0:
                    channel_norm(w - 2)
                if 2 * CT - 2 + PR + w < len(VPLAN):
                    taps(2 * CT - 2 + PR + w)
                if w == 0:
                    continue
                dve.wait_ge(pf, job.num(1))
                nc.vector.tensor_copy(tail[:, j, 0:QH], t1[:, SEQ - QH:SEQ])
                step(nc.vector.tensor_copy(raws[:, j, :, QH:QH + DS], t1[:, SEQ:TOK].rearrange("p (b t) -> p b t", b=DB)))
                nc.vector.tensor_copy(tail[:, j, QH:].rearrange("p (b r) -> p b r", b=DB), raws[:, j, :, DS:DS + QH])
                y = (t2, t3)[j % 2]
                wait(dve, silu_done, j - 1)
                ys = y[:, SEQ:TOK].rearrange("p (b t) -> p b t", b=DB)
                nc.vector.tensor_scalar(ys, raws[:, j, :, 0:DS], wsh[:, 0, j:j + 1], None, ALU.mult)
                step(nc.vector.tensor_scalar(y[:, 0:SEQ], t1[:, 0:SEQ], wsh[:, SC - 1, j:j + 1], None, ALU.mult))
                for k in range(1, SC):
                    nc.vector.scalar_tensor_tensor(out=ys, in0=raws[:, j, :, k:k + DS], scalar=wsh[:, k, j:j + 1], in1=ys,
                                                   op0=ALU.mult, op1=ALU.add)
                    ins = nc.vector.scalar_tensor_tensor(out=y[:, k:SEQ], in0=t1[:, 0:SEQ - k], scalar=wsh[:, SC - 1 - k, j:j + 1],
                                                         in1=y[:, k:SEQ], op0=ALU.mult, op1=ALU.add)
                    if k < SC - 1:
                        step(ins)
                    else:
                        ins.then_inc(y_done, 1)
                if 2 <= w < 2 * CT + 4 and w % 2:
                    channel_norm(w - 2)

            dve.wait_ge(gs_act, 10)

            def heads(t):
                return t.rearrange("p (h e) -> p h e", e=HD)

            def scaled(t):
                n, _ = tile_tokens(t)
                dve.wait_ge(g_qk, t + 1)
                wait(dve, g_bt, 4 * t)
                if t == NT:
                    dve.wait_ge(st_h, 16 * (4 + DB))
                outs = (Kbe[:, t, :], Kd[:, t, :], Vb[:, t, :]) if t < NT else (dKbe, dKd, dV)
                for bank, out, f in ((1, tk[0], rn[0:n, t, H:2 * H]), (1, tk[1], scb[0:n, 0, t, :]), (0, tk[2], scb[0:n, 3, t, :]),
                                     (0, tk[3], scb[0:n, 4, t, :]), (1, outs[0], scb[0:n, 1, t, :]), (1, outs[1], scb[0:n, 2, t, :]),
                                     (2, outs[2], beta[0:n, t, :])):
                    if bank == 2:
                        dve.wait_ge(g_tok, t + 1)
                    nc.vector.tensor_tensor(heads(out[0:n, :]), heads(ps[0:n, bank, :]), bc(f, 2, HD), ALU.mult).then_inc(g_big, 1)

            def decayed(t):
                n, _ = tile_tokens(t)
                D_ = Dm[t % 2]
                dve.wait_ge(d_exp, exps(t) + 2 * (n // C))
                tr = consts["tri" if t < NT else "tri4"]
                nc.vector.tensor_tensor(D_[0:n, :, :], D_[0:n, :, :], bc(tr[0:n, :], 1, H), ALU.mult).then_inc(d_msk, 1)
                dve.wait_ge(d_msk, t + 1)
                dve.wait_ge(g_aq, t + 1)
                for b in range(n // C):
                    r = slice(b * C, (b + 1) * C)
                    last = nc.vector.tensor_tensor(LQ[r, t, :, :, :] if t < NT else LQd[:, :, :, :],
                                                   ps[r, 3:7, :].rearrange("p k (x w c) -> p (k x) w c", x=2, w=2)[:, :, :, r],
                                                   bc(D_[r, :, :], 2, 2), ALU.mult)
                last.then_inc(g_lq, 1)

            def gate_sum(t):
                n, _ = tile_tokens(t)
                dve.wait_ge(o_sq, t + 1)
                nc.vector.tensor_reduce(ss[0:n, 0:H], sqt[0:n, 0:DW].rearrange("p (h e) -> p h e", e=HD), AX, ALU.add).then_inc(o_ss, 1)

            def gate_norm(t):
                n, _ = tile_tokens(t)
                dve.wait_ge(o_r, t + 1)
                wait(dve, o_tr, t)
                if t < NT:
                    for r in range(2):
                        last = nc.vector.tensor_tensor(onr[0:n, :].rearrange("p (q r e) -> p r q e", r=2, e=HD)[:, r],
                                                       ps[0:n, 4 - 4 * (t % 2) + r, 0:PR * HD].rearrange("p (q e) -> p q e", e=HD),
                                                       bc(ss[0:n, r * PR:(r + 1) * PR], 2, HD), ALU.mult)
                else:
                    last = nc.vector.tensor_tensor(heads(onr[0:n, :]), heads(ps[0:n, 4, :]), bc(ss[0:n, 0:H], 2, HD), ALU.mult)
                last.then_inc(o_n, 1)

            def gate_out(t):
                n, t0 = tile_tokens(t)
                dve.wait_ge(o_tr, t + 1)
                nc.vector.scalar_tensor_tensor(out=zs[:, :, t0:t0 + n], in0=ps[:, 7, :].rearrange("p (q t) -> p q t", q=PR)[:, :, 0:n],
                                               scalar=g2, in1=zs[:, :, t0:t0 + n], op0=ALU.mult, op1=ALU.mult).then_inc(o_g, 1)

            dve.wait_ge(n_r, 1)
            rq, rk = rn[:, :, 0:H], rn[:, :, H:2 * H]
            nc.vector.tensor_tensor(scb[:, 0, :, :], rk, beta[:, :, :], ALU.mult)
            nc.vector.tensor_tensor(scb[:, 2, :, :], rk, ekd[:, :, :], ALU.mult)
            step(nc.vector.tensor_scalar(scb[:, 3, :, :], rq, HD ** -0.5, None, ALU.mult))
            nc.vector.tensor_tensor(scb[:, 1, :, :], scb[:, 0, :, :], egc[:, :, :], ALU.mult)
            step(nc.vector.tensor_tensor(scb[:, 4, :, :], scb[:, 3, :, :], egc[:, :, :], ALU.mult))
            for par in range(2):
                nc.vector.memset(S[par * HD:(par + 1) * HD, :, :], 0.0).then_inc(s_up[par], 1)
            scaled(0)
            for t in range(NT + 1):
                if t < NT:
                    scaled(t + 1)
                decayed(t)

            def decode_step(n):
                if n == 0:
                    dve.wait_ge(g_lq, NT + 1)
                    nc.vector.tensor_tensor(Ns[:, :, :], LQd[:, :, 0, :], bc(consts["str4"][0:NS, :], 1, H), ALU.mult).then_inc(sp_dve, 1)
                elif n == 1:
                    dve.wait_ge(sp_mm, 2)
                    nc.vector.tensor_tensor(Ms[:, :, :], ps[0:NS, 1, 0:H * C].rearrange("p (s c) -> p s c", c=C),
                                            bc(ident[0:NS, 0:C], 1, H), ALU.add).then_inc(sp_dve, 1)
                elif n == 2:
                    dve.wait_ge(sp_dve, 2)
                    dve.wait_ge(sp_mm, 3)
                    nc.vector.tensor_tensor(Ts[:, :, :], Ms[:, :, :], ps[0:NS, 2, 0:H * C].rearrange("p (s c) -> p s c", c=C), ALU.subtract).then_inc(sp_dve, 1)
                else:
                    dve.wait_ge(sp_mm, 6)
                    dve.wait_ge(sp_act, 2)
                    nc.vector.tensor_tensor(dV[:, :], dV[:, :], ps[0:NS, 3, :], ALU.subtract).then_inc(sp_dve, 1)

            decode_step(0)
            Xm = Xp[:, :, :].rearrange("p g (m c) -> p g m c", c=C)
            Lm = Lp[:, :, :].rearrange("p g (m c) -> p g m c", c=C)
            step(nc.vector.memset(Xp[:, :, :], 0.0))
            step(nc.vector.memset(Xp[:, :, 0:C * C:C + 1], 1.0))
            dve.wait_ge(lt_ld, 32)
            for c in range(1, C):
                pr = prod[:, :, 0:c * c].rearrange("p g (m j) -> p g m j", j=c)
                step(nc.vector.tensor_tensor(pr, Xm[:, :, 0:c, 0:c], bc(Lm[:, :, 0:c, c], 2, c), ALU.mult))
                ins = nc.vector.tensor_reduce(Xm[:, :, 0:c, c], pr, AX, ALU.add, negate=True)
                if c < C - 1:
                    step(ins)
                else:
                    ins.then_inc(inv, 1)
                if c in (10, 14, 24):
                    decode_step({10: 1, 14: 2, 24: 3}[c])
            for t in range(NT):
                dve.wait_ge(uw_ev, 2 * t + 1)
                for b in range(CPT):
                    if t and b:
                        (gate_sum, gate_norm, gate_out)[b - 1](t - 1)
                    n = t * CPT + b
                    r = slice(b * C, (b + 1) * C)
                    for par in range(2):
                        dve.wait_ge(ws_mm[par], n + 1)
                        pv = lambda x: x.rearrange("p (q r e) -> p r q e", r=2, e=HD)[:, par]
                        nc.vector.tensor_tensor(pv(Vn[r, :]), pv(Vb[r, t, :]), ps[r, 2 + par, 0:PR * HD].rearrange("p (q e) -> p q e", e=HD),
                                                ALU.subtract).then_inc(vn_d[par], 1)
                    if b == 0 and 2 <= t < 2 + PR:
                        q = t - 2
                        dve.wait_ge(sp_g, q + 1)
                        dve.wait_ge(sp_ds, q + 1)
                        nc.vector.tensor_tensor(S0[:, q, :, :], S0[:, q, :, :], ps[:, 7, :].rearrange("p (b e) -> p b e", e=HD), ALU.add).then_inc(sp_up, 1)
                    for par in range(2):
                        rows = slice(par * HD, (par + 1) * HD)
                        dve.wait_ge(sd, n + 1)
                        dve.wait_ge(ds_mm[par], n + 1)
                        nc.vector.tensor_tensor(S[rows, :, :], Sd[rows, :, :], ps[rows, 6, 0:PR * HD].rearrange("p (q e) -> p q e", e=HD),
                                                ALU.add).then_inc(s_up[par], 1)
            dve.wait_ge(w_lod, J_OUT)
            split_lo(Job(0, J_OUT))

            def operand_lo(i):
                k = ORDER[i]
                dve.wait_ge(op_hi, i + 1)
                src = zs[:, k, :] if k < PR else gl[:, k - PR, :]
                nc.vector.tensor_tensor(op[1][:, k, :], src, op[0][:, k, :].bitcast(F32), ALU.subtract).then_inc(op_lo, 1)

            gate_sum(NT - 1)
            gate_norm(NT - 1)
            gate_out(NT - 1)
            gate_sum(NT)
            operand_lo(0)
            operand_lo(1)
            gate_norm(NT)
            gate_out(NT)
            dve.wait_ge(st_p, 32)
            for i in range(2, KT):
                operand_lo(i)

            def low_rows(phase, i, m):
                dve.wait_ge(h_hi, (phase + 1) * KT + i + 1)
                nc.vector.scalar_tensor_tensor(out=hh[1][:, m, :], in0=xT[:, m, :], scalar=gains[:, phase + 1, m:m + 1],
                                               in1=hh[0][:, m, :].bitcast(F32), op0=ALU.mult, op1=ALU.subtract).then_inc(h_lo, 1)

            def add_rows(job, m):
                wait(dve, mm, job.num(1))
                nc.vector.tensor_tensor(tri3(pick(xT, m)), tri3(pick(xT, m)), acc(job.slot), ALU.add).then_inc(pf, 1)

            for i in range(KT):
                job = Job(0, J_OUT + i)
                split_lo(job.next())
                if i in (0, KT // 2):
                    dve.wait_ge(ld_xT[i // (KT // 2)], 16)
                add_rows(job, ORDER[i])
                low_rows(0, i, ORDER[i])
            for q in range(FQ):
                up, down = J_MLP + 2 * KT * q, J_MLP + 2 * KT * q + KT

                def hidden(job, j, q=q):
                    n = q * KT + j
                    split_lo(job.next())
                    if q == 0 and isinstance(j, int) and j == 0:
                        dve.wait_ge(rs_done, 1)
                    wait(dve, pf, job.num(1))
                    wait(dve, u_sq, n)
                    wait(dve, u_hi, n)
                    nc.vector.tensor_tensor(t2[:, :], t1[:, :], rsb[:, :], ALU.mult).then_inc(t_done, 1)
                    wait(dve, u_sq, n + 1)
                    wait(dve, u_hi, n + 1)
                    nc.vector.tensor_tensor(pick(uu[1], j), t3[:, :], pick(uu[0], j).bitcast(F32), ALU.subtract).then_inc(u_lo, 1)
                jobs(dve, up, KT, hidden)

                def out(job, j, q=q, down=down):
                    split_lo(job.next())
                    add_rows(job, j)
                    if q == FQ - 1:
                        low_rows(1, j, j)
                if q < FQ - 1:
                    jobs(dve, down, KT, out)
                else:
                    for m in range(KT):
                        if 1 <= m <= 3 * PK:
                            k, g = divmod(m - 1, 3)
                            w = 512 if g < 2 else NS
                            dve.wait_ge(p_tr, m)
                            nc.vector.tensor_copy(pT[k][:, g * 512:g * 512 + w], ps[:, 6 + (m - 1) % 2, 0:w]).then_inc(p_cp, 1)
                        out(Job(0, down + m), m)
            for k in range(PK):
                dve.wait_ge(p_hi, k + 1)
                nc.vector.tensor_tensor(pp[1][:, k, :], pT[k][:, :], pp[0][:, k, :].bitcast(F32), ALU.subtract).then_inc(p_lo, 1)
            for m in range(KT):
                jg, jp = Job(0, J_GATE + 2 * m), Job(0, J_GATE + 2 * m + 1)
                split_lo(jp, kts=PK)
                if m == 0:
                    dve.wait_ge(rs_done, 2)
                    dve.wait_ge(p_lo, PK)
                dve.wait_ge(mm, jg.num(1))
                wait(dve, gt_done, m)
                nc.vector.tensor_tensor(tri3(t1[:, :]), acc(jg.slot), tri3(rsb[:, :]), ALU.mult).then_inc(pf, 1)
                if m < KT - 1:
                    split_lo(jp.next())
                dve.wait_ge(mm, jp.num(1))
                dve.wait_ge(gt_done, m + 1)
                nc.vector.tensor_tensor(tri3(pg[:, :]), acc(jp.slot), tri3(gt[:, :]), ALU.mult).then_inc(pf, 1)
                dve.wait_ge(pf, jp.num(1))
                nc.vector.tensor_tensor(xT[:, m, :], xT[:, m, :], pg[:, :], ALU.add).then_inc(x_new, 1)
                dve.wait_ge(sq_done, 2 * KT + m + 1)
                dve.wait_ge(x_new, m + 1)
                nc.vector.tensor_scalar(xT[:, m, :], xT[:, m, :], gains[:, 3, m:m + 1], None, ALU.mult).then_inc(xg_done, 1)


def bc(ap, axis, n):
    ap = ap.unsqueeze(axis)
    shape = list(ap.shape)
    shape[axis] = n
    return ap.to_broadcast(shape)


_INS = ["x_prompt", "x_sample", "state_ssm", "state_qkv_conv", "state_conf_conv", "p_prompt", "p_sample", "g_mix", "w_in",
        "w_short", "a_log", "dt_bias", "g_o", "w_dw", "b_dw", "g_cln", "b_cln", "w_out", "g_mlp", "w_up", "w_down",
        "w_ple", "g_ple", "w_ple_gate", "g_final"]
_OUTS = [("y_p", (1, SEQ, D)), ("y_s", (DB, DS, D)), ("ssm_p", (1, 1, H, HD, HD)), ("qkv_p", (1, 1, QH, 3 * DW)),
         ("conf_p", (1, 1, HIST, CC)), ("ssm_s", (1, DB, H, HD, HD)), ("qkv_s", (1, DB, QH, 3 * DW)),
         ("conf_s", (1, DB, HIST, CC))]


def kernel(**inputs):
    import concourse.bacc as _bacc
    from concourse.bass_utils import run_bass_kernel_spmd as _run

    nc = _bacc.Bacc("TRN2", target_bir_lowering=False, num_devices=1, dynamic_dma_scratch_size=1024)
    arrays, a, o = {}, {}, {}
    for name in _INS:
        arrays[f"in_{name}"] = np.ascontiguousarray(inputs[name])
    arrays["in_consts"] = shape_constants()
    for name, arr in arrays.items():
        a[name[3:]] = nc.dram_tensor(name, arr.shape, mybir.dt.from_np(arr.dtype), kind="ExternalInput").ap()
    for name, shape in _OUTS:
        o[name] = nc.dram_tensor(f"out_{name}", shape, F32, kind="ExternalOutput").ap()
    build(nc, a, o)
    r = _run(nc, [arrays], core_ids=[0])
    return tuple(r.results[0][f"out_{name}"] for name, _ in _OUTS)
```
